# Optimizing a Trainium2 kernel written in Bass

```python
import math
import jax, jax.numpy as jnp
from jax import lax
import numpy as np
import jax
import jax.numpy as jnp

D_MODEL = 1024
BATCH = 1
SEQ = 256
DEPTH = 2

N_A = DEPTH // 2
N_B = DEPTH - N_A
HEAD_DIM = 64
MIX_WIDTH = D_MODEL
MEM_HEADS = 4
MEM_WIDTH = MEM_HEADS * HEAD_DIM
MEM_LEN = 256
CONV_CH = MIX_WIDTH - MEM_WIDTH
CONV_K = 3
NSA_HEADS = CONV_CH // HEAD_DIM
NSA_KV_GROUPS = 2
NSA_HPG = NSA_HEADS // NSA_KV_GROUPS
N_BRANCH = 3
NSA_Q_WIDTH = NSA_HEADS * HEAD_DIM
NSA_GATE_WIDTH = NSA_HEADS * N_BRANCH
CMP_LEN = 32
CMP_STRIDE = 16
CMP_HIDDEN = 256
SEL_BLOCK = 64
SEL_TOPK = 16
N_LOCAL_SEL = 2
WINDOW = 512
Q_BLOCK = 128
REL_BUCKETS = 32
REL_MAX_DIST = 1024
FF_DIM = 4 * D_MODEL
EPS = 1e-6
NEG = -1e30
FORCE_SCORE = 1e4


def rmsnorm(x, g):
    xf = x.astype(jnp.float32)
    y = xf * lax.rsqrt(jnp.mean(xf * xf, axis=-1, keepdims=True) + EPS)
    return (y * g.astype(jnp.float32)).astype(x.dtype)

def rel_bucket(dist):
    n = jnp.maximum(dist, 0)
    max_exact = REL_BUCKETS // 2
    nf = jnp.maximum(n, 1).astype(jnp.float32)
    large = max_exact + (jnp.log(nf / max_exact) / math.log(REL_MAX_DIST / max_exact)
                         * (REL_BUCKETS - max_exact)).astype(jnp.int32)
    large = jnp.minimum(large, REL_BUCKETS - 1)
    return jnp.where(n < max_exact, n, large)

def masked_softmax(logits, mask):
    p = jax.nn.softmax(jnp.where(mask, logits, NEG), axis=-1)
    return jnp.where(mask, p, 0.0)

def selection_overlap(n_cmp, n_sel):
    c0 = np.arange(n_cmp)[:, None] * CMP_STRIDE
    s0 = np.arange(n_sel)[None, :] * SEL_BLOCK
    ov = np.minimum(c0 + CMP_LEN, s0 + SEL_BLOCK) - np.maximum(c0, s0)
    return np.clip(ov, 0, None).astype(np.float32) / CMP_LEN

def short_conv_mixer(z, conv_w):
    gate_b, gate_c, u = jnp.split(z, 3, axis=-1)
    v = gate_c * u
    y = lax.conv_general_dilated(
        v, conv_w[:, None, :].astype(v.dtype), window_strides=(1,),
        padding=[(CONV_K - 1, 0)], dimension_numbers=('NWC', 'WIO', 'NWC'),
        feature_group_count=CONV_CH)
    return gate_b * y

def memory_attention(q_raw, mem_k, mem_v, q_gain):
    b, s, _ = q_raw.shape
    q = rmsnorm(q_raw.reshape(b, s, MEM_HEADS, HEAD_DIM), q_gain) * (HEAD_DIM ** -0.5)
    lg = jnp.einsum('bshd,bmhd->bhsm', q, mem_k).astype(jnp.float32)
    p = jax.nn.softmax(lg, axis=-1).astype(mem_v.dtype)
    return jnp.einsum('bhsm,bmhd->bshd', p, mem_v).reshape(b, s, MEM_WIDTH)

def compress(u, pos, w1, w2):
    b, s, g, d = u.shape
    ch = u.reshape(b, s // CMP_STRIDE, CMP_STRIDE, g, d)
    blk = jnp.concatenate([ch[:, :-1], ch[:, 1:]], axis=2) + pos[:, None, :]
    flat = blk.transpose(0, 1, 3, 2, 4).reshape(b, -1, g, CMP_LEN * d)
    return jax.nn.gelu(flat @ w1) @ w2

def build_shared_kv(x, kv_norm, w_kv_shared, k_gain, cmp_pos, cmp_w1, cmp_w2):
    b, s, _ = x.shape
    h = rmsnorm(x, kv_norm)
    kv = (h @ w_kv_shared).reshape(b, s, 6, NSA_KV_GROUPS, HEAD_DIM)
    kc = rmsnorm(compress(kv[:, :, 0], cmp_pos[0], cmp_w1[0], cmp_w2[0]), k_gain[0])
    vc = compress(kv[:, :, 1], cmp_pos[1], cmp_w1[1], cmp_w2[1])
    n_sel = s // SEL_BLOCK
    def to_blocks(u):
        return u.reshape(b, n_sel, SEL_BLOCK, NSA_KV_GROUPS, HEAD_DIM).transpose(0, 3, 1, 2, 4)
    ks = to_blocks(rmsnorm(kv[:, :, 2], k_gain[1]))
    vs = to_blocks(kv[:, :, 3])
    def pad_front(u):
        return jnp.pad(u, ((0, 0), (WINDOW, 0), (0, 0), (0, 0)))
    kw = pad_front(rmsnorm(kv[:, :, 4], k_gain[2]))
    vw = pad_front(kv[:, :, 5])
    return (kc, vc, ks, vs, kw, vw)

def nsa_mixer(q_raw, gate_logits, q_gain, kc, vc, ks, vs, kw, vw, rel_bias):
    b, s, _ = q_raw.shape
    G, Hg, hd = NSA_KV_GROUPS, NSA_HPG, HEAD_DIM
    q = rmsnorm(q_raw.reshape(b, s, G, Hg, hd), q_gain) * (hd ** -0.5)
    gates = jax.nn.sigmoid(gate_logits.reshape(b, s, G, Hg, N_BRANCH))
    n_cmp = kc.shape[1]
    n_sel = ks.shape[2]
    topk = min(SEL_TOPK, n_sel)
    overlap = jnp.asarray(selection_overlap(n_cmp, n_sel), dtype=jnp.float32)
    cmp_end = jnp.arange(n_cmp) * CMP_STRIDE + CMP_LEN - 1
    sel_idx = jnp.arange(n_sel)
    table = rel_bias.astype(jnp.float32)
    table_g = table.reshape(REL_BUCKETS, G, Hg).transpose(1, 0, 2)
    bi = jnp.arange(b)[:, None, None, None]
    gi = jnp.arange(G)[None, :, None, None]
    kw_len = WINDOW + Q_BLOCK

    def block(i):
        s0 = i * Q_BLOCK
        tq = s0 + jnp.arange(Q_BLOCK)
        qb = lax.dynamic_slice_in_dim(q, s0, Q_BLOCK, axis=1)
        gb = lax.dynamic_slice_in_dim(gates, s0, Q_BLOCK, axis=1)
        d_c = tq[:, None] - cmp_end[None, :]
        bias_c = table[rel_bucket(d_c)].reshape(Q_BLOCK, n_cmp, G, Hg).transpose(2, 3, 0, 1)
        lg = jnp.einsum('bqghd,bcgd->bghqc', qb, kc).astype(jnp.float32) + bias_c
        p_c = masked_softmax(lg, d_c >= 0)
        o_c = jnp.einsum('bghqc,bcgd->bqghd', p_c.astype(vc.dtype), vc)
        imp = jnp.einsum('bghqc,cj->bgqj', p_c, overlap)
        back = (tq // SEL_BLOCK)[:, None] - sel_idx[None, :]
        forced = (sel_idx[None, :] == 0) | ((back >= 0) & (back < N_LOCAL_SEL))
        score = jnp.where(back >= 0, jnp.where(forced, FORCE_SCORE, imp), NEG)
        _, idx = lax.top_k(score, topk)
        k_sel = ks[bi, gi, idx].reshape(b, G, Q_BLOCK, topk * SEL_BLOCK, hd)
        v_sel = vs[bi, gi, idx].reshape(b, G, Q_BLOCK, topk * SEL_BLOCK, hd)
        pos_s = (idx[..., None] * SEL_BLOCK + jnp.arange(SEL_BLOCK)).reshape(b, G, Q_BLOCK, topk * SEL_BLOCK)
        d_s = tq[None, None, :, None] - pos_s
        bias_s = table_g[gi, rel_bucket(d_s)].transpose(0, 1, 4, 2, 3)
        lg = jnp.einsum('bqghd,bgqkd->bghqk', qb, k_sel).astype(jnp.float32) + bias_s
        p_s = masked_softmax(lg, (d_s >= 0)[:, :, None])
        o_s = jnp.einsum('bghqk,bgqkd->bqghd', p_s.astype(v_sel.dtype), v_sel)
        k_w = lax.dynamic_slice_in_dim(kw, s0, kw_len, axis=1)
        v_w = lax.dynamic_slice_in_dim(vw, s0, kw_len, axis=1)
        pos_w = s0 - WINDOW + jnp.arange(kw_len)
        d_w = tq[:, None] - pos_w[None, :]
        mask_w = (d_w >= 0) & (d_w < WINDOW) & (pos_w[None, :] >= 0)
        bias_w = table[rel_bucket(d_w)].reshape(Q_BLOCK, kw_len, G, Hg).transpose(2, 3, 0, 1)
        lg = jnp.einsum('bqghd,bkgd->bghqk', qb, k_w).astype(jnp.float32) + bias_w
        p_w = masked_softmax(lg, mask_w)
        o_w = jnp.einsum('bghqk,bkgd->bqghd', p_w.astype(v_w.dtype), v_w)
        return gb[..., 0:1] * o_c + gb[..., 1:2] * o_s + gb[..., 2:3] * o_w

    out = lax.map(block, jnp.arange(s // Q_BLOCK))
    return jnp.moveaxis(out, 0, 1).reshape(b, s, NSA_Q_WIDTH)

def first_inputs(seed: int = 0) -> dict:
    key = jax.random.key(seed)
    ks = jax.random.split(key, 22)
    def nrm(k, shape, scale):
        return jax.random.normal(k, shape, jnp.float32) * scale
    def gain(k, shape):
        return 1.0 + 0.1 * jax.random.normal(k, shape, jnp.float32)
    a_in = 3 * CONV_CH + MEM_WIDTH
    b_in = NSA_Q_WIDTH + NSA_GATE_WIDTH + MEM_WIDTH
    return {
        "x": nrm(ks[0], (BATCH, SEQ, D_MODEL), 1.0),
        "mem": nrm(ks[1], (BATCH, MEM_LEN, D_MODEL), 1.0),
        "mix_norm": gain(ks[2], (DEPTH, D_MODEL)),
        "a_w_in": nrm(ks[3], (N_A, D_MODEL, a_in), D_MODEL ** -0.5),
        "a_conv_w": nrm(ks[4], (N_A, CONV_K, CONV_CH), CONV_K ** -0.5),
        "b_w_in": nrm(ks[5], (N_B, D_MODEL, b_in), D_MODEL ** -0.5),
        "b_q_gain": gain(ks[6], (N_B, HEAD_DIM)),
        "kv_norm": gain(ks[7], (D_MODEL,)),
        "w_kv_shared": nrm(ks[8], (D_MODEL, 6 * NSA_KV_GROUPS * HEAD_DIM), D_MODEL ** -0.5),
        "k_gain": gain(ks[9], (N_BRANCH, HEAD_DIM)),
        "cmp_pos": nrm(ks[10], (2, CMP_LEN, HEAD_DIM), 0.1),
        "cmp_w1": nrm(ks[11], (2, CMP_LEN * HEAD_DIM, CMP_HIDDEN), (CMP_LEN * HEAD_DIM) ** -0.5),
        "cmp_w2": nrm(ks[12], (2, CMP_HIDDEN, HEAD_DIM), CMP_HIDDEN ** -0.5),
        "rel_bias": nrm(ks[13], (REL_BUCKETS, NSA_HEADS), 0.5),
        "mem_norm": gain(ks[14], (D_MODEL,)),
        "mem_w_kv": nrm(ks[15], (DEPTH, D_MODEL, 2 * MEM_WIDTH), D_MODEL ** -0.5),
        "mem_q_gain": gain(ks[16], (DEPTH, HEAD_DIM)),
        "mem_k_gain": gain(ks[17], (DEPTH, HEAD_DIM)),
        "w_out": nrm(ks[18], (DEPTH, MIX_WIDTH, D_MODEL), MIX_WIDTH ** -0.5),
        "mlp_norm": gain(ks[19], (DEPTH, D_MODEL)),
        "w_up": nrm(ks[20], (DEPTH, D_MODEL, FF_DIM), D_MODEL ** -0.5),
        "w_down": nrm(ks[21], (DEPTH, FF_DIM, D_MODEL), FF_DIM ** -0.5),
    }

def first_block(x, mem, mix_norm, a_w_in, a_conv_w, b_w_in, b_q_gain, kv_norm, w_kv_shared,
              k_gain, cmp_pos, cmp_w1, cmp_w2, rel_bias, mem_norm, mem_w_kv, mem_q_gain,
              mem_k_gain, w_out, mlp_norm, w_up, w_down):
    b, m, _ = mem.shape
    mem_h = rmsnorm(mem, mem_norm)
    shared = None
    for layer in range(DEPTH):
        h = rmsnorm(x, mix_norm[layer])
        mkv = (mem_h @ mem_w_kv[layer]).reshape(b, m, 2, MEM_HEADS, HEAD_DIM)
        mem_k = rmsnorm(mkv[:, :, 0], mem_k_gain[layer])
        mem_v = mkv[:, :, 1]
        if layer < N_A:
            z = h @ a_w_in[layer]
            y_tok = short_conv_mixer(z[..., :3 * CONV_CH], a_conv_w[layer])
            q_mem = z[..., 3 * CONV_CH:]
        else:
            j = layer - N_A
            z = h @ b_w_in[j]
            y_tok = nsa_mixer(z[..., :NSA_Q_WIDTH],
                              z[..., NSA_Q_WIDTH:NSA_Q_WIDTH + NSA_GATE_WIDTH],
                              b_q_gain[j], *shared, rel_bias)
            q_mem = z[..., NSA_Q_WIDTH + NSA_GATE_WIDTH:]
        y_mem = memory_attention(q_mem, mem_k, mem_v, mem_q_gain[layer])
        x = x + jnp.concatenate([y_tok, y_mem], axis=-1) @ w_out[layer]
        hm = rmsnorm(x, mlp_norm[layer])
        x = x + jnp.square(jax.nn.relu(hm @ w_up[layer])) @ w_down[layer]
        if layer == N_A - 1:
            shared = build_shared_kv(x, kv_norm, w_kv_shared, k_gain, cmp_pos, cmp_w1, cmp_w2)
    return x


DEPTH_2 = 1

CHUNK = 64
NORM_EPS = 1e-6

RWKV_HEAD = 64
RWKV_WIDTH = D_MODEL
RWKV_HEADS = RWKV_WIDTH // RWKV_HEAD
DECAY_LORA = 64
AAA_LORA = 64
GATE_LORA = 128
RWKV_GN_EPS = 64e-5
RWKV_SPLITS = (RWKV_WIDTH, 2 * RWKV_WIDTH, 3 * RWKV_WIDTH, 3 * RWKV_WIDTH + DECAY_LORA, 3 * RWKV_WIDTH + DECAY_LORA + AAA_LORA)
RWKV_COLS = 3 * RWKV_WIDTH + DECAY_LORA + AAA_LORA + GATE_LORA

SSD_WIDTH = 2 * D_MODEL
SSD_HEAD = 64
SSD_HEADS = SSD_WIDTH // SSD_HEAD
SSD_GROUPS = 4
SSD_HEADS_PER_GROUP = SSD_HEADS // SSD_GROUPS
SSD_STATE = 128
SSD_CONV = 4
SSD_CONV_CH = SSD_WIDTH + 2 * SSD_GROUPS * SSD_STATE
SSD_COLS = SSD_WIDTH + SSD_CONV_CH + SSD_HEADS

N_BRANCH_2 = 2
GATE_COLS = N_BRANCH_2 * D_MODEL
IN_COLS = RWKV_COLS + SSD_COLS + GATE_COLS

N_GROUPS = 4
EXP_PER_GROUP = 8
N_EXPERTS = N_GROUPS * EXP_PER_GROUP
TOP_K = 2
D_EXPERT = 512
MOE_BLOCK = 128


def rmsnorm_2(x, g):
    xf = x.astype(jnp.float32)
    y = xf * lax.rsqrt(jnp.mean(xf * xf, axis=-1, keepdims=True) + NORM_EPS)
    return (y * g.astype(jnp.float32)).astype(x.dtype)

def token_shift(u):
    return jnp.pad(u[:, :-1], ((0, 0), (1, 0), (0, 0)))

def rwkv7_mix(p, mu, w0, w_decay, a0, w_a, w_g, k_k, k_a, r_k, ln_g, ln_b):
    B_, S_, _ = p.shape
    f32 = jnp.float32
    u = p + mu * (token_shift(p) - p)
    r, k, v, zw, za, zg = jnp.split(u, RWKV_SPLITS, axis=-1)
    w = -jax.nn.softplus(-(w0 + jnp.tanh(zw) @ w_decay)) - 0.5
    decay = jnp.exp(-jnp.exp(w.astype(f32)))
    a = jax.nn.sigmoid(a0 + za @ w_a)
    g = jax.nn.sigmoid(zg) @ w_g

    def heads(t):
        return t.astype(f32).reshape(B_, S_, RWKV_HEADS, RWKV_HEAD)

    kk = heads(k * k_k)
    kk = kk / jnp.maximum(jnp.sqrt(jnp.sum(kk * kk, axis=-1, keepdims=True)), 1e-12)
    k = k * (1.0 + (a - 1.0) * k_a)
    r_h, k_h, v_h, a_h, w_h = heads(r), heads(k), heads(v), heads(a), heads(decay)

    def step(state, inp):
        r_t, w_t, k_t, v_t, kk_t, a_t = inp
        sa = jnp.einsum('bhij,bhj->bhi', state, -kk_t)
        state = (state * w_t[:, :, None, :]
                 + sa[..., None] * (kk_t * a_t)[:, :, None, :]
                 + v_t[..., None] * k_t[:, :, None, :])
        y_t = jnp.einsum('bhij,bhj->bhi', state, r_t)
        return state, y_t

    xs = tuple(jnp.moveaxis(t, 1, 0) for t in (r_h, w_h, k_h, v_h, kk, a_h))
    state0 = jnp.zeros((B_, RWKV_HEADS, RWKV_HEAD, RWKV_HEAD), f32)
    _, ys = lax.scan(step, state0, xs)
    y = jnp.moveaxis(ys, 0, 1)

    mean = jnp.mean(y, axis=-1, keepdims=True)
    var = jnp.mean(jnp.square(y - mean), axis=-1, keepdims=True)
    y = ((y - mean) * lax.rsqrt(var + RWKV_GN_EPS)).reshape(B_, S_, RWKV_WIDTH)
    y = y * ln_g + ln_b
    bonus = jnp.sum(r_h * k_h * r_k, axis=-1, keepdims=True) * v_h
    out = (y + bonus.reshape(B_, S_, RWKV_WIDTH)) * g
    return out.astype(p.dtype)

def causal_dwconv(u, w, b):
    c = u.shape[-1]
    y = lax.conv_general_dilated(u, w[:, None, :], window_strides=(1,), padding=[(SSD_CONV - 1, 0)],
                                 dimension_numbers=('NWC', 'WIO', 'NWC'), feature_group_count=c)
    return y + b

def ssd_chunked(xs, dt, A, Bm, Cm):
    f32 = jnp.float32
    B_, S_, _ = xs.shape
    nc = S_ // CHUNK
    G, Hg, P, N = SSD_GROUPS, SSD_HEADS_PER_GROUP, SSD_HEAD, SSD_STATE
    x = xs.astype(f32).reshape(B_, nc, CHUNK, G, Hg, P)
    dt = dt.reshape(B_, nc, CHUNK, G, Hg)
    Bc = Bm.astype(f32).reshape(B_, nc, CHUNK, G, N)
    Cc = Cm.astype(f32).reshape(B_, nc, CHUNK, G, N)
    a_dt = dt * A.reshape(G, Hg)
    a_cs = jnp.cumsum(a_dt, axis=2)
    xdt = x * dt[..., None]

    seg = a_cs[:, :, :, None] - a_cs[:, :, None, :]
    tril = jnp.tril(jnp.ones((CHUNK, CHUNK), dtype=bool))[None, None, :, :, None, None]
    decay_in = jnp.exp(jnp.where(tril, seg, -jnp.inf))
    cb = jnp.einsum('bclgn,bcsgn->bclsg', Cc, Bc)
    y_diag = jnp.einsum('bclsgh,bcsghp->bclghp', cb[..., None] * decay_in, xdt)

    decay_st = jnp.exp(a_cs[:, :, -1:] - a_cs)
    states = jnp.einsum('bcsgn,bcsghp->bcghpn', Bc, xdt * decay_st[..., None])
    chunk_decay = jnp.exp(a_cs[:, :, -1])

    def step(h, inp):
        s_c, d_c = inp
        return h * d_c[..., None, None] + s_c, h

    h0 = jnp.zeros((B_, G, Hg, P, N), f32)
    _, prev = lax.scan(step, h0, (jnp.moveaxis(states, 1, 0), jnp.moveaxis(chunk_decay, 1, 0)))
    prev = jnp.moveaxis(prev, 0, 1)
    y_off = jnp.einsum('bclgn,bcghpn->bclghp', Cc, prev) * jnp.exp(a_cs)[..., None]
    return (y_diag + y_off).reshape(B_, S_, SSD_WIDTH)

def ssd_mix(p, conv_w, conv_b, dt_bias, a_log, d_skip, norm_g):
    B_, S_, _ = p.shape
    f32 = jnp.float32
    z = p[..., :SSD_WIDTH]
    xbc = p[..., SSD_WIDTH:SSD_WIDTH + SSD_CONV_CH]
    dt_raw = p[..., SSD_WIDTH + SSD_CONV_CH:]
    xbc = jax.nn.silu(causal_dwconv(xbc, conv_w, conv_b))
    xs = xbc[..., :SSD_WIDTH]
    Bm = xbc[..., SSD_WIDTH:SSD_WIDTH + SSD_GROUPS * SSD_STATE]
    Cm = xbc[..., SSD_WIDTH + SSD_GROUPS * SSD_STATE:]
    dt = jax.nn.softplus(dt_raw.astype(f32) + dt_bias.astype(f32))
    A = -jnp.exp(a_log.astype(f32))
    y = ssd_chunked(xs, dt, A, Bm, Cm)
    y = y + (xs.astype(f32).reshape(B_, S_, SSD_HEADS, SSD_HEAD) * d_skip[:, None]).reshape(B_, S_, SSD_WIDTH)
    u = y * jax.nn.silu(z.astype(f32))
    u = u.reshape(B_, S_, SSD_GROUPS, SSD_WIDTH // SSD_GROUPS)
    u = u * lax.rsqrt(jnp.mean(u * u, axis=-1, keepdims=True) + NORM_EPS)
    u = u.reshape(B_, S_, SSD_WIDTH) * norm_g
    return u.astype(p.dtype)

def hier_moe(h, w_rg, b_rg, w_re, b_re, w_gate, w_up, w_down):
    B_, S_, D = h.shape
    T = B_ * S_
    f32 = jnp.float32
    ht = h.reshape(T, D)
    g_logits = (ht @ w_rg + b_rg).astype(f32)
    g_prob = jax.nn.softmax(g_logits, axis=-1)
    grp = jnp.argmax(g_logits, axis=-1)
    g_w = jnp.take_along_axis(g_prob, grp[:, None], axis=1)[:, 0]
    e_logits = (ht @ w_re + b_re).astype(f32).reshape(T, N_GROUPS, EXP_PER_GROUP)
    e_logits = jnp.take_along_axis(e_logits, grp[:, None, None], axis=1)[:, 0]
    e_prob = jax.nn.softmax(e_logits, axis=-1)
    top_p, top_i = lax.top_k(e_prob, TOP_K)
    gate = g_w[:, None] * top_p / jnp.sum(top_p, axis=-1, keepdims=True)
    expert = grp[:, None] * EXP_PER_GROUP + top_i

    n_assign = T * TOP_K
    e_flat = expert.reshape(-1)
    tok_flat = jnp.repeat(jnp.arange(T, dtype=jnp.int32), TOP_K)
    w_flat = gate.reshape(-1)
    order = jnp.argsort(e_flat)
    e_sorted, tok_sorted, w_sorted = e_flat[order], tok_flat[order], w_flat[order]
    counts = jnp.bincount(e_flat, length=N_EXPERTS)
    starts = jnp.cumsum(counts) - counts
    pad_counts = (counts + MOE_BLOCK - 1) // MOE_BLOCK * MOE_BLOCK
    pad_ends = jnp.cumsum(pad_counts)
    pad_starts = pad_ends - pad_counts
    dest = pad_starts[e_sorted] + (jnp.arange(n_assign) - starts[e_sorted])
    n_blocks = n_assign // MOE_BLOCK + N_EXPERTS
    buf_tok = jnp.zeros((n_blocks * MOE_BLOCK,), jnp.int32).at[dest].set(tok_sorted)
    buf_w = jnp.zeros((n_blocks * MOE_BLOCK,), f32).at[dest].set(w_sorted)
    block_exp = jnp.minimum(jnp.searchsorted(pad_ends, jnp.arange(n_blocks) * MOE_BLOCK, side='right'), N_EXPERTS - 1)

    def run_block(args):
        tok, e = args
        xb = ht[tok]
        hid = jax.nn.silu(xb @ w_gate[e]) * (xb @ w_up[e])
        return hid @ w_down[e]

    y_blocks = lax.map(run_block, (buf_tok.reshape(n_blocks, MOE_BLOCK), block_exp))
    y = jnp.zeros((T, D), f32).at[buf_tok].add(y_blocks.reshape(-1, D).astype(f32) * buf_w[:, None])
    return y.reshape(B_, S_, D).astype(h.dtype)

def second_inputs(seed: int = 0) -> dict:
    key = jax.random.key(seed)
    ks = iter(jax.random.split(key, 40))
    f32 = jnp.float32
    L = DEPTH_2

    def nrm(shape, scale):
        return jax.random.normal(next(ks), shape, f32) * scale

    def unif(shape, lo, hi):
        return jax.random.uniform(next(ks), shape, f32, lo, hi)

    x = nrm((BATCH, SEQ, D_MODEL), 1.0)
    attn_norm_g = 1.0 + nrm((L, D_MODEL), 0.05)
    w_in = nrm((L, D_MODEL, IN_COLS), D_MODEL ** -0.5)
    b_gate = nrm((L, GATE_COLS), 0.1)
    rwkv_mu = unif((L, RWKV_COLS), 0.2, 0.8)
    rwkv_w0 = unif((L, RWKV_WIDTH), -6.0, -1.0)
    rwkv_w_decay = nrm((L, DECAY_LORA, RWKV_WIDTH), 0.5 * DECAY_LORA ** -0.5)
    rwkv_a0 = nrm((L, RWKV_WIDTH), 0.5)
    rwkv_w_a = nrm((L, AAA_LORA, RWKV_WIDTH), AAA_LORA ** -0.5)
    rwkv_w_g = nrm((L, GATE_LORA, RWKV_WIDTH), GATE_LORA ** -0.5)
    rwkv_k_k = 0.85 + nrm((L, RWKV_WIDTH), 0.05)
    rwkv_k_a = 1.0 + nrm((L, RWKV_WIDTH), 0.05)
    rwkv_r_k = nrm((L, RWKV_HEADS, RWKV_HEAD), 0.1)
    rwkv_ln_g = 1.0 + nrm((L, RWKV_WIDTH), 0.05)
    rwkv_ln_b = nrm((L, RWKV_WIDTH), 0.05)
    w_up_rwkv = nrm((L, RWKV_WIDTH, D_MODEL), RWKV_WIDTH ** -0.5)
    ssd_conv_w = nrm((L, SSD_CONV, SSD_CONV_CH), SSD_CONV ** -0.5)
    ssd_conv_b = nrm((L, SSD_CONV_CH), 0.05)
    dt0 = jnp.exp(unif((L, SSD_HEADS), float(np.log(1e-3)), float(np.log(1e-1))))
    ssd_dt_bias = dt0 + jnp.log(-jnp.expm1(-dt0))
    ssd_a_log = jnp.log(unif((L, SSD_HEADS), 1.0, 16.0))
    ssd_d = 1.0 + nrm((L, SSD_HEADS), 0.1)
    ssd_norm_g = 1.0 + nrm((L, SSD_WIDTH), 0.05)
    w_up_ssd = nrm((L, SSD_WIDTH, D_MODEL), SSD_WIDTH ** -0.5)
    w_out = nrm((L, D_MODEL, D_MODEL), D_MODEL ** -0.5)
    ffn_norm_g = 1.0 + nrm((L, D_MODEL), 0.05)
    w_router_group = nrm((L, D_MODEL, N_GROUPS), D_MODEL ** -0.5)
    b_router_group = nrm((L, N_GROUPS), 0.01)
    w_router_expert = nrm((L, D_MODEL, N_EXPERTS), D_MODEL ** -0.5)
    b_router_expert = nrm((L, N_EXPERTS), 0.01)
    w_exp_gate = nrm((L, N_EXPERTS, D_MODEL, D_EXPERT), D_MODEL ** -0.5)
    w_exp_up = nrm((L, N_EXPERTS, D_MODEL, D_EXPERT), D_MODEL ** -0.5)
    w_exp_down = nrm((L, N_EXPERTS, D_EXPERT, D_MODEL), D_EXPERT ** -0.5)
    final_norm_g = 1.0 + nrm((D_MODEL,), 0.05)
    return {'x': x, 'attn_norm_g': attn_norm_g, 'w_in': w_in, 'b_gate': b_gate,
            'rwkv_mu': rwkv_mu, 'rwkv_w0': rwkv_w0, 'rwkv_w_decay': rwkv_w_decay, 'rwkv_a0': rwkv_a0,
            'rwkv_w_a': rwkv_w_a, 'rwkv_w_g': rwkv_w_g, 'rwkv_k_k': rwkv_k_k, 'rwkv_k_a': rwkv_k_a,
            'rwkv_r_k': rwkv_r_k, 'rwkv_ln_g': rwkv_ln_g, 'rwkv_ln_b': rwkv_ln_b, 'w_up_rwkv': w_up_rwkv,
            'ssd_conv_w': ssd_conv_w, 'ssd_conv_b': ssd_conv_b, 'ssd_dt_bias': ssd_dt_bias,
            'ssd_a_log': ssd_a_log, 'ssd_d': ssd_d, 'ssd_norm_g': ssd_norm_g, 'w_up_ssd': w_up_ssd,
            'w_out': w_out, 'ffn_norm_g': ffn_norm_g, 'w_router_group': w_router_group,
            'b_router_group': b_router_group, 'w_router_expert': w_router_expert,
            'b_router_expert': b_router_expert, 'w_exp_gate': w_exp_gate, 'w_exp_up': w_exp_up,
            'w_exp_down': w_exp_down, 'final_norm_g': final_norm_g}

def second_block(x, attn_norm_g, w_in, b_gate, rwkv_mu, rwkv_w0, rwkv_w_decay, rwkv_a0, rwkv_w_a, rwkv_w_g,
              rwkv_k_k, rwkv_k_a, rwkv_r_k, rwkv_ln_g, rwkv_ln_b, w_up_rwkv, ssd_conv_w, ssd_conv_b,
              ssd_dt_bias, ssd_a_log, ssd_d, ssd_norm_g, w_up_ssd, w_out, ffn_norm_g, w_router_group,
              b_router_group, w_router_expert, b_router_expert, w_exp_gate, w_exp_up, w_exp_down,
              final_norm_g):
    for l in range(DEPTH_2):
        h = rmsnorm_2(x, attn_norm_g[l])
        proj = h @ w_in[l]
        p_rwkv = proj[..., :RWKV_COLS]
        p_ssd = proj[..., RWKV_COLS:RWKV_COLS + SSD_COLS]
        p_gate = proj[..., RWKV_COLS + SSD_COLS:] + b_gate[l]
        y_a = rwkv7_mix(p_rwkv, rwkv_mu[l], rwkv_w0[l], rwkv_w_decay[l], rwkv_a0[l], rwkv_w_a[l], rwkv_w_g[l],
                        rwkv_k_k[l], rwkv_k_a[l], rwkv_r_k[l], rwkv_ln_g[l], rwkv_ln_b[l])
        y_b = ssd_mix(p_ssd, ssd_conv_w[l], ssd_conv_b[l], ssd_dt_bias[l], ssd_a_log[l], ssd_d[l], ssd_norm_g[l])
        gates = jax.nn.sigmoid(p_gate)
        g_a = gates[..., :D_MODEL]
        g_b = gates[..., D_MODEL:]
        merged = g_a * (y_a @ w_up_rwkv[l]) + g_b * (y_b @ w_up_ssd[l])
        x = x + merged @ w_out[l]
        h2 = rmsnorm_2(x, ffn_norm_g[l])
        x = x + hier_moe(h2, w_router_group[l], b_router_group[l], w_router_expert[l], b_router_expert[l],
                         w_exp_gate[l], w_exp_up[l], w_exp_down[l])
    return rmsnorm_2(x, final_norm_g)


def setup_inputs(seed=0):
    out = dict(first_inputs(seed))
    for name, value in second_inputs(seed + 1).items():
        if name != "x":
            out[name + "_2"] = value
    return out


def reference(
    x, mem, mix_norm, a_w_in, a_conv_w, b_w_in, b_q_gain, kv_norm, w_kv_shared, k_gain, cmp_pos,
    cmp_w1, cmp_w2, rel_bias, mem_norm, mem_w_kv, mem_q_gain, mem_k_gain, w_out, mlp_norm, w_up,
    w_down, attn_norm_g_2, w_in_2, b_gate_2, rwkv_mu_2, rwkv_w0_2, rwkv_w_decay_2, rwkv_a0_2,
    rwkv_w_a_2, rwkv_w_g_2, rwkv_k_k_2, rwkv_k_a_2, rwkv_r_k_2, rwkv_ln_g_2, rwkv_ln_b_2,
    w_up_rwkv_2, ssd_conv_w_2, ssd_conv_b_2, ssd_dt_bias_2, ssd_a_log_2, ssd_d_2, ssd_norm_g_2,
    w_up_ssd_2, w_out_2, ffn_norm_g_2, w_router_group_2, b_router_group_2, w_router_expert_2,
    b_router_expert_2, w_exp_gate_2, w_exp_up_2, w_exp_down_2, final_norm_g_2,
):
    x = first_block(
        x, mem, mix_norm, a_w_in, a_conv_w, b_w_in, b_q_gain, kv_norm, w_kv_shared, k_gain,
        cmp_pos, cmp_w1, cmp_w2, rel_bias, mem_norm, mem_w_kv, mem_q_gain, mem_k_gain, w_out,
        mlp_norm, w_up, w_down,
    )
    return second_block(
        x, attn_norm_g_2, w_in_2, b_gate_2, rwkv_mu_2, rwkv_w0_2, rwkv_w_decay_2, rwkv_a0_2,
        rwkv_w_a_2, rwkv_w_g_2, rwkv_k_k_2, rwkv_k_a_2, rwkv_r_k_2, rwkv_ln_g_2, rwkv_ln_b_2,
        w_up_rwkv_2, ssd_conv_w_2, ssd_conv_b_2, ssd_dt_bias_2, ssd_a_log_2, ssd_d_2,
        ssd_norm_g_2, w_up_ssd_2, w_out_2, ffn_norm_g_2, w_router_group_2, b_router_group_2,
        w_router_expert_2, b_router_expert_2, w_exp_gate_2, w_exp_up_2, w_exp_down_2,
        final_norm_g_2,
    )


_drawn_inputs = setup_inputs


def setup_inputs(seed=0):
    import zlib

    import numpy as np

    out = dict(_drawn_inputs(seed))
    spreads = {}
    factors = {'b_q_gain': 5.214,
     'k_gain': 3.906,
     'mem_norm': 4.303,
     'mem_q_gain': 8.0,
     'mem_k_gain': 4.683,
     'b_gate_2': 3.558,
     'rwkv_w_decay_2': 4.713,
     'rwkv_k_k_2': 8.729,
     'rwkv_ln_g_2': 5.847,
     'rwkv_ln_b_2': 8.0,
     'ssd_norm_g_2': 3.428,
     'b_router_group_2': 38.469,
     'b_router_expert_2': 42.945,
     'cmp_pos': 2.811,
     'rwkv_r_k_2': 4.353,
     'ffn_norm_g_2': 4.361}
    for name, (base, spread) in spreads.items():
        noise = np.random.default_rng([zlib.crc32(name.encode()), seed]).standard_normal(out[name].shape)
        drawn = base * np.exp(spread * noise) if base else spread * noise
        out[name] = jnp.asarray(drawn.astype(out[name].dtype))
    for name, factor in factors.items():
        out[name] = (out[name] * factor).astype(out[name].dtype)
    return out
```

```python
from contextlib import ExitStack, contextmanager

import numpy as np

import concourse.bass as bass
from concourse import mybir

F32 = mybir.dt.float32
ALU = mybir.AluOpType
ACT = mybir.ActivationFunctionType
AX = mybir.AxisListType

P = 128
S = 256
NT = S // P
D = 1024
KD = D // P
HD = 64
NEG = -1e30
EPS = 1e-6

CONV_CH = 768
NH = CONV_CH // HD
G = 2
HPG = NH // G
MW = 256
MH = MW // HD
M = 256
FF = 4096
NBK = 32
CMP_L, CMP_S = 32, 16
NC = S // CMP_S - 1
CMP_H = 256

RW = 1024
RH = RW // HD
RC = RW // P
LORA = 64
R_COLS = 3 * RW + 2 * LORA + P
SW = 2048
SH = SW // HD
SG = 4
SN = 128
XBC = SW + 2 * SG * SN
KAPPA = float(np.exp(-0.5))
GN_EPS = 64e-5

NE, NG, EPG, DE = 32, 4, 8, 512
RING = 4
UC = 512


def bucket_of(dist):
    n = np.maximum(dist, 0)
    nf = np.maximum(n, 1).astype(np.float32)
    large = 16 + (np.log(nf / np.float32(16)) / np.float32(np.log(64.0)) * np.float32(16)).astype(np.int32)
    return np.where(n < 16, n, np.minimum(large, 31))


def constants():
    i = np.arange(P)
    parts = {}
    parts["ident"] = np.eye(P)
    parts["flip"] = np.eye(P)[::-1]
    parts["headones"] = (i[:, None] // HD == i[None, :] // HD)
    parts["strict_incl"] = np.concatenate([i[:, None] < i[None, :], i[:, None] <= i[None, :]], 1)
    level = []
    for b in (1, 2, 4, 8, 16, 32, 64):
        blk = i // b
        lower = (blk[:, None] // 2 == blk[None, :] // 2) & (blk[:, None] % 2 == 1) & (blk[None, :] % 2 == 0)
        level.append(lower.T if b == 1 else lower)
    parts["levels"] = np.concatenate(level, 1)
    y = 255 - np.arange(512)
    hot = np.zeros((P, 512))
    hot[np.where(y >= 0, bucket_of(y), NBK), np.arange(512)] = 1
    parts["hot"] = hot
    parts["headsel"] = np.arange(2)[None, :] == (i // HD)[:, None]
    parts["cmp_rows"] = (i[:, None] + P * np.arange(NT)[None, :]) >= CMP_L - 1
    parts["desc4"] = np.broadcast_to(4.0 - np.arange(4), (P, 4))
    parts["desc8"] = np.broadcast_to(8.0 - np.arange(8), (P, 8))
    parts["ones"] = np.ones((P, P))
    parts["noughts"] = np.zeros((P, UC))
    at, n = {}, 0
    for k, v in parts.items():
        at[k] = (n, n + v.shape[1])
        n += v.shape[1]
    return np.concatenate([np.asarray(v, np.float32) for v in parts.values()], 1), at


class Chain:

    def __init__(self, eng, sem):
        self.eng, self.sem, self.n = eng, sem, 0

    def __call__(self, ins):
        self.n += 1
        ins.then_inc(self.sem, 1)
        self.eng.wait_ge(self.sem, self.n)


class Stream:

    def __init__(self, slots, sems):
        self.slots, self.sems = slots, sems
        self.src = []
        self.need = {}
        self.done = {}
        self.issued = 0

    def count(self):
        loads = [0] * RING
        for n, src in enumerate(self.src):
            if src is not None:
                loads[n % RING] += 1
                self.need[n] = 16 * loads[n % RING]

    def view(self, n):
        _, kc, cols = self.src[n]
        return self.slots[:, n % RING, 0:kc * cols].rearrange("p (k c) -> p k c", k=kc)

    def arrived(self, pe, n):
        pe.wait_ge(self.sems[n % RING], self.need[n])
        return self.view(n)

    def load(self, sp, n):
        src, kc, cols = self.src[n]
        before = [u for u in range(n - RING, -1, -RING) if self.src[u] is not None][:1]
        if before and before[0] in self.done:
            sp.wait_ge(*self.done[before[0]])
        sp.dma_start(self.view(n), src).then_inc(self.sems[n % RING], 16)

    def prefetch(self, sp, end):
        while self.issued < min(end + RING, len(self.src)):
            if self.src[self.issued] is not None:
                self.load(sp, self.issued)
            self.issued += 1


def program(nc, a, out, at, dumps=()):
    with ExitStack() as ctx:
        seen = {}

        def sb(name, shape, dt=F32, on=None):
            seen[name] = seen.get(name, 0) + 1
            name = name if seen[name] == 1 else f"{name}_{seen[name]}"
            return (on or ctx).enter_context(nc.sbuf_tensor(name, shape, dt))

        used, cooling = [], []

        def sem(name):
            used.append(nc.alloc_semaphore(name=f"{name}_{len(seen)}_{len(used)}"))
            return used[-1]

        def end_stage():
            for s in cooling:
                nc.release_semaphore(s)
            cooling[:] = used
            for s in used:
                nc.gpsimd.sem_clear(s)
            used.clear()
            stream.done.clear()

        @contextmanager
        def meeting():
            with nc.Block() as block:
                yield block
            end_stage()

        ps = ctx.enter_context(nc.psum_tensor("ps", [P, 8, 512], F32))
        slots = sb("weight_slots", [P, RING, KD * UC])
        n_const = max(e for _, e in at.values())
        const = sb("const", [P, n_const])
        x = sb("x", [P, NT, D])
        hT = sb("hT", [P, KD, S])

        def c_(name):
            lo, hi = at[name]
            return const[:, lo:hi]

        ident = c_("ident")

        def dump(name, t):
            if name in dumps:
                dd = nc.dram_tensor("dump_" + name, list(t.shape), F32, kind="ExternalOutput").ap()
                ds = sem("dump")
                with meeting() as block:
                    @block.sync
                    def _(sp):
                        sp.dma_start(dd, t[tuple(slice(None) for _ in t.shape)]).then_inc(ds, 16)
                        sp.wait_ge(ds, 16)

        stream = Stream(slots, [ctx.enter_context(nc.semaphore(f"weights_landed_{s}")) for s in range(RING)])
        unit = {}

        def kxn(w, r0, rows, c0, cols):
            return (w[r0:r0 + rows, c0:c0 + cols].rearrange("(k p) c -> p k c", p=P), rows // P, cols)

        def plan(name, *views):
            unit[name] = len(stream.src)
            stream.src.extend(views)

        def gap():
            while len(stream.src) % RING:
                stream.src.append(None)

        def columns(w, c0, c1, rows=D):
            return [kxn(w, 0, rows, c, min(UC, c1 - c)) for c in range(c0, c1, UC)]

        def mlp_units(layer):
            v = []
            for j in range(FF // UC):
                v.append(kxn(a["w_up"][layer], 0, D, j * UC, UC))
                v.append(kxn(a["w_down"][layer], j * UC, UC, 0, D))
            return v

        a_w, b_w, w2 = a["a_w_in"][0], a["b_w_in"][0], a["w_in_2"][0]
        Z0 = R_COLS
        X0 = Z0 + SW
        T0 = X0 + XBC
        G0 = T0 + SH
        QG = CONV_CH + 3 * NH
        plan("mem_kv", *[kxn(a["mem_w_kv"][l], 0, D, 0, 2 * MW) for l in range(2)])
        plan("a_in", *columns(a_w, 0, 3 * CONV_CH + MW))
        plan("out0", *columns(a["w_out"][0], 0, D))
        gap()
        plan("mlp0", *mlp_units(0))
        plan("kv", *columns(a["w_kv_shared"], 0, 6 * G * HD))
        plan("cmp1", *[kxn(a["cmp_w1"][i], 0, CMP_L * HD, 0, CMP_H) for i in range(2)])
        plan("b_in", kxn(b_w, 0, D, 0, UC), kxn(b_w, 0, D, UC, QG - UC), kxn(b_w, 0, D, QG, MW))
        plan("out1", *columns(a["w_out"][1], 0, D))
        gap()
        plan("mlp1", *mlp_units(1))
        plan("rwkv", *columns(w2, 0, R_COLS))
        plan("up_rwkv", *columns(a["w_up_rwkv_2"][0], 0, D))
        plan("xbc", *columns(w2, X0, T0))
        plan("dt", kxn(w2, 0, D, T0, SH))
        plan("z", *columns(w2, Z0, X0))
        plan("up_ssd", *[kxn(a["w_up_ssd_2"][0], r * D, D, n * UC, UC) for n in range(2) for r in range(2)])
        plan("gate", *columns(w2, G0, G0 + 2 * D))
        plan("out2", *columns(a["w_out_2"][0], 0, D))
        gap()
        experts = []
        for e in range(NE):
            experts += [kxn(a["w_exp_gate_2"][0, e], 0, D, 0, DE), kxn(a["w_exp_up_2"][0, e], 0, D, 0, DE),
                        kxn(a["w_exp_down_2"][0, e], 0, DE, 0, D)]
        plan("moe", *experts)
        stream.count()

        def stage(name, n_jobs, produce, consume, on_vector=lambda j: j % 2 == 0, uses=(), loads=()):
            full, free_v, free_a = sem(name + "_full"), sem(name + "_free_v"), sem(name + "_free_a")
            chain_v, chain_a = sem(name + "_chain_v"), sem(name + "_chain_a")
            loaded = sem(name + "_loaded")
            n_banks = 8
            bank = lambda j: ps[:, j % n_banks]
            nth = [sum(on_vector(i) == on_vector(j) for i in range(j + 1)) for j in range(n_jobs)]
            with meeting() as block:
                @block.tensor
                def _(pe):
                    for j in range(n_jobs):
                        if j >= n_banks:
                            b = j - n_banks
                            pe.wait_ge(free_v if on_vector(b) else free_a, nth[b])
                        produce(pe, j, bank(j)).then_inc(full, 1)
                    for u, j in dict(uses).items():
                        stream.done[u] = (full, j + 1)

                @block.vector
                def _(dve):
                    chain = Chain(dve, chain_v)
                    for j in range(n_jobs):
                        if on_vector(j):
                            dve.wait_ge(full, j + 1)
                            consume(dve, j, bank(j), chain, True).then_inc(free_v, 1)

                @block.scalar
                def _(act):
                    chain = Chain(act, chain_a)
                    for j in range(n_jobs):
                        if not on_vector(j):
                            act.wait_ge(full, j + 1)
                            consume(act, j, bank(j), chain, False).then_inc(free_a, 1)

                @block.sync
                def _(sp):
                    for dst, src in loads:
                        sp.dma_start(dst, src).then_inc(loaded, 16)
                    if loads:
                        sp.wait_ge(loaded, 16 * len(loads))
                    if uses:
                        stream.prefetch(sp, max(dict(uses)) + 1)

        def copy(eng, vector, dst, src):
            return eng.tensor_copy(dst, src) if vector else eng.activation(dst, src, ACT.Copy)

        def feature_chunk(pe, u, c0, width, dst, src=None):
            w, h = stream.view(u), hT if src is None else src
            for k in range(KD):
                mm = pe.matmul(dst, w[:, k, c0:c0 + width], h[:, k, :], start=(k == 0), stop=(k == KD - 1))
            return mm

        def token_tile(pe, u, c0, width, t, dst, src=None, first=True, last=True):
            w, h = stream.view(u), hT if src is None else src
            kc = stream.src[u][1]
            for k in range(kc):
                mm = pe.matmul(dst, h[:, k, t * P:(t + 1) * P], w[:, k, c0:c0 + width],
                               start=(first and k == 0), stop=(last and k == kc - 1))
            return mm

        rows_of = [
            [("mem_norm", a["mem_norm"]), ("mix_norm", a["mix_norm"]), ("kv_norm", a["kv_norm"]),
             ("mlp_norm", a["mlp_norm"]), ("attn_norm", a["attn_norm_g_2"]), ("ffn_norm", a["ffn_norm_g_2"]),
             ("conv_w", a["a_conv_w"])],
            [("mu", a["rwkv_mu_2"]), ("w0", a["rwkv_w0_2"]), ("a0", a["rwkv_a0_2"]), ("k_k", a["rwkv_k_k_2"]),
             ("k_a", a["rwkv_k_a_2"]), ("r_k", a["rwkv_r_k_2"]), ("ssd_conv_b", a["ssd_conv_b_2"]),
             ("ssd_norm", a["ssd_norm_g_2"])],
            [("ssd_conv_w", a["ssd_conv_w_2"]), ("cmp_pos", a["cmp_pos"])],
        ]
        cols = sb("cols", [P, 3, P])
        col_at = {}
        n_loads = 0
        row_list = []
        for tile, group in enumerate(rows_of):
            r = 0
            for name, v in group:
                size = int(np.prod(v.shape))
                n = size // P
                col_at[name] = (tile, r)
                row_list.append((tile, r, n, bass.AP(v.tensor, v.offset, [[P, n], [1, P]])))
                r += n
            assert r <= P
        row_counts = [sum(n for t, _, n, _ in row_list if t == tile) for tile in range(3)]

        def col(name, i, n=1):
            tile, r = col_at[name]
            return cols[:, tile, r + i:r + i + n]

        gain_rows = [("q_gain", a["b_q_gain"], 64), ("k_gain", a["k_gain"], 192), ("mem_q_gain", a["mem_q_gain"], 128),
                     ("mem_k_gain", a["mem_k_gain"], 128), ("d_skip", a["ssd_d_2"], 32),
                     ("b_rg", a["b_router_group_2"], NG), ("b_re", a["b_router_expert_2"], NE)]
        ssd_cols = sb("ssd_cols", [SH, 4])
        gains = sb("gains", [P, sum(n for _, _, n in gain_rows)])
        g_at, r = {}, 0
        for name, _, n in gain_rows:
            g_at[name] = (r, n)
            r += n

        def everywhere(v, n, off=0):
            return bass.AP(v.tensor, v.offset + off, [[0, P], [1, n]])

        def gain(name, i=0, n=HD):
            lo = g_at[name][0] + i
            return gains[:, lo:lo + n]

        first = ctx.enter_context(ExitStack())
        dist = sb("dist_bias", [P, NH, 3 * P], on=first)
        acs_row = nc.dram_tensor("acs_row", [SH, S], F32, kind="Internal").ap()
        gate_row = nc.dram_tensor("gate_row", [NE, S], F32, kind="Internal").ap()
        dist_row = nc.dram_tensor("dist_row", [NH, 512], F32, kind="Internal").ap()
        cmp2 = sb("cmp_w2", [P, 2, 2, HD], on=first)
        mem_kT = sb("mem_kT", [P, 2, MW // P, M], on=first)
        mem_v = sb("mem_v", [P, 2, M // P, MW], on=first)

        def setup(mem, rows, table, hb):
            landed, bias_out, bias_in = sem("setup_landed"), sem("bias_row_out"), sem("bias_rows_in")
            turned, taken, cleared = sem("setup_turned"), sem("setup_taken"), sem("setup_cleared")
            n = 0
            with meeting() as block:
                @block.gpsimd
                def _(pool):
                    pool.memset(rows[:, :, :], 0.0).then_inc(cleared, 1)

                @block.sync
                def _(sp):
                    nonlocal n
                    for dst, src in [(x[:, :, :], a["x"][0].rearrange("(t p) d -> p t d", p=P)),
                                     (mem[:, :, :], a["mem"][0].rearrange("(t p) d -> p t d", p=P)),
                                     (const[:, :], a["const"])]:
                        sp.dma_start(dst, src).then_inc(landed, 16)
                        n += 1
                    stream.prefetch(sp, 0)
                    sp.wait_ge(cleared, 1)
                    for tile, r, k, src in row_list:
                        sp.dma_start(rows[r:r + k, tile, :], src).then_inc(landed, 16)
                        n += 1
                    sp.wait_ge(taken, 1)
                    sp.dma_start(dist_row, hb[0:NH, :]).then_inc(bias_out, 16)
                    sp.wait_ge(bias_out, 16)
                    sp.dma_start(dist[:, :, :], bass.AP(dist_row.tensor, 0, [[1, P], [512, NH], [1, 3 * P]]))\
                        .then_inc(bias_in, 16)
                    sp.wait_ge(bias_in, 16)

                @block.scalar
                def _(act):
                    nonlocal n
                    for name, v, k in gain_rows:
                        lo = g_at[name][0]
                        act.dma_start(gains[:, lo:lo + k], everywhere(v, k)).then_inc(landed, 16)
                        n += 1
                    for i, v in enumerate((a["ssd_dt_bias_2"], a["ssd_a_log_2"])):
                        act.dma_start(ssd_cols[:, i:i + 1], bass.AP(v.tensor, v.offset, [[1, SH], [1, 1]]))\
                            .then_inc(landed, 16)
                        n += 1
                    act.dma_start(cmp2[:, :, :, :], a["cmp_w2"].rearrange("i (k p) d -> p i k d", p=P))\
                        .then_inc(landed, 16)
                    act.wait_ge(cleared, 2)
                    act.dma_start(table[0:NBK, :], a["rel_bias"]).then_inc(landed, 16)
                    n += 2

                @block.tensor
                def _(pe):
                    pe.wait_ge(cleared, 2)
                    pe.wait_ge(landed, 16 * n)
                    pe.matmul(ps[0:NH, 3, :], table[0:NBK + 1, :], c_("hot")[0:NBK + 1, :],
                              start=True, stop=True).then_inc(turned, 1)
                    for i in range(3):
                        pe.transpose(ps[:, i, 0:P], rows[:, i, :], ident).then_inc(turned, 1)

                @block.vector
                def _(dve):
                    dve.wait_ge(cleared, 1)
                    dve.memset(table[:, :], NEG).then_inc(cleared, 1)
                    dve.wait_ge(turned, 1)
                    dve.tensor_copy(hb[0:NH, :], ps[0:NH, 3, :]).then_inc(taken, 1)
                    dve.wait_ge(turned, 4)
                    for i in range(3):
                        dve.tensor_copy(cols[:, i, :], ps[:, i, 0:P]).then_inc(taken, 1)

        def norm(name, src, outs):
            with ExitStack() as on:
                scaled = sb(name + "_scaled", [P, NT, D], on=on)
                stat = sb(name + "_stat", [P, 4, NT], on=on)
                squares, roots, scale = sem(name + "_squares"), sem(name + "_roots"), sem(name + "_scale")
                turned, free_v, free_a = sem(name + "_turned"), sem(name + "_free_v"), sem(name + "_free_a")
                with meeting() as block:
                    @block.scalar
                    def _(act):
                        for t in range(NT):
                            act.activation(scaled[:, t, :], src[:, t, :], ACT.Square,
                                           accum_out=stat[:, 0, t:t + 1]).then_inc(squares, 1)
                        act.wait_ge(scale, 1)
                        act.activation(stat[:, 2, :], stat[:, 1, :], ACT.Sqrt).then_inc(roots, 1)
                        for c in range(1, KD, 2):
                            act.wait_ge(turned, c + 1)
                            for gname, g0, dst in outs:
                                last = act.activation(dst[:, c, :], ps[:, c % 8, 0:S], ACT.Copy,
                                                      scale=col(gname, g0 + c))

                    @block.vector
                    def _(dve):
                        dve.wait_ge(squares, NT)
                        dve.tensor_scalar(stat[:, 1, :], stat[:, 0, :], 1.0 / D, EPS, ALU.mult, ALU.add)\
                            .then_inc(scale, 1)
                        dve.wait_ge(roots, 1)
                        dve.reciprocal(stat[:, 3, :], stat[:, 2, :]).then_inc(scale, 1)
                        dve.wait_ge(scale, 2)
                        for t in range(NT):
                            dve.tensor_scalar(scaled[:, t, :], src[:, t, :], stat[:, 3, t:t + 1], None, ALU.mult)\
                                .then_inc(scale, 1)
                        for c in range(0, KD, 2):
                            dve.wait_ge(turned, c + 1)
                            for gname, g0, dst in outs:
                                dve.tensor_scalar(dst[:, c, :], ps[:, c % 8, 0:S], col(gname, g0 + c), None, ALU.mult)

                    @block.tensor
                    def _(pe):
                        pe.wait_ge(scale, 2 + NT)
                        for c in range(KD):
                            for t in range(NT):
                                mm = pe.transpose(ps[:, c % 8, t * P:(t + 1) * P],
                                                  scaled[:, t, c * P:(c + 1) * P], ident)
                            mm.then_inc(turned, 1)

        def head_norm(name, items, copies=()):
            sums, means, roots, scale = (sem(f"{name}_{s}") for s in ("squares", "means", "roots", "scale"))
            with meeting() as block:
                @block.scalar
                def _(act):
                    for dst, src, sq, st, g, k in items:
                        act.activation(sq, src, ACT.Square).then_inc(sums, 1)
                    for n, (dst, src, sq, st, g, k) in enumerate(items):
                        act.wait_ge(means, 2 * n + 2)
                        act.activation(st[:, 1], st[:, 0], ACT.Sqrt).then_inc(roots, 1)

                @block.vector
                def _(dve):
                    for n, (dst, src, sq, st, g, k) in enumerate(items):
                        dve.wait_ge(sums, n + 1)
                        dve.tensor_reduce(st[:, 0], sq, AX.X, ALU.add).then_inc(means, 1)
                        dve.wait_ge(means, 2 * n + 1)
                        dve.tensor_scalar(st[:, 0], st[:, 0], 1.0 / HD / (k * k), EPS / (k * k), ALU.mult, ALU.add)\
                            .then_inc(means, 1)
                    for dst, src in copies:
                        dve.tensor_copy(dst, src)
                    at = 0
                    for n, (dst, src, sq, st, g, k) in enumerate(items):
                        shape = list(src.shape)
                        dve.wait_ge(roots, n + 1)
                        dve.reciprocal(st[:, 0], st[:, 1]).then_inc(scale, 1)
                        dve.wait_ge(scale, at + 1)
                        dve.tensor_tensor(sq, src, st[:, 0].unsqueeze(3).broadcast_to(shape), ALU.mult)\
                            .then_inc(scale, 1)
                        dve.wait_ge(scale, at + 2)
                        for d in dst:
                            dve.tensor_tensor(d, sq, g.unsqueeze(1).unsqueeze(1).broadcast_to(shape), ALU.mult)
                        at += 2

        def heads(v):
            return v.rearrange("p t (h d) -> p t h d", d=HD)

        def memory(memT):
            with ExitStack() as on:
                kv = sb("mem_kv", [P, 2, NT, 2 * MW], on=on)
                kn = sb("mem_kn", [P, 2, NT, MW], on=on)
                sq = sb("mem_sq", [P, 2, NT, MW], on=on)
                st = sb("mem_st", [P, 2, 2, NT, MH], on=on)

                def produce(pe, j, bank):
                    layer, t = divmod(j, NT)
                    u = unit["mem_kv"] + layer
                    if t == 0:
                        stream.arrived(pe, u)
                    return token_tile(pe, u, 0, 2 * MW, t, bank, src=memT)

                def consume(eng, j, bank, chain, vector):
                    return copy(eng, vector, kv[:, j // NT, j % NT, :], bank)

                stage("mem_kv", 2 * NT, produce, consume,
                      uses={unit["mem_kv"] + l: l * NT + 1 for l in range(2)})
                head_norm("mem_k", [([heads(kn[:, l])], heads(kv[:, l, :, 0:MW]), heads(sq[:, l]), st[:, l],
                                     gain("mem_k_gain", l * HD), 1.0) for l in range(2)],
                          copies=[(mem_v[:, l], kv[:, l, :, MW:]) for l in range(2)])

                def turn(pe, j, bank):
                    layer, pair = divmod(j, MW // P)
                    for t in range(NT):
                        mm = pe.transpose(bank[:, t * P:(t + 1) * P], kn[:, layer, t, pair * P:(pair + 1) * P], ident)
                    return mm

                stage("mem_turn", 2 * MW // P, turn,
                      lambda eng, j, bank, chain, vector: copy(eng, vector, mem_kT[:, j // 2, j % 2, :], bank[:, 0:M]))

        def attention(name, groups, sums):
            items = []
            for g, grp in enumerate(groups):
                for h0 in range(0, len(grp["heads"]), grp["per"]):
                    hs = grp["heads"][h0:h0 + grp["per"]]
                    items.append((g, h0, hs, h0 + grp["per"] >= len(grp["heads"])))
            n = len(items)
            logits, top, probs, turned, turned_taken, given, combined = \
                (sem(f"{name}_{s}") for s in ("logits", "top", "probs", "turned", "turned_taken", "given", "combined"))
            chain_sem = sem(name + "_chain")
            exps = [0]
            for g, h0, hs, last in items:
                exps.append(exps[-1] + len(hs))
            with ExitStack() as on:
                nmax = sb(name + "_nmax", [P, 2, 4], on=on)
                probs_sb = sb(name + "_probs", [P, 2, 512], on=on)
                pT = sb(name + "_pT", [P, 2, 4 * P], on=on)
                coef = sb(name + "_coef", [P, 2, 12], on=on)
                part = sb(name + "_part", [P, CONV_CH], on=on)

                def bank_l(i):
                    return ps[:, i % 2]

                def bank_t(i):
                    return ps[:, 2 + i % 2]

                def bank_o(g):
                    return ps[:, 4 + 2 * (g % 2):6 + 2 * (g % 2)].rearrange("p b n -> p (b n)")

                with meeting() as block:
                    @block.tensor
                    def _(pe):
                        def scores(i):
                            g, h0, hs, last = items[i]
                            grp = groups[g]
                            nk = sum(grp["keys"])
                            if i >= 2:
                                pe.wait_ge(probs, exps[i - 1])
                            for n_h, h in enumerate(hs):
                                dst = bank_l(i)[:, n_h * nk:(n_h + 1) * nk]
                                bias = grp["bias"](h) if grp["bias"] else None
                                mm = pe.matmul(dst, grp["q"](h), grp["k"](h), start=True, stop=bias is None)
                                if bias is not None:
                                    mm = pe.matmul(dst, c_("flip"), bias, start=False, stop=True)
                            mm.then_inc(logits, 1)

                        def turn(i):
                            g, h0, hs, last = items[i]
                            grp = groups[g]
                            nk = sum(grp["keys"])
                            pe.wait_ge(probs, exps[i + 1])
                            if i >= 2:
                                pe.wait_ge(turned_taken, i - 1)
                            b = 0
                            for n_h in range(len(hs)):
                                k0 = 0
                                for w in grp["keys"]:
                                    lo = n_h * nk + k0
                                    mm = pe.transpose(bank_t(i)[0:w, b * P:(b + 1) * P],
                                                      probs_sb[:, i % 2, lo:lo + w], ident)
                                    k0 += w
                                    b += 1
                            mm.then_inc(turned, 1)

                        def values(i):
                            g, h0, hs, last = items[i]
                            grp = groups[g]
                            pe.wait_ge(turned_taken, i + 1)
                            if h0 == 0 and g >= 2:
                                pe.wait_ge(combined, g - 1)
                            b = 0
                            for n_h, h in enumerate(hs):
                                at_h = h * HD
                                for kt, w in enumerate(grp["keys"]):
                                    mm = pe.matmul(bank_o(g)[:, at_h:at_h + HD], pT[0:w, i % 2, b * P:(b + 1) * P],
                                                   grp["v"](h, kt), start=(kt == 0), stop=(kt == len(grp["keys"]) - 1))
                                    b += 1
                            mm.then_inc(given, 1)

                        scores(0)
                        for i in range(n):
                            if i + 1 < n:
                                scores(i + 1)
                            turn(i)
                            if i:
                                values(i - 1)
                        values(n - 1)

                    @block.vector
                    def _(dve):
                        chain = Chain(dve, chain_sem)

                        def maxima(i):
                            g, h0, hs, last = items[i]
                            nk = sum(groups[g]["keys"])
                            dve.wait_ge(logits, i + 1)
                            if i >= 2:
                                dve.wait_ge(probs, exps[i - 1])
                            dve.tensor_reduce(nmax[:, i % 2, 0:len(hs)],
                                              bank_l(i)[:, 0:len(hs) * nk].rearrange("p (h k) -> p h k", k=nk),
                                              AX.X, ALU.max, negate=True).then_inc(top, 1)

                        def take(i):
                            g, h0, hs, last = items[i]
                            w, nb = max(groups[g]["keys"]), len(hs) * len(groups[g]["keys"])
                            dve.wait_ge(turned, i + 1)
                            if i >= 2:
                                dve.wait_ge(given, i - 1)
                            dve.tensor_copy(pT[0:w, i % 2, 0:nb * P], bank_t(i)[0:w, 0:nb * P])\
                                .then_inc(turned_taken, 1)

                        def combine(g, i):
                            grp = groups[g]
                            nh = len(grp["heads"])
                            dve.wait_ge(probs, exps[i + 1])
                            k = coef[:, g % 2, 0:nh]
                            chain(dve.reciprocal(k, sums[:, grp["slot"], 0:nh]))
                            for m in grp["factors"]:
                                chain(dve.tensor_tensor(k, k, m, ALU.mult))
                            dve.wait_ge(given, i + 1)
                            o = bank_o(g)[:, 0:nh * HD].rearrange("p (h d) -> p h d", d=HD)
                            kb = k.unsqueeze(2).broadcast_to([P, nh, HD])
                            dst = grp["out"]
                            if grp["add"]:
                                pv = part[:, 0:nh * HD].rearrange("p (h d) -> p h d", d=HD)
                                chain(dve.tensor_tensor(pv, o, kb, ALU.mult))
                                if g:
                                    dve.wait_ge(combined, g)
                                dve.tensor_tensor(dst, dst, pv, ALU.add).then_inc(combined, 1)
                            else:
                                dve.tensor_tensor(dst, o, kb, ALU.mult).then_inc(combined, 1)

                        for i in range(n + 2):
                            if i < n:
                                maxima(i)
                            if 1 <= i <= n:
                                take(i - 1)
                            if i >= 2 and items[i - 2][3]:
                                combine(items[i - 2][0], i - 2)

                    @block.scalar
                    def _(act):
                        for i in range(n):
                            g, h0, hs, last = items[i]
                            nk = sum(groups[g]["keys"])
                            act.wait_ge(top, i + 1)
                            if i >= 2:
                                act.wait_ge(turned, i - 1)
                            for n_h, h in enumerate(hs):
                                act.activation(probs_sb[:, i % 2, n_h * nk:(n_h + 1) * nk],
                                               bank_l(i)[:, n_h * nk:(n_h + 1) * nk], ACT.Exp,
                                               bias=nmax[:, i % 2, n_h:n_h + 1],
                                               accum_out=sums[:, groups[g]["slot"], h:h + 1])\
                                    .then_inc(probs, 1)

        def add_projection(name, u0, src):
            def produce(pe, j, bank):
                half, t = divmod(j, NT)
                if t == 0:
                    stream.arrived(pe, u0 + half)
                return token_tile(pe, u0 + half, 0, UC, t, bank, src=src)

            def consume(eng, j, bank, chain, vector):
                half, t = divmod(j, NT)
                dst = x[:, t, half * UC:(half + 1) * UC]
                return eng.tensor_tensor(dst, dst, bank, ALU.add)

            stage(name, 2 * NT, produce, consume, on_vector=lambda j: True,
                  uses={u0: NT - 1, u0 + 1: 2 * NT - 1})

        def turn_into(name, src, chunks, dst, dst0=0, scale=None):
            def produce(pe, j, bank):
                for t in range(NT):
                    mm = pe.transpose(bank[:, t * P:(t + 1) * P], src[:, t, j * P:(j + 1) * P], ident)
                return mm

            def consume(eng, j, bank, chain, vector):
                if scale is None:
                    return copy(eng, vector, dst[:, dst0 + j, :], bank[:, 0:S])
                if vector:
                    return eng.tensor_scalar(dst[:, dst0 + j, :], bank[:, 0:S], scale(j), None, ALU.mult)
                return eng.activation(dst[:, dst0 + j, :], bank[:, 0:S], ACT.Copy, scale=scale(j))

            stage(name, chunks, produce, consume)

        def close_sums(pe):
            for b in range(4, 8):
                mm = pe.matmul(ps[:, b], c_("noughts")[:, 0:P], c_("noughts"), start=False, stop=True)
            return mm

        def mlp(layer):
            u0 = unit[f"mlp{layer}"]
            n_units = 2 * FF // UC
            trips = n_units // RING
            up_v = a["w_up"][layer].rearrange("(k p) (i b c) -> i b p k c", p=P, b=2, c=UC)
            down_v = a["w_down"][layer].rearrange("(i b k p) c -> i b p k c", p=P, b=2, k=UC // P)
            ups, rect, hid_ready, downs, taken = \
                (sem(f"mlp{layer}_{s}") for s in ("ups", "rectified", "hidden", "downs", "taken"))
            nm = UC // P
            with ExitStack() as on:
                hid = sb("hid", [P, nm, S], on=on)
                rec = sb("rec", [P, nm, S], on=on)

                def up_chunk(m):
                    return ps[:, m // 2, (m % 2) * S:(m % 2 + 1) * S]

                def both(buf, b):
                    return buf[:, 2 * b:2 * b + 2, :].rearrange("p m s -> p (m s)")

                nb = nm // 2

                with meeting() as block:
                    @block.tensor
                    def _(pe):
                        for t in range(NT):
                            for h in range(2):
                                pe.matmul(ps[:, 4 + 2 * t + h], ident, x[:, t, h * UC:(h + 1) * UC],
                                          start=True, stop=False)
                        with pe.Fori(0, trips) as i:
                            for b in range(2):
                                u = u0 + 2 * b
                                w = stream.view(u)
                                pe.wait_ge(stream.sems[u % RING], i * 16 + stream.need[u])
                                for m in range(nm):
                                    for k in range(KD):
                                        mm = pe.matmul(up_chunk(m), w[:, k, m * P:(m + 1) * P], hT[:, k, :],
                                                       start=(k == 0), stop=(k == KD - 1))
                                    if m % 2:
                                        mm.then_inc(ups, 1)
                                u += 1
                                w = stream.view(u)
                                pe.wait_ge(stream.sems[u % RING], i * 16 + stream.need[u])
                                for f in range(nm):
                                    if f % 2 == 0:
                                        pe.wait_ge(hid_ready, i * (2 * nb) + (b * nb + f // 2 + 1))
                                    for t in range(NT):
                                        for h in range(2):
                                            mm = pe.matmul(ps[:, 4 + 2 * t + h], hid[:, f, t * P:(t + 1) * P],
                                                           w[:, f, h * UC:(h + 1) * UC], start=False, stop=False,
                                                           skip_group_check=True)
                                mm.then_inc(downs, 1)
                        close_sums(pe).then_inc(downs, 1)

                    @block.scalar
                    def _(act):
                        with act.Fori(0, trips) as i:
                            for b in range(2):
                                for m in range(nb):
                                    act.wait_ge(ups, i * (2 * nb) + (b * nb + m + 1))
                                    act.activation(both(rec, m), ps[:, m], ACT.Relu).then_inc(rect, 1)

                    @block.vector
                    def _(dve):
                        with dve.Fori(0, trips) as i:
                            for b in range(2):
                                for m in range(nb):
                                    dve.wait_ge(rect, i * (2 * nb) + (b * nb + m + 1))
                                    dve.tensor_tensor(both(hid, m), both(rec, m), both(rec, m), ALU.mult)\
                                        .then_inc(hid_ready, 1)
                        dve.wait_ge(downs, 2 * trips + 1)
                        for t in range(NT):
                            for h in range(2):
                                dve.tensor_copy(x[:, t, h * UC:(h + 1) * UC], ps[:, 4 + 2 * t + h])

                    @block.sync
                    def _(sp):
                        stream.prefetch(sp, u0)
                        with sp.Fori(0, trips - 1) as i:
                            for b in range(2):
                                for kind, v in enumerate((up_v, down_v)):
                                    u = u0 + 2 * b + kind
                                    if kind == 0:
                                        sp.wait_ge(ups, i * (2 * nb) + (b + 1) * nb)
                                    else:
                                        sp.wait_ge(downs, i * 2 + (b + 1))
                                    sp.dma_start(stream.view(u), v[i + 1, b]).then_inc(stream.sems[u % RING], 16)
                        for b in range(2):
                            stream.done[u0 + n_units - RING + 2 * b] = (ups, (2 * trips - 1 + b) * nb)
                            stream.done[u0 + n_units - RING + 2 * b + 1] = (downs, 2 * trips - 1 + b)
                        stream.issued = u0 + n_units
                        stream.prefetch(sp, u0 + n_units)

        def conv_layer():
            with ExitStack() as on:
                z = sb("conv_z", [P, 3 * CONV_CH // P, S], on=on)
                q = sb("conv_q", [P, NT, MW], on=on)
                nconv = CONV_CH // P
                cat = sb("cat", [P, KD, S], on=on)
                u0 = unit["a_in"]
                n_fm = 3 * nconv

                def produce(pe, j, bank):
                    if j < n_fm:
                        if j % 4 == 0:
                            stream.arrived(pe, u0 + j // 4)
                        return feature_chunk(pe, u0 + j // 4, (j % 4) * P, P, bank[:, 0:S])
                    return token_tile(pe, u0 + 4, 2 * P, MW, j - n_fm, bank[:, 0:MW])

                def consume(eng, j, bank, chain, vector):
                    dst = z[:, j, :] if j < n_fm else q[:, j - n_fm, :]
                    return copy(eng, vector, dst, bank[:, 0:S])

                stage("a_in", n_fm + NT, produce, consume,
                      uses={u0: 3, u0 + 1: 7, u0 + 2: 11, u0 + 3: 15, u0 + 4: n_fm + NT - 1})

                conv_step = sem("conv_step")
                with meeting() as block:
                    @block.vector
                    def _(dve):
                        n = 0
                        gb, gc, gu = (z[:, i * nconv:(i + 1) * nconv, :] for i in range(3))
                        dve.tensor_tensor(gc, gc, gu, ALU.mult).then_inc(conv_step, 1)
                        n += 1
                        dve.wait_ge(conv_step, n)
                        for c in range(nconv):
                            dve.tensor_scalar(gu[:, c, :], gc[:, c, :], col("conv_w", 2 * nconv + c), None, ALU.mult)\
                                .then_inc(conv_step, 1)
                        n += nconv
                        dve.wait_ge(conv_step, n)
                        for tap in (1, 0):
                            back = 2 - tap
                            for c in range(nconv):
                                dve.scalar_tensor_tensor(gu[:, c, back:], gc[:, c, 0:S - back],
                                                         col("conv_w", tap * nconv + c), gu[:, c, back:],
                                                         ALU.mult, ALU.add).then_inc(conv_step, 1)
                            n += nconv
                            dve.wait_ge(conv_step, n)
                        dve.tensor_tensor(cat[:, 0:nconv, :], gb, gu, ALU.mult)
                memory_attention(0, q, cat, nconv)
                add_projection("out0", unit["out0"], cat)

        def memory_attention(layer, q, cat, chunk0, more=None, more_norms=(), gates=None):
            with ExitStack() as on:
                qn = sb("mq_n", [P, NT, MW], on=on)
                sq = sb("mq_sq", [P, NT, MW], on=on)
                st = sb("mq_st", [P, 2, NT, MH], on=on)
                qT = sb("mq_T", [P, MW // P, S], on=on)
                ym = sb("ym", [P, NT, MW], on=on)
                sums = sb("mq_sums", [P, NT, MH], on=on)
                head_norm(f"mq{layer}", [([heads(qn)], heads(q), heads(sq), st,
                                          gain("mem_q_gain", layer * HD), HD ** -0.5)])
                turn_into(f"mq_turn{layer}", qn, MW // P, qT)
                groups = []
                for t in range(NT):
                    groups.append(dict(
                        heads=[0, 2, 1, 3], per=2, keys=[P, P], bias=None, slot=t, factors=[], add=False,
                        q=lambda h, t=t: qT[(h % 2) * HD:(h % 2 + 1) * HD, h // 2, t * P:(t + 1) * P],
                        k=lambda h: mem_kT[(h % 2) * HD:(h % 2 + 1) * HD, layer, h // 2, :],
                        v=lambda h, kt: mem_v[:, layer, kt, h * HD:(h + 1) * HD],
                        out=ym[:, t, :].rearrange("p (h d) -> p h d", d=HD)))
                attention(f"mem_attn{layer}", groups, sums)
                turn_into(f"ym_turn{layer}", ym, MW // P, cat, chunk0)

        def shared_buffers(on):
            return dict(
                kT={b: sb(f"{b}_kT", [P, G, S], on=on) for b in ("s", "w")},
                v={b: sb(f"{b}_v", [P, NT, G * HD], on=on) for b in ("s", "w")},
                kcT=sb("c_kT", [P, G, NC], on=on), vc=sb("c_v", [NC, G, HD], on=on))

        def shared_kv(sh, hkv):
            with ExitStack() as on2:
                kv = sb("kv_rest", [P, NT, 4 * G * HD], on=on2)
                pair = sb("cmp_pairs", [P, 2, G, S], on=on2)
                flat = sb("cmp_flat", [P, 2, CMP_L // 2, G * NC], on=on2)
                u0 = unit["kv"]

                def produce(pe, j, bank):
                    if j == 0:
                        stream.arrived(pe, u0)
                    if j == 2 + NT:
                        stream.arrived(pe, u0 + 1)
                    if j < 2:
                        return feature_chunk(pe, u0, j * P, P, bank[:, 0:S], src=hkv)
                    second, t = divmod(j - 2, NT)
                    return token_tile(pe, u0 + second, 0 if second else 2 * P, 2 * P, t, bank[:, 0:2 * P], src=hkv)

                def consume(eng, j, bank, chain, vector):
                    if j < 2:
                        for g in range(G):
                            src = bank[g * HD:(g + 1) * HD, 0:S]
                            eng.tensor_copy(pair[0:HD, j, g, :], src)
                            last = eng.tensor_copy(pair[HD:P, j, g, 0:S - 1], src[:, 1:S])
                            if g == 0:
                                chain(last)
                        return last
                    second, t = divmod(j - 2, NT)
                    return copy(eng, vector, kv[:, t, second * 2 * P:(second + 1) * 2 * P], bank[:, 0:2 * P])

                stage("kv", 2 + 2 * NT, produce, consume, on_vector=lambda j: j < 2 or j % 2 == 0,
                      uses={u0: 1 + NT, u0 + 1: 1 + 2 * NT})

                half = CMP_S // 2
                with meeting() as block:
                    @block.vector
                    def _(dve):
                        for i in range(2):
                            for g in range(G):
                                for part in range(2):
                                    src = pair[:, i, g, part * CMP_S:part * CMP_S + NC * CMP_S]\
                                        .rearrange("p (c l two) -> p l c two", c=NC, two=2)[:, :, :, 0]
                                    pos = col("cmp_pos", i * CMP_L // 2 + part * half, half)
                                    dve.tensor_tensor(flat[:, i, part * half:(part + 1) * half, g * NC:(g + 1) * NC],
                                                      src, pos.unsqueeze(2).broadcast_to([P, half, NC]), ALU.add)

                hidden = sb("cmp_hidden", [G * NC, 2, CMP_H], on=on2)
                u1 = unit["cmp1"]

                def mlp1(pe, j, bank):
                    w = stream.arrived(pe, u1 + j)
                    for k in range(CMP_L // 2):
                        mm = pe.matmul(bank[0:G * NC, 0:CMP_H], flat[:, j, k, :], w[:, k, :],
                                       start=(k == 0), stop=(k == CMP_L // 2 - 1))
                    return mm

                stage("cmp1", 2, mlp1, lambda eng, j, bank, chain, vector:
                      eng.activation(hidden[:, j, :], bank[0:G * NC, 0:CMP_H], ACT.Gelu_apprx_tanh),
                      on_vector=lambda j: False, uses={u1: 0, u1 + 1: 1})
                hiddenT = sb("cmp_hiddenT", [P, 2, 2, G * NC], on=on2)

                def turn(pe, j, bank):
                    for k in range(2):
                        mm = pe.transpose(bank[:, k * P:k * P + G * NC], hidden[:, j, k * P:(k + 1) * P],
                                          ident[0:G * NC, 0:G * NC])
                    return mm

                stage("cmp_turn", 2, turn, lambda eng, j, bank, chain, vector:
                      copy(eng, vector, hiddenT[:, j, :, :],
                           bank[:, 0:2 * P].rearrange("p (k n) -> p k n", k=2)[:, :, 0:G * NC]))
                kc = sb("cmp_k", [NC, 1, G, HD], on=on2)
                dup = sb("kn_dup", [P, 2, NT, G, 2, HD], on=on2)
                cdup = sb("kc_dup", [NC, G, 2, HD], on=on2)

                def mlp2(pe, j, bank):
                    for g in range(G):
                        for k in range(2):
                            mm = pe.matmul(bank[0:NC, g * HD:(g + 1) * HD], hiddenT[:, j, k, g * NC:(g + 1) * NC],
                                           cmp2[:, j, k, :], start=(k == 0), stop=(k == 1))
                    return mm

                stage("cmp2", 2, mlp2, lambda eng, j, bank, chain, vector:
                      eng.tensor_copy(kc[:, 0] if j == 0 else sh["vc"][:, :, :],
                                      bank[0:NC, 0:G * HD].rearrange("p (g d) -> p g d", g=G)),
                      on_vector=lambda j: True)
                sq = sb("kn_sq", [P, 3, NT, G, HD], on=on2)
                st = sb("kn_st", [P, 3, 2, NT, G], on=on2)
                items = [([cdup[:, :, w].unsqueeze(1) for w in range(2)], kc[:, :, :, :], sq[0:NC, 2, 0:1],
                          st[0:NC, 2, :, 0:1], gain("k_gain", 0)[0:NC, :], 1.0)]
                for b in range(2):
                    src = heads(kv[:, :, 2 * b * P:(2 * b + 1) * P])
                    items.append(([dup[:, b, :, :, w] for w in range(2)], src, sq[:, b], st[:, b],
                                  gain("k_gain", (1 + b) * HD), 1.0))
                head_norm("kn", items, copies=[(sh["v"][b][:, :, :], kv[:, :, (2 * n + 1) * P:(2 * n + 2) * P])
                                               for n, b in enumerate(("s", "w"))])

                def turn_keys(pe, j, bank):
                    if j == 2 * G:
                        for g in range(G):
                            mm = pe.transpose(bank[:, g * P:g * P + NC], cdup[:, g].rearrange("p a d -> p (a d)"),
                                              ident[0:NC, 0:NC])
                        return mm
                    b, g = divmod(j, G)
                    for t in range(NT):
                        mm = pe.transpose(bank[:, t * P:(t + 1) * P], dup[:, b, t, g].rearrange("p a d -> p (a d)"),
                                          ident)
                    return mm

                def take_keys(eng, j, bank, chain, vector):
                    if j == 2 * G:
                        return copy(eng, vector, sh["kcT"][:, :, :],
                                    bank[:, 0:G * P].rearrange("p (g n) -> p g n", g=G)[:, :, 0:NC])
                    b, g = divmod(j, G)
                    return copy(eng, vector, sh["kT"]["sw"[b]][:, g, :], bank[:, 0:S])

                stage("kn_turn", 2 * G + 1, turn_keys, take_keys)

        def nsa_layer(sh):
            with ExitStack() as on:
                q = sb("nsa_q", [P, NT, CONV_CH], on=on)
                gates = sb("nsa_gates", [P, NT, NH, 3], on=on)
                mq = sb("nsa_mq", [P, NT, MW], on=on)
                qT = sb("nsa_qT", [P, NH // 2, S], on=on)
                y = sb("nsa_y", [P, NT, CONV_CH], on=on)
                sums = sb("nsa_sums", [P, 3 * NT, NH], on=on)
                cat = sb("cat", [P, KD, S], on=on)
                u0 = unit["b_in"]
                rest = CONV_CH - UC
                with ExitStack() as on2:
                    qn = sb("nsa_qn", [P, NT, CONV_CH], on=on2)
                    sq = sb("nsa_sq", [P, NT, CONV_CH], on=on2)
                    st = sb("nsa_st", [P, 2, NT, NH], on=on2)

                    def produce(pe, j, bank):
                        part, t = divmod(j, NT)
                        width = stream.src[u0 + part][2]
                        if t == 0:
                            stream.arrived(pe, u0 + part)
                        return token_tile(pe, u0 + part, 0, width, t, bank[:, 0:width])

                    def consume(eng, j, bank, chain, vector):
                        part, t = divmod(j, NT)
                        if part == 0:
                            return eng.activation(q[:, t, 0:UC], bank, ACT.Copy)
                        if part == 1:
                            eng.activation(q[:, t, UC:], bank[:, 0:rest], ACT.Copy)
                            return eng.activation(gates[:, t], bank[:, rest:rest + 3 * NH]
                                                  .rearrange("p (h b) -> p h b", b=3), ACT.Sigmoid)
                        return eng.activation(mq[:, t, :], bank[:, 0:MW], ACT.Copy)

                    stage("b_in", 3 * NT, produce, consume, on_vector=lambda j: False,
                          uses={u0 + i: i * NT + 1 for i in range(3)})
                    head_norm("nsa_q", [([heads(qn)], heads(q), heads(sq), st, gain("q_gain"), HD ** -0.5)])
                    turn_into("nsa_qturn", qn, NH // 2, qT)
                groups = []
                for t in range(NT):
                    yt = y[:, t, :].rearrange("p (h d) -> p h d", d=HD)
                    x0 = P * (1 - t)
                    for n, b in enumerate(("c", "s", "w")):
                        grp = dict(
                            heads=[*range(0, NH, 2), *range(1, NH, 2)], slot=t * 3 + n, out=yt, add=n > 0,
                            q=lambda h, t=t: qT[(h % 2) * HD:(h % 2 + 1) * HD, h // 2, t * P:(t + 1) * P],
                            factors=[gates[:, t, :, n]])
                        if b == "c":
                            grp["factors"].append(c_("cmp_rows")[:, t:t + 1].broadcast_to([P, NH]))
                            grp.update(per=3, keys=[NC],
                                       k=lambda h: sh["kcT"][(h % 2) * HD:(h % 2 + 1) * HD, h // HPG, :],
                                       v=lambda h, kt: sh["vc"][:, h // HPG, :],
                                       bias=lambda h, x0=x0: dist[:, h, x0 + CMP_L - 1:x0 + CMP_L + (NC - 1) * CMP_S:CMP_S])
                        else:
                            nk = (t + 1) * P
                            grp.update(per=3 - t, keys=[P] * (t + 1),
                                       k=lambda h, b=b, nk=nk: sh["kT"][b][(h % 2) * HD:(h % 2 + 1) * HD, h // HPG, 0:nk],
                                       v=lambda h, kt, b=b: sh["v"][b][:, kt, (h // HPG) * HD:(h // HPG + 1) * HD],
                                       bias=lambda h, x0=x0, nk=nk: dist[:, h, x0:x0 + nk])
                        groups.append(grp)
                attention("nsa", groups, sums)
                turn_into("nsa_yturn", y, CONV_CH // P, cat)
                memory_attention(1, mq, cat, CONV_CH // P)
                add_projection("out1", unit["out1"], cat)


        def rwkv(ya):
            with ExitStack() as on:
                lora = sb("rw_lora", [P, 2, S], on=on)
                v = sb("rw_v", [P, RC, S], on=on)
                qr = sb("rw_qr", [P, RC, NT, 2 * P], on=on)
                bh = sb("rw_b", [P, RC, S], on=on)
                kh = sb("rw_k", [P, RC, S], on=on)
                kk = sb("rw_kk", [P, RC, S], on=on)
                mid = sb("rw_mid", [P, 4, RC * NT], on=on)
                carry = sb("rw_carry", [P, 2, RC], on=on)
                u0 = unit["rwkv"]
                with ExitStack() as on2:
                    r = sb("rw_r", [P, RC, S], on=on2)
                    k = sb("rw_kraw", [P, RC, S], on=on2)
                    dec = sb("rw_dec", [P, RC, S], on=on2)
                    aa = sb("rw_a", [P, RC, S], on=on2)
                    tmp = sb("rw_tmp", [P, RC, S], on=on2)
                    sums = sb("rw_sums", [P, RC, NT, P + 1], on=on2)
                    w_da = sums[:, :, :, :].rearrange("p c t n -> p (c t n)")[:, 0:RW]
                    shifted = tmp[:, :, :].rearrange("p c s -> p (c s)")[:, 0:2 * (S + 1)]\
                        .rearrange("p (n s) -> p n s", n=2)
                    raw = lambda j: (r, k, v, lora)[j // RC][:, j % RC, :]

                    def produce(pe, j, bank):
                        if j % 4 == 0:
                            stream.arrived(pe, u0 + j // 4)
                        return feature_chunk(pe, u0 + j // 4, (j % 4) * P, P, bank[:, 0:S])

                    def consume(eng, j, bank, chain, vector):
                        if j == 0:
                            chain(eng.memset(shifted[:, :, 0:1], 0.0))
                        sh = shifted[:, j % 2]
                        chain(eng.tensor_scalar(sh[:, 1:], bank[:, 0:S], col("mu", j), None, ALU.mult))
                        chain(eng.tensor_tensor(raw(j), bank[:, 0:S], sh[:, 1:], ALU.subtract))
                        return eng.tensor_tensor(raw(j), raw(j), sh[:, 0:S], ALU.add)

                    n_ch = R_COLS // P
                    stage("rwkv_in", n_ch, produce, consume, on_vector=lambda j: True,
                          uses={u0 + i: min(4 * i + 3, n_ch - 1) for i in range(7)},
                          loads=[(w_da[0:LORA, :], a["rwkv_w_decay_2"][0]), (w_da[LORA:P, :], a["rwkv_w_a_2"][0])])
                    lora_ready = sem("lora_ready")
                    with meeting() as block:
                        @block.scalar
                        def _(act):
                            act.activation(lora[0:LORA, 0, :], lora[0:LORA, 0, :], ACT.Tanh)
                            act.activation(lora[:, 1, :], lora[:, 1, :], ACT.Sigmoid)

                        @block.vector
                        def _(dve):
                            for c in range(RC):
                                dve.tensor_scalar(kk[:, c, :], k[:, c, :], col("k_k", c), None, ALU.mult)

                    def lora_up(pe, j, bank):
                        which, c = divmod(j, RC)
                        lo = which * LORA
                        return pe.matmul(bank[:, 0:S], w_da[lo:lo + LORA, c * P:(c + 1) * P],
                                         lora[lo:lo + LORA, 0, :], start=True, stop=True)

                    stage("lora_up", 2 * RC, lora_up, lambda eng, j, bank, chain, vector:
                          eng.activation((dec, aa)[j // RC][:, j % RC, :], bank[:, 0:S], ACT.Sigmoid,
                                         bias=col(("w0", "a0")[j // RC], j % RC)), on_vector=lambda j: False)

                    flat = lambda z: z[:, :, :].rearrange("p c s -> p (c s)")
                    squares, lengths, roots, made = (sem("kk_" + s) for s in ("squares", "lengths", "roots", "made"))
                    with meeting() as block:
                        @block.scalar
                        def _(act):
                            act.activation(flat(tmp), flat(kk), ACT.Square).then_inc(squares, 1)
                            for b in range(4):
                                act.wait_ge(lengths, b + 1)
                                act.activation(flat(tmp)[:, b * 512:(b + 1) * 512], ps[:, b], ACT.Sqrt).then_inc(roots, 1)

                        @block.tensor
                        def _(pe):
                            pe.wait_ge(squares, 1)
                            for b in range(4):
                                pe.matmul(ps[:, b], c_("headones"), flat(tmp)[:, b * 512:(b + 1) * 512],
                                          start=True, stop=True).then_inc(lengths, 1)

                        @block.vector
                        def _(dve):
                            chain = Chain(dve, made)
                            chain(dve.memset(sums[:, :, :, 0:1], 0.0))
                            for c in range(RC):
                                for t in range(NT):
                                    dve.tensor_tensor_scan(sums[:, c, t, 1:], c_("ones"), dec[:, c, t * P:(t + 1) * P],
                                                           0.0, ALU.mult, ALU.add)
                            dve.wait_ge(roots, 4)
                            chain(dve.tensor_scalar(flat(tmp), flat(tmp), 1e-12, None, ALU.max))
                            chain(dve.reciprocal(flat(dec), flat(tmp)))
                            chain(dve.tensor_tensor(flat(kk), flat(kk), flat(dec), ALU.mult))
                            middle = sums[:, :, :, P // 2].rearrange("p c t -> p (c t)")
                            dve.tensor_scalar(mid[:, 0, :], middle, KAPPA, None, ALU.mult)
                            chain(dve.tensor_scalar(mid[:, 1, :], middle, -KAPPA, None, ALU.mult))
                            chain(dve.tensor_tensor(carry[:, 1, :], sums[:, :, 0, P // 2], sums[:, :, 0, P], ALU.subtract))
                            chain(dve.tensor_tensor(carry[:, 1, :], carry[:, 1, :], sums[:, :, 1, P // 2], ALU.subtract))
                            k_a = col("k_a", 0, RC)
                            chain(dve.tensor_scalar(mid[:, 2, 0:RC], k_a, -1.0, 1.0, ALU.mult, ALU.add))
                            for c in range(RC):
                                dve.tensor_scalar(kh[:, c, :], aa[:, c, :], col("k_a", c), mid[:, 2, c:c + 1],
                                                  ALU.mult, ALU.add)
                            chain(dve.tensor_tensor(flat(bh), flat(kk), flat(aa), ALU.mult))
                            dve.tensor_tensor(flat(kh), flat(kh), flat(k), ALU.mult)

                    exps, scaled = sem("rw_exps"), sem("rw_scaled")
                    with meeting() as block:
                        @block.scalar
                        def _(act):
                            act.activation(carry[:, 0, :], carry[:, 1, :], ACT.Exp, scale=KAPPA)
                            for c in range(RC):
                                for t in range(NT):
                                    n = c * NT + t
                                    act.activation(qr[:, c, t, 0:P], sums[:, c, t, 0:P], ACT.Exp,
                                                   scale=-KAPPA, bias=mid[:, 0, n:n + 1])
                                    act.activation(qr[:, c, t, P:], sums[:, c, t, 1:], ACT.Exp,
                                                   scale=-KAPPA, bias=mid[:, 0, n:n + 1])
                                    act.activation(tmp[:, c, t * P:(t + 1) * P], sums[:, c, t, 1:], ACT.Exp,
                                                   scale=KAPPA, bias=mid[:, 1, n:n + 1]).then_inc(exps, 1)

                        @block.vector
                        def _(dve):
                            for c in range(RC):
                                dve.scalar_tensor_tensor(dec[:, c, :], r[:, c, :], col("r_k", c), kh[:, c, :],
                                                         ALU.mult, ALU.mult).then_inc(scaled, 1)
                            for c in range(RC):
                                dve.wait_ge(scaled, c + 1)
                                dve.wait_ge(exps, NT * (c + 1))
                                tiles = lambda z: z[:, c, :].rearrange("p (t s) -> p t s", t=NT)
                                dve.tensor_tensor(qr[:, c, :, 0:P], qr[:, c, :, 0:P], tiles(kk), ALU.mult)
                                dve.tensor_tensor(qr[:, c, :, P:], qr[:, c, :, P:], tiles(r), ALU.mult)
                                dve.tensor_tensor(bh[:, c, :], bh[:, c, :], tmp[:, c, :], ALU.mult)
                                dve.tensor_tensor(kh[:, c, :], kh[:, c, :], tmp[:, c, :], ALU.mult)
                                dve.wait_ge(scaled, RC)
                    with meeting() as block:
                        @block.vector
                        def _(dve):
                            dve.tensor_copy(flat(kk), flat(dec))
                v_tok = sb("rw_v_tok", [P, NT, RW], on=on)
                b_tok = sb("rw_b_tok", [P, RW], on=on)
                k_tok = sb("rw_k_tok", [P, RW], on=on)
                bonus = sb("rw_bonus", [P, NT, RH], on=on)
                turns = [(v, 0, v_tok[:, 0, :]), (v, 1, v_tok[:, 1, :]), (bh, 0, b_tok), (kh, 0, k_tok)]

                def turn(pe, j, bank):
                    if j == 8:
                        for t in range(NT):
                            for c in range(RC):
                                lo = t * RH + 2 * c
                                mm = pe.matmul(bank[:, lo:lo + 2], kk[:, c, t * P:(t + 1) * P], c_("headsel"),
                                               start=True, stop=True)
                        return mm
                    src, t, _ = turns[j // 2]
                    for i in range(4):
                        mm = pe.transpose(bank[:, i * P:(i + 1) * P], src[:, (j % 2) * 4 + i, t * P:(t + 1) * P], ident)
                    return mm

                def take(eng, j, bank, chain, vector):
                    if j == 8:
                        return copy(eng, vector, bonus[:, :, :], bank[:, 0:NT * RH].rearrange("p (t h) -> p t h", t=NT))
                    return copy(eng, vector, turns[j // 2][2][:, (j % 2) * 512:(j % 2 + 1) * 512], bank)

                stage("rw_turn", 9, turn, take)
                with ExitStack() as on2:
                    rwkv_tiles(on2, qr, bh, kh, v_tok, b_tok, k_tok, carry, ya)
                rwkv_out(ya, v_tok, bonus, lora)

        def rwkv_tiles(on, qr, bh, kh, v_tok, b_tok, k_tok, carry, ya):
            ac = sb("rw_ac", [P, 2, 4, 2 * P], on=on)
            bd = sb("rw_bd", [P, 2, 4, 2 * P], on=on)
            inv = sb("rw_inv", [P, 2, 4, P], on=on)
            invT = sb("rw_invT", [P, 2, 4, P], on=on)
            half = sb("rw_half", [P, 2, 4, P], on=on)
            w = sb("rw_w", [P, 2, P], on=on)
            uu = sb("rw_u", [P, 2, P], on=on)
            state = sb("rw_state", [P, 2, HD], on=on)
            levels = 7
            n_steps = 2 * levels + 6
            made, taken, chain_sem = sem("rw_made"), sem("rw_taken"), sem("rw_chain")
            hp_rows = lambda hp: slice(hp * HD, (hp + 1) * HD)

            def level(i):
                return c_("levels")[:, i * P:(i + 1) * P].unsqueeze(1).broadcast_to([P, 4, P])

            def products(pe, c, p, s):
                bank = lambda b: ps[:, 4 * p + b]
                four = lambda b: bank(b).rearrange("p (u n) -> p u n", u=4)
                hcols = lambda hp: slice((2 * c + hp) * HD, (2 * c + hp + 1) * HD)
                if s == 0:
                    for n, left in enumerate((bh, kh)):
                        for t in range(NT):
                            for hp in range(2):
                                mm = pe.matmul(bank(2 * n + hp)[:, t * 2 * P:(t + 1) * 2 * P],
                                               left[hp_rows(hp), c, t * P:(t + 1) * P], qr[hp_rows(hp), c, t, :],
                                               start=True, stop=True)
                    return mm
                if s == 1:
                    for u in range(4):
                        mm = pe.transpose(four(0)[:, u], invT[:, p, u], ident)
                    return mm
                if s < 2 * levels:
                    for u in range(4):
                        if s % 2 == 0:
                            mm = pe.matmul(four(1)[:, u], ac[:, p, u, 0:P], inv[:, p, u], start=True, stop=True)
                        else:
                            if s < 2 * levels - 1:
                                pe.matmul(four(2)[:, u], invT[:, p, u], half[:, p, u], start=True, stop=True)
                            mm = pe.matmul(four(3)[:, u], half[:, p, u], invT[:, p, u], start=True, stop=True)
                    return mm
                s -= 2 * levels
                for hp in range(2):
                    t = 0 if s < 3 else 1
                    u = 2 * hp + t
                    vt = v_tok[:, t, hcols(hp)]
                    us = uu[:, p, hp * HD:(hp + 1) * HD]
                    cols2 = slice(hp * HD, (hp + 1) * HD)
                    q_, r_ = qr[hp_rows(hp), c, 1, 0:P], qr[hp_rows(hp), c, 1, P:]
                    st = state[hp_rows(hp), p, :]
                    if s == 0:
                        mm = pe.matmul(bank(0)[:, cols2], bd[:, p, u, 0:P], vt, start=True, stop=True)
                    elif s in (1, 4):
                        mm = pe.matmul(bank(2)[:, cols2], invT[:, p, u], w[:, p, cols2], start=True, stop=True)
                    elif s == 2:
                        pe.matmul(bank(0)[:, cols2], ac[:, p, u, P:], us, start=True, stop=False)
                        pe.matmul(bank(0)[:, cols2], bd[:, p, u, P:], vt, start=False, stop=True)
                        pe.matmul(bank(3)[hp_rows(hp), 0:HD], b_tok[:, hcols(hp)], us, start=True, stop=False)
                        mm = pe.matmul(bank(3)[hp_rows(hp), 0:HD], k_tok[:, hcols(hp)], vt, start=False, stop=True)
                    elif s == 3:
                        pe.matmul(bank(hp)[:, 0:HD], q_, st, start=True, stop=False)
                        mm = pe.matmul(bank(hp)[:, 0:HD], bd[:, p, u, 0:P], vt, start=False, stop=True)
                    else:
                        pe.matmul(bank(hp)[:, 0:HD], r_, st, start=True, stop=False)
                        pe.matmul(bank(hp)[:, 0:HD], ac[:, p, u, P:], us, start=False, stop=False)
                        mm = pe.matmul(bank(hp)[:, 0:HD], bd[:, p, u, P:], vt, start=False, stop=True)
                return mm

            def results(dve, chain, c, p, s):
                bank = lambda b: ps[:, 4 * p + b]
                four = lambda b: bank(b).rearrange("p (u n) -> p u n", u=4)
                if s == 0:
                    mask = c_("strict_incl").unsqueeze(1).broadcast_to([P, NT, 2 * P])
                    for n, dst in enumerate((ac, bd)):
                        for hp in range(2):
                            last = dve.tensor_tensor(dst[:, p, 2 * hp:2 * hp + 2, :],
                                                     bank(2 * n + hp).rearrange("p (t n) -> p t n", t=NT), mask, ALU.mult)
                    chain(last)
                    chain(dve.tensor_tensor(half[:, p], ac[:, p, :, 0:P], level(0), ALU.mult))
                    return dve.tensor_tensor(invT[:, p], ident.unsqueeze(1).broadcast_to([P, 4, P]), half[:, p],
                                             ALU.subtract)
                if s == 1:
                    return dve.tensor_copy(inv[:, p], four(0))
                if s < 2 * levels:
                    if s % 2 == 0:
                        return dve.tensor_tensor(half[:, p], four(1), level(s // 2), ALU.mult)
                    if s < 2 * levels - 1:
                        dve.tensor_tensor(inv[:, p], inv[:, p], four(2), ALU.subtract)
                    return dve.tensor_tensor(invT[:, p], invT[:, p], four(3), ALU.subtract)
                s -= 2 * levels
                t = 0 if s < 3 else 1
                if s == 0:
                    return dve.tensor_scalar(w[:, p, :], bank(0)[:, 0:P], -1.0, None, ALU.mult)
                if s in (1, 4):
                    return dve.tensor_copy(uu[:, p, :], bank(2)[:, 0:P])
                if s == 2:
                    dve.tensor_copy(ya[:, 0, c * P:(c + 1) * P], bank(0)[:, 0:P])
                    return dve.tensor_scalar(state[:, p, :], bank(3)[:, 0:HD], carry[:, 0, c:c + 1], None, ALU.mult)
                for hp in range(2):
                    cols2 = slice(hp * HD, (hp + 1) * HD)
                    if s == 3:
                        last = dve.tensor_scalar(w[:, p, cols2], bank(hp)[:, 0:HD], -1.0, None, ALU.mult)
                    else:
                        last = dve.tensor_copy(ya[:, 1, c * P + hp * HD:c * P + (hp + 1) * HD], bank(hp)[:, 0:HD])
                return last

            order = [(2 * i + p, p, s) for i in range(RC // 2) for s in range(n_steps) for p in range(2)]
            with meeting() as block:
                @block.tensor
                def _(pe):
                    for n, (c, p, s) in enumerate(order):
                        if n >= 2:
                            pe.wait_ge(taken, n - 1)
                        products(pe, c, p, s).then_inc(made, 1)

                @block.vector
                def _(dve):
                    chain = Chain(dve, chain_sem)
                    for n, (c, p, s) in enumerate(order):
                        dve.wait_ge(made, n + 1)
                        if n >= 2:
                            dve.wait_ge(taken, n - 1)
                        results(dve, chain, c, p, s).then_inc(taken, 1)

        def rwkv_out(ya, v_tok, bonus, lora):
            with ExitStack() as on:
                w_g = sb("rw_wg", [P, RW], on=on)
                ln = sb("rw_ln", [P, 2, RW], on=on)
                gate = sb("rw_gate", [P, NT, RW], on=on)
                sq = sb("rw_sq", [P, NT, RW], on=on)
                st = sb("rw_gn", [P, 3, NT, RH], on=on)
                landed = sem("rw_out_landed")
                centred, squared, rooted, work = (sem("gn_" + s) for s in ("centred", "squared", "rooted", "work"))
                yh, sh_, vh = heads(ya), heads(sq), heads(v_tok)
                shape = [P, NT, RH, HD]
                wide = lambda z: z.unsqueeze(3).broadcast_to(shape)
                rows = lambda z: z.unsqueeze(1).broadcast_to([P, NT, RW])
                with meeting() as block:
                    @block.sync
                    def _(sp):
                        sp.dma_start(w_g[:, :], a["rwkv_w_g_2"][0]).then_inc(landed, 16)
                        sp.dma_start(ln[:, 0, :], everywhere(a["rwkv_ln_g_2"], RW)).then_inc(landed, 16)
                        sp.dma_start(ln[:, 1, :], everywhere(a["rwkv_ln_b_2"], RW)).then_inc(landed, 16)

                    @block.tensor
                    def _(pe):
                        pe.wait_ge(landed, 48)
                        for t in range(NT):
                            for h in range(2):
                                mm = pe.matmul(ps[:, 2 * t + h], lora[:, 1, t * P:(t + 1) * P],
                                               w_g[:, h * UC:(h + 1) * UC], start=True, stop=True)
                        mm.then_inc(squared, 1)

                    @block.scalar
                    def _(act):
                        act.wait_ge(centred, 1)
                        act.wait_ge(squared, 1)
                        act.activation(sh_, yh, ACT.Square).then_inc(squared, 1)
                        act.activation(gate[:, :, :], ps[:, 0:4].rearrange("p (t b) n -> p t (b n)", t=NT), ACT.Copy)\
                            .then_inc(squared, 1)
                        act.wait_ge(centred, 2)
                        act.activation(st[:, 2], st[:, 1], ACT.Sqrt).then_inc(rooted, 1)

                    @block.vector
                    def _(dve):
                        chain = Chain(dve, work)
                        chain(dve.tensor_reduce(st[:, 0], yh, AX.X, ALU.add))
                        chain(dve.tensor_scalar(st[:, 0], st[:, 0], 1.0 / HD, None, ALU.mult))
                        dve.tensor_tensor(yh, yh, wide(st[:, 0]), ALU.subtract).then_inc(centred, 1)
                        dve.wait_ge(squared, 2)
                        chain(dve.tensor_reduce(st[:, 1], sh_, AX.X, ALU.add))
                        dve.tensor_scalar(st[:, 1], st[:, 1], 1.0 / HD, GN_EPS, ALU.mult, ALU.add).then_inc(centred, 1)
                        dve.wait_ge(rooted, 1)
                        chain(dve.reciprocal(st[:, 0], st[:, 2]))
                        chain(dve.tensor_tensor(yh, yh, wide(st[:, 0]), ALU.mult))
                        dve.wait_ge(landed, 48)
                        chain(dve.tensor_tensor(ya[:, :, :], ya[:, :, :], rows(ln[:, 0, :]), ALU.mult))
                        chain(dve.tensor_tensor(ya[:, :, :], ya[:, :, :], rows(ln[:, 1, :]), ALU.add))
                        chain(dve.tensor_tensor(sh_, vh, wide(bonus[:, :, :]), ALU.mult))
                        chain(dve.tensor_tensor(yh, yh, sh_, ALU.add))
                        dve.wait_ge(squared, 3)
                        dve.tensor_tensor(ya[:, :, :], ya[:, :, :], gate[:, :, :], ALU.mult)

        def ssd(u_out):
            HG = SH // SG
            GW = SW // SG
            with ExitStack() as on:
                bc = sb("ssd_bc", [P, 2 * SG, S], on=on)
                xs = sb("ssd_x", [P, NT, SW], on=on)
                dts = sb("ssd_dt", [SH, 6, S], on=on)
                dt_tok = sb("ssd_dt_tok", [P, 2, NT, SH], on=on)
                u0, ud = unit["xbc"], unit["dt"]
                with ExitStack() as on2:
                    xT = sb("ssd_xT", [P, SW // P, S], on=on2)
                    nx, nb = SW // P, 2 * SG
                    part = lambda j: xT[:, j, :] if j < nx else bc[:, j - nx, :]

                    def produce(pe, j, bank):
                        if j == nx + nb:
                            stream.arrived(pe, ud)
                            return feature_chunk(pe, ud, 0, SH, bank[0:SH, 0:S])
                        if j % 4 == 0:
                            stream.arrived(pe, u0 + j // 4)
                        return feature_chunk(pe, u0 + j // 4, (j % 4) * P, P, bank[:, 0:S])

                    def consume(eng, j, bank, chain, vector):
                        if j == nx + nb:
                            return eng.tensor_scalar(dts[:, 0, :], bank[0:SH, 0:S], ssd_cols[:, 0:1], None, ALU.add)
                        d = part(j)
                        chain(eng.tensor_scalar(d, bank[:, 0:S], col("ssd_conv_w", 3 * (nx + nb) + j),
                                                col("ssd_conv_b", j), ALU.mult, ALU.add))
                        for tap in (2, 1, 0):
                            back = 3 - tap
                            last = eng.scalar_tensor_tensor(d[:, back:], bank[:, 0:S - back],
                                                            col("ssd_conv_w", tap * (nx + nb) + j), d[:, back:],
                                                            ALU.mult, ALU.add)
                            if tap:
                                chain(last)
                        return last

                    stage("xbc", nx + nb + 1, produce, consume, on_vector=lambda j: True,
                          uses={**{u0 + i: 4 * i + 3 for i in range(6)}, ud: nx + nb})

                    work, acted = sem("dt_work"), sem("dt_acted")
                    z_, e_, u_, d_, l_, out_ = (dts[:, i, :] for i in range(6))
                    with meeting() as block:
                        @block.scalar
                        def _(act):
                            act.activation(e_, z_, ACT.Abs).then_inc(acted, 1)
                            act.wait_ge(acted, 1)
                            act.activation(e_, e_, ACT.Exp, scale=-1.0).then_inc(acted, 1)
                            act.activation(ssd_cols[:, 2:3], ssd_cols[:, 1:2], ACT.Exp).then_inc(acted, 1)
                            act.wait_ge(work, 1)
                            act.activation(l_, u_, ACT.Ln).then_inc(acted, 1)
                            for i in range(0, nx, 4):
                                act.activation(xT[:, i:i + 4, :], xT[:, i:i + 4, :], ACT.Silu)
                            for i in range(0, nb, 4):
                                act.activation(bc[:, i:i + 4, :], bc[:, i:i + 4, :], ACT.Silu)

                        @block.vector
                        def _(dve):
                            chain = Chain(dve, work)
                            dve.wait_ge(acted, 3)
                            chain(dve.tensor_scalar(u_, e_, 1.0, None, ALU.add))
                            chain(dve.tensor_scalar(d_, u_, -1.0, None, ALU.add))
                            chain(dve.tensor_scalar(out_, d_, 0.0, None, ALU.is_equal))
                            chain(dve.tensor_tensor(out_, out_, e_, ALU.mult))
                            chain(dve.tensor_scalar(d_, d_, 1e-30, None, ALU.max))
                            dve.wait_ge(acted, 4)
                            chain(dve.reciprocal(u_, d_))
                            chain(dve.tensor_tensor(e_, e_, u_, ALU.mult))
                            chain(dve.tensor_tensor(e_, e_, l_, ALU.mult))
                            chain(dve.tensor_tensor(e_, e_, out_, ALU.add))
                            chain(dve.tensor_scalar(z_, z_, 0.0, None, ALU.max))
                            chain(dve.tensor_tensor(z_, z_, e_, ALU.add))
                            chain(dve.tensor_scalar(d_, z_, ssd_cols[:, 2:3], -1.0, ALU.mult, ALU.mult))
                            chain(dve.memset(l_, 1.0))
                            dve.tensor_tensor_scan(u_, l_, d_, 0.0, ALU.mult, ALU.add)

                    def turn(pe, j, bank):
                        if j == 8:
                            for i, src in enumerate((z_, u_)):
                                for t in range(NT):
                                    lo = (i * NT + t) * SH
                                    mm = pe.transpose(bank[:, lo:lo + SH], src[:, t * P:(t + 1) * P], ident[0:SH, 0:SH])
                            return mm
                        t, i4 = divmod(j, 4)
                        for i in range(4):
                            mm = pe.transpose(bank[:, i * P:(i + 1) * P], xT[:, i4 * 4 + i, t * P:(t + 1) * P], ident)
                        return mm

                    def take(eng, j, bank, chain, vector):
                        if j == 8:
                            return copy(eng, vector, dt_tok[:, :, :, :],
                                        bank[:, 0:2 * NT * SH].rearrange("p (i t h) -> p i t h", i=2, t=NT))
                        t, i4 = divmod(j, 4)
                        return copy(eng, vector, xs[:, t, i4 * 512:(i4 + 1) * 512], bank)

                    stage("ssd_turn", 9, turn, take, loads=[(acs_row, u_)])

                uz = unit["z"]

                def produce_z(pe, j, bank):
                    n, t = divmod(j, NT)
                    if t == 0:
                        stream.arrived(pe, uz + n)
                    return token_tile(pe, uz + n, 0, UC, t, bank)

                stage("z", 4 * NT, produce_z, lambda eng, j, bank, chain, vector:
                      eng.activation(u_out[:, j % NT, (j // NT) * UC:(j // NT + 1) * UC], bank, ACT.Silu),
                      on_vector=lambda j: False, uses={uz + n: n * NT + 1 for n in range(4)})

                acs = sb("ssd_acs", [P, 2, HG, S], on=on)
                cb = sb("ssd_cb", [P, SG, 3 * P], on=on)
                xdt = sb("ssd_xdt", [P, 2, NT, GW], on=on)
                seg = sb("ssd_seg", [P, 2, 3 * P], on=on)
                dec = sb("ssd_dec", [P, 2, 3 * P], on=on)
                mix = sb("ssd_mix", [P, 2, 3 * P], on=on)
                xd = sb("ssd_xd", [P, 2, GW], on=on)
                cb_made, cb_taken, rows_in, segs, decs, mixes, xdts, given, finished, chain_sem = \
                    (sem("ssd_" + s) for s in ("cb_made", "cb_taken", "rows_in", "segs", "decs", "mixes", "xdts",
                                               "given", "finished", "chain"))
                rows_in2 = sem("ssd_rows_in2")
                incl = c_("strict_incl")[:, P:]
                per_head = lambda z: z.rearrange("p (h d) -> p h d", d=HD)
                wide = lambda z: z.unsqueeze(2).broadcast_to([P, HG, HD])
                with meeting() as block:
                    @block.sync
                    def _(sp):
                        for g in range(SG):
                            if g >= 2:
                                sp.wait_ge(segs, (g - 1) * HG)
                            sp.dma_start(acs[:, g % 2, :, :], bass.AP(acs_row.tensor, g * HG * S, [[0, P], [1, HG * S]])
                                         .rearrange("p (h s) -> p h s", h=HG)).then_inc((rows_in, rows_in2)[g % 2], 16)

                    @block.tensor
                    def _(pe):
                        for g in range(SG):
                            pe.matmul(ps[:, g, 0:S], bc[:, g, 0:P], bc[:, SG + g, :], start=True, stop=True)
                            pe.matmul(ps[:, g, S:3 * P], bc[:, g, P:], bc[:, SG + g, P:], start=True, stop=True)\
                                .then_inc(cb_made, 1)
                        for g in range(SG):
                            if g >= 2:
                                pe.wait_ge(finished, g - 1)
                            pe.wait_ge(xdts, g + 1)
                            for hg in range(HG):
                                h = g * HG + hg
                                pe.wait_ge(mixes, h + 1)
                                o = [ps[:, 4 + 2 * (g % 2) + t, hg * HD:(hg + 1) * HD] for t in range(NT)]
                                xv = [xdt[:, g % 2, t, hg * HD:(hg + 1) * HD] for t in range(NT)]
                                pe.matmul(o[0], mix[:, h % 2, 0:P], xv[0], start=True, stop=True)
                                pe.matmul(o[1], mix[:, h % 2, P:2 * P], xv[0], start=True, stop=False)
                                pe.matmul(o[1], mix[:, h % 2, 2 * P:], xv[1], start=False, stop=True).then_inc(given, 1)

                    @block.scalar
                    def _(act):
                        for h in range(SH):
                            act.wait_ge(segs, h + 1)
                            if h >= 2:
                                act.wait_ge(mixes, h - 1)
                            act.activation(dec[:, h % 2, :], seg[:, h % 2, :], ACT.Exp).then_inc(decs, 1)

                    @block.vector
                    def _(dve):
                        chain = Chain(dve, chain_sem)
                        for g in range(SG):
                            dve.wait_ge(cb_made, g + 1)
                            dve.tensor_tensor(cb[:, g, 0:P], ps[:, g, 0:P], incl, ALU.mult)
                            dve.tensor_copy(cb[:, g, P:2 * P], ps[:, g, P:2 * P])
                            dve.tensor_tensor(cb[:, g, 2 * P:], ps[:, g, 2 * P:3 * P], incl, ALU.mult)\
                                .then_inc(cb_taken, 1)

                        def differences(h):
                            g, hg = divmod(h, HG)
                            if hg == 0:
                                dve.wait_ge((rows_in, rows_in2)[g % 2], 16 * (g // 2 + 1))
                            if h >= 2:
                                dve.wait_ge(decs, h - 1)
                            dve.tensor_scalar(seg[:, h % 2, 0:S], acs[:, g % 2, hg, :], dt_tok[:, 1, 0, h:h + 1], 0.0,
                                              ALU.subtract, ALU.min)
                            dve.tensor_scalar(seg[:, h % 2, S:], acs[:, g % 2, hg, P:], dt_tok[:, 1, 1, h:h + 1], 0.0,
                                              ALU.subtract, ALU.min).then_inc(segs, 1)

                        def weigh(h):
                            dve.wait_ge(decs, h + 1)
                            if h >= 2:
                                dve.wait_ge(given, h - 1)
                            dve.tensor_tensor(mix[:, h % 2, :], dec[:, h % 2, :], cb[:, h // HG, :], ALU.mult)\
                                .then_inc(mixes, 1)

                        def inputs(g):
                            if g >= 2:
                                dve.wait_ge(given, (g - 1) * HG)
                            for t in range(NT):
                                last = dve.tensor_tensor(per_head(xdt[:, g % 2, t, :]),
                                                         per_head(xs[:, t, g * GW:(g + 1) * GW]),
                                                         wide(dt_tok[:, 0, t, g * HG:(g + 1) * HG]), ALU.mult)
                            last.then_inc(xdts, 1)

                        def finish(g):
                            dve.wait_ge(given, (g + 1) * HG)
                            for t in range(NT):
                                cols_g = slice(g * GW, (g + 1) * GW)
                                chain(dve.tensor_tensor(per_head(xd[:, t, :]), per_head(xs[:, t, cols_g]),
                                                        wide(gain("d_skip", g * HG, HG)), ALU.mult))
                                chain(dve.tensor_tensor(xd[:, t, :], xd[:, t, :], ps[:, 4 + 2 * (g % 2) + t], ALU.add))
                                last = dve.tensor_tensor(u_out[:, t, cols_g], u_out[:, t, cols_g], xd[:, t, :], ALU.mult)
                            last.then_inc(finished, 1)

                        dve.wait_ge(cb_taken, SG)
                        differences(0)
                        for h in range(SH):
                            if h % HG == 0:
                                inputs(h // HG)
                            if h + 1 < SH:
                                differences(h + 1)
                            weigh(h)
                            if h % HG == 1 and h >= HG:
                                finish(h // HG - 1)
                        finish(SG - 1)

                sums, scaled, rooted = sem("sn_sums"), sem("sn_scaled"), sem("sn_rooted")
                st = sb("ssd_st", [P, 3, NT, SG], on=on)
                junk = xs
                with meeting() as block:
                    @block.scalar
                    def _(act):
                        for t in range(NT):
                            for g in range(SG):
                                act.activation(junk[:, t, g * GW:(g + 1) * GW], u_out[:, t, g * GW:(g + 1) * GW],
                                               ACT.Square, accum_out=st[:, 0, t, g:g + 1]).then_inc(sums, 1)
                        act.wait_ge(scaled, 1)
                        act.activation(st[:, 2], st[:, 1], ACT.Sqrt).then_inc(rooted, 1)

                    @block.vector
                    def _(dve):
                        dve.wait_ge(sums, NT * SG)
                        dve.tensor_scalar(st[:, 1], st[:, 0], 1.0 / GW, EPS, ALU.mult, ALU.add).then_inc(scaled, 1)
                        dve.wait_ge(rooted, 1)
                        dve.reciprocal(st[:, 0], st[:, 2]).then_inc(scaled, 1)
                        dve.wait_ge(scaled, 2)
                        for t in range(NT):
                            v = u_out[:, t, :].rearrange("p (g n) -> p g n", g=SG)
                            dve.tensor_tensor(v, v, st[:, 0, t, :].unsqueeze(2).broadcast_to([P, SG, GW]), ALU.mult)

        def project(name, u0, src, dst, parts=1):
            def produce(pe, j, bank):
                half, t = divmod(j, NT)
                for r in range(parts):
                    u = u0 + half * parts + r
                    if t == 0:
                        stream.arrived(pe, u)
                    mm = token_tile(pe, u, 0, UC, t, bank, src=src[:, r * KD:(r + 1) * KD, :],
                                    first=r == 0, last=r == parts - 1)
                return mm

            stage(name, 2 * NT, produce, lambda eng, j, bank, chain, vector:
                  copy(eng, vector, dst[:, j % NT, (j // NT) * UC:(j // NT + 1) * UC], bank),
                  uses={u0 + half * parts + r: half * NT + 1 for half in range(2) for r in range(parts)})

        def merge(by_a, by_b):
            with ExitStack() as on:
                gates = sb("merge_gates", [P, NT, 2 * D], on=on)
                bias = sb("merge_bias", [P, 2 * D], on=on)
                landed = sem("gate_bias_landed")
                with meeting() as block:
                    @block.sync
                    def _(sp):
                        sp.dma_start(bias[:, :], everywhere(a["b_gate_2"], 2 * D)).then_inc(landed, 16)
                        sp.wait_ge(landed, 16)
                ug = unit["gate"]

                def produce(pe, j, bank):
                    n, t = divmod(j, NT)
                    if t == 0:
                        stream.arrived(pe, ug + n)
                    return token_tile(pe, ug + n, 0, UC, t, bank)

                stage("gate", 4 * NT, produce, lambda eng, j, bank, chain, vector:
                      eng.tensor_tensor(gates[:, j % NT, (j // NT) * UC:(j // NT + 1) * UC], bank,
                                        bias[:, (j // NT) * UC:(j // NT + 1) * UC], ALU.add),
                      on_vector=lambda j: True, uses={ug + n: n * NT + 1 for n in range(4)})
                opened, work = sem("gates_opened"), sem("merge_work")
                with meeting() as block:
                    @block.scalar
                    def _(act):
                        for i in range(2):
                            act.activation(gates[:, :, i * D:(i + 1) * D], gates[:, :, i * D:(i + 1) * D], ACT.Sigmoid)\
                                .then_inc(opened, 1)

                    @block.vector
                    def _(dve):
                        chain = Chain(dve, work)
                        for i, src in enumerate((by_a, by_b)):
                            dve.wait_ge(opened, i + 1)
                            chain(dve.tensor_tensor(src[:, :, :], src[:, :, :], gates[:, :, i * D:(i + 1) * D], ALU.mult))
                        dve.tensor_tensor(by_a[:, :, :], by_a[:, :, :], by_b[:, :, :], ALU.add)
            with ExitStack() as on:
                mT = sb("mergedT", [P, KD, S], on=on)
                turn_into("merge_turn", by_a, KD, mT)
                add_projection("out2", unit["out2"], mT)

        def router(gate_rows):
            NR = NG + NE
            with ExitStack() as on:
                wr = sb("w_router", [P, KD, NR], on=on)
                lg = sb("router_logits", [P, NT, NR], on=on)
                gsel = sb("r_gsel", [P, NT, NG], on=on)
                t4 = sb("r_t4", [P, NT, NG], on=on)
                el = sb("r_el", [P, NT, EPG, NG], on=on)
                pr = sb("r_pr", [P, NT, EPG], on=on)
                left = sb("r_left", [P, NT, EPG], on=on)
                one = sb("r_one", [P, 2, NT, EPG], on=on)
                t8 = sb("r_t8", [P, NT, EPG], on=on)
                s1 = sb("r_s1", [P, 8, NT], on=on)
                dense = sb("r_dense", [P, NT, NG, EPG], on=on)
                denseT = sb("r_denseT", [NE, S], on=on)
                landed = sem("router_landed")
                with meeting() as block:
                    @block.sync
                    def _(sp):
                        for lo, w in ((0, a["w_router_group_2"][0]), (NG, a["w_router_expert_2"][0])):
                            n = w.shape[1]
                            sp.dma_start(wr[:, :, lo:lo + n], w.rearrange("(k p) c -> p k c", p=P)).then_inc(landed, 16)
                        sp.wait_ge(landed, 32)

                def produce(pe, j, bank):
                    for k in range(KD):
                        mm = pe.matmul(bank[:, 0:NR], hT[:, k, j * P:(j + 1) * P], wr[:, k, :], start=(k == 0),
                                       stop=(k == KD - 1))
                    return mm

                stage("router", NT, produce, lambda eng, j, bank, chain, vector:
                      eng.tensor_tensor(lg[:, j, :], bank[:, 0:NR], gains[:, g_at["b_rg"][0]:g_at["b_rg"][0] + NR],
                                        ALU.add), on_vector=lambda j: True)
                work, asked, acted = sem("r_work"), sem("r_asked"), sem("r_acted")
                gl = lg[:, :, 0:NG]
                shape4, shape8 = [P, NT, NG], [P, NT, EPG]
                over = lambda v, shape: v.unsqueeze(2).broadcast_to(shape)
                with meeting() as block:
                    @block.scalar
                    def _(act):
                        act.wait_ge(asked, 1)
                        act.activation(t4[:, :, :], t4[:, :, :], ACT.Exp).then_inc(acted, 1)
                        act.wait_ge(asked, 2)
                        act.activation(pr[:, :, :], pr[:, :, :], ACT.Exp).then_inc(acted, 1)

                    @block.vector
                    def _(dve):
                        chain = Chain(dve, work)

                        def first_max(dst, src, top, desc, shape, scratch, s_top):
                            chain(dve.tensor_reduce(top, src, AX.X, ALU.max))
                            chain(dve.tensor_tensor(dst, src, over(top, shape), ALU.is_equal))
                            chain(dve.tensor_tensor(dst, dst, desc.unsqueeze(1).broadcast_to(shape), ALU.mult))
                            chain(dve.tensor_reduce(s_top, dst, AX.X, ALU.max))
                            chain(dve.tensor_tensor(dst, dst, over(s_top, shape), ALU.is_equal))

                        first_max(gsel[:, :, :], gl, s1[:, 0, :], c_("desc4"), shape4, None, s1[:, 1, :])
                        dve.tensor_tensor(t4[:, :, :], gl, over(s1[:, 0, :], shape4), ALU.subtract).then_inc(asked, 1)
                        for t in range(NT):
                            chain(dve.tensor_tensor(el[:, t], lg[:, t, NG:].rearrange("p (g e) -> p e g", g=NG),
                                                    gsel[:, t, :].unsqueeze(1).broadcast_to([P, EPG, NG]), ALU.mult))
                        chain(dve.tensor_reduce(left[:, :, :], el[:, :, :, :], AX.X, ALU.add))
                        chain(dve.tensor_reduce(s1[:, 2, :], left[:, :, :], AX.X, ALU.max))
                        dve.tensor_tensor(pr[:, :, :], left[:, :, :], over(s1[:, 2, :], shape8), ALU.subtract)\
                            .then_inc(asked, 1)
                        dve.wait_ge(acted, 1)
                        chain(dve.tensor_reduce(s1[:, 3, :], t4[:, :, :], AX.X, ALU.add))
                        dve.wait_ge(acted, 2)
                        chain(dve.tensor_reduce(s1[:, 4, :], pr[:, :, :], AX.X, ALU.add))
                        chain(dve.reciprocal(s1[:, 5, :], s1[:, 4, :]))
                        chain(dve.tensor_tensor(pr[:, :, :], pr[:, :, :], over(s1[:, 5, :], shape8), ALU.mult))
                        first_max(one[:, 0], pr[:, :, :], s1[:, 0, :], c_("desc8"), shape8, None, s1[:, 1, :])
                        chain(dve.tensor_scalar(t8[:, :, :], one[:, 0], -2.0, None, ALU.mult))
                        chain(dve.tensor_tensor(left[:, :, :], pr[:, :, :], t8[:, :, :], ALU.add))
                        first_max(one[:, 1], left[:, :, :], s1[:, 2, :], c_("desc8"), shape8, None, s1[:, 1, :])
                        chain(dve.tensor_tensor(s1[:, 4, :], s1[:, 0, :], s1[:, 2, :], ALU.add))
                        chain(dve.tensor_tensor(s1[:, 4, :], s1[:, 4, :], s1[:, 3, :], ALU.mult))
                        chain(dve.reciprocal(s1[:, 5, :], s1[:, 4, :]))
                        chain(dve.tensor_tensor(one[:, 0], one[:, 0], one[:, 1], ALU.add))
                        chain(dve.tensor_tensor(one[:, 0], one[:, 0], pr[:, :, :], ALU.mult))
                        chain(dve.tensor_tensor(one[:, 0], one[:, 0], over(s1[:, 5, :], shape8), ALU.mult))
                        for t in range(NT):
                            dve.tensor_tensor(dense[:, t], one[:, 0, t, :].unsqueeze(1).broadcast_to([P, NG, EPG]),
                                              gsel[:, t, :].unsqueeze(2).broadcast_to([P, NG, EPG]), ALU.mult)

                def turn(pe, j, bank):
                    for t in range(NT):
                        mm = pe.transpose(bank[0:NE, t * P:(t + 1) * P], dense[:, t].rearrange("p g e -> p (g e)"), ident)
                    return mm

                stage("gate_turn", 1, turn, lambda eng, j, bank, chain, vector:
                      copy(eng, vector, denseT[:, :], bank[0:NE, 0:S]))
                stored, back = sem("gates_stored"), sem("gates_back")
                with meeting() as block:
                    @block.sync
                    def _(sp):
                        sp.dma_start(gate_row, denseT[:, :]).then_inc(stored, 16)
                        sp.wait_ge(stored, 16)
                        sp.dma_start(gate_rows[:, :, :], bass.AP(gate_row.tensor, 0, [[0, P], [S, NE], [1, S]]))\
                            .then_inc(back, 16)
                        sp.wait_ge(back, 16)

        def experts_stage(gate_rows):
            u0 = unit["moe"]
            body = 4
            trips = NE // body
            per = 3 * body // RING
            views = [a["w_exp_gate_2"][0].rearrange("(i b) (k p) c -> i b p k c", b=body, p=P),
                     a["w_exp_up_2"][0].rearrange("(i b) (k p) c -> i b p k c", b=body, p=P),
                     a["w_exp_down_2"][0].rearrange("(i b) (k p) c -> i b p k c", b=body, p=P)]
            grown, opened, hid_ready, downs, chain_sem = \
                (sem("moe_" + s) for s in ("grown", "opened", "hidden", "downs", "chain"))
            nm = DE // P
            nb = nm // 2
            with ExitStack() as on:
                hid = sb("moe_hid", [P, nm, S], on=on)
                act_ = sb("moe_act", [P, nm, S], on=on)
                both = lambda buf, b: buf[:, 2 * b:2 * b + 2, :].rearrange("p m s -> p (m s)")

                with meeting() as block:
                    @block.tensor
                    def _(pe):
                        for t in range(NT):
                            for h in range(2):
                                pe.matmul(ps[:, 4 + 2 * t + h], ident, x[:, t, h * UC:(h + 1) * UC],
                                          start=True, stop=False)
                        with pe.Fori(0, trips) as i:
                            for b in range(body):
                                for kind in range(2):
                                    u = u0 + 3 * b + kind
                                    w = stream.view(u)
                                    pe.wait_ge(stream.sems[u % RING], i * (16 * per) + stream.need[u])
                                    for m in range(nm):
                                        dst = ps[:, 2 * kind + m // 2, (m % 2) * S:(m % 2 + 1) * S]
                                        for k in range(KD):
                                            mm = pe.matmul(dst, w[:, k, m * P:(m + 1) * P], hT[:, k, :],
                                                           start=(k == 0), stop=(k == KD - 1))
                                        if m % 2:
                                            mm.then_inc(grown, 1)
                                u = u0 + 3 * b + 2
                                w = stream.view(u)
                                pe.wait_ge(stream.sems[u % RING], i * (16 * per) + stream.need[u])
                                for f in range(nm):
                                    if f % 2 == 0:
                                        pe.wait_ge(hid_ready, i * (body * nb) + (b * nb + f // 2 + 1))
                                    for t in range(NT):
                                        for h in range(2):
                                            mm = pe.matmul(ps[:, 4 + 2 * t + h], hid[:, f, t * P:(t + 1) * P],
                                                           w[:, f, h * UC:(h + 1) * UC], start=False, stop=False,
                                                           skip_group_check=True)
                                mm.then_inc(downs, 1)
                        close_sums(pe).then_inc(downs, 1)

                    @block.scalar
                    def _(act):
                        with act.Fori(0, trips) as i:
                            for b in range(body):
                                for m in range(nb):
                                    act.wait_ge(grown, i * (body * 2 * nb) + (b * 2 * nb + m + 1))
                                    act.activation(both(act_, m), ps[:, m], ACT.Silu).then_inc(opened, 1)

                    @block.vector
                    def _(dve):
                        with dve.Fori(0, trips) as i:
                            rows_i = gate_rows[:, bass.ds(i * body, body), :]
                            for b in range(body):
                                for m in range(nb):
                                    dve.wait_ge(opened, i * (body * nb) + (b * nb + m + 1))
                                    dve.tensor_tensor(act_[:, 2 * m:2 * m + 2, :], act_[:, 2 * m:2 * m + 2, :],
                                                      rows_i[:, b, :].unsqueeze(1).broadcast_to([P, 2, S]), ALU.mult)\
                                        .then_inc(chain_sem, 1)
                                    dve.wait_ge(chain_sem, i * (body * nb) + (b * nb + m + 1))
                                    dve.wait_ge(grown, i * (body * 2 * nb) + (b * 2 * nb + nb + m + 1))
                                    dve.tensor_tensor(both(hid, m), both(act_, m), ps[:, 2 + m], ALU.mult)\
                                        .then_inc(hid_ready, 1)
                        dve.wait_ge(downs, body * trips + 1)
                        for t in range(NT):
                            for h in range(2):
                                dve.tensor_copy(x[:, t, h * UC:(h + 1) * UC], ps[:, 4 + 2 * t + h])

                    @block.sync
                    def _(sp):
                        stream.prefetch(sp, u0)

                        def load(n, i):
                            last = n - RING
                            b, kind = divmod(last % (3 * body), 3)
                            j = i if last >= 0 else i - 1
                            if kind == 2:
                                sp.wait_ge(downs, j * body + (b + 1))
                            else:
                                sp.wait_ge(grown, j * (body * 2 * nb) + (b * 2 * nb + (kind + 1) * nb))
                            sp.dma_start(stream.view(u0 + n), views[n % 3][i, n // 3])\
                                .then_inc(stream.sems[n % RING], 16)

                        with sp.Fori(0, trips - 1) as i:
                            for n in range(RING, 3 * body):
                                load(n, i)
                            for n in range(RING):
                                load(n, i + 1)
                        for n in range(RING, 3 * body):
                            load(n, trips - 1)

        def final_norm():
            with ExitStack() as on:
                row = sb("final_gain", [P, D], on=on)
                sq = sb("final_sq", [P, D], on=on)
                st = sb("final_st", [P, 4, NT], on=on)
                y = sb("final_y", [P, NT, D], on=on)
                landed, sums, scaled, rooted, done = (sem("final_" + s) for s in ("landed", "sums", "scaled", "rooted", "done"))
                stored = sem("stored")
                with meeting() as block:
                    @block.sync
                    def _(sp):
                        sp.dma_start(row[:, :], everywhere(a["final_norm_g_2"], D)).then_inc(landed, 16)
                        for t in range(NT):
                            sp.wait_ge(done, t + 1)
                            sp.dma_start(out[0, t * P:(t + 1) * P, :], y[:, t, :]).then_inc(stored, 16)
                        sp.wait_ge(stored, 16 * NT)

                    @block.scalar
                    def _(act):
                        for t in range(NT):
                            if t:
                                act.wait_ge(sums, t)
                            act.activation(sq[:, :], x[:, t, :], ACT.Square, accum_out=st[:, 0, t:t + 1])\
                                .then_inc(sums, 1)
                        act.wait_ge(scaled, 1)
                        act.activation(st[:, 2, :], st[:, 1, :], ACT.Sqrt).then_inc(rooted, 1)

                    @block.vector
                    def _(dve):
                        dve.wait_ge(sums, NT)
                        dve.tensor_scalar(st[:, 1, :], st[:, 0, :], 1.0 / D, EPS, ALU.mult, ALU.add).then_inc(scaled, 1)
                        dve.wait_ge(rooted, 1)
                        dve.reciprocal(st[:, 3, :], st[:, 2, :]).then_inc(scaled, 1)
                        dve.wait_ge(scaled, 2)
                        dve.wait_ge(landed, 16)
                        for t in range(NT):
                            dve.scalar_tensor_tensor(y[:, t, :], x[:, t, :], st[:, 3, t:t + 1], row[:, :],
                                                     ALU.mult, ALU.mult).then_inc(done, 1)

        with ExitStack() as on:
            mem = sb("mem", [P, NT, D], on=on)
            with ExitStack() as on2:
                rows = sb("rows", [P, 3, P], on=on2)
                table = sb("table", [NBK + 1, NH], on=on2)
                hb = sb("dist_rows", [NH, 512], on=on2)
                setup(mem, rows, table, hb)
            norm("mem", mem, [("mem_norm", 0, hT)])
            memory(hT)
        norm("n0", x, [("mix_norm", 0, hT)])
        conv_layer()
        norm("n1", x, [("mlp_norm", 0, hT)])
        mlp(0)
        with ExitStack() as on:
            sh = shared_buffers(on)
            with ExitStack() as on2:
                hkv = sb("hkv", [P, KD, S], on=on2)
                norm("n2", x, [("kv_norm", 0, hkv), ("mix_norm", KD, hT)])
                shared_kv(sh, hkv)
            nsa_layer(sh)
        norm("n3", x, [("mlp_norm", KD, hT)])
        mlp(1)
        first.close()
        with ExitStack() as on:
            by_a = sb("by_a", [P, NT, D], on=on)
            norm("n4", x, [("attn_norm", 0, hT)])
            with ExitStack() as on2:
                rwkv(by_a)
                dump("ya", by_a)
                yaT = sb("yaT", [P, RC, S], on=on2)
                turn_into("ya_turn", by_a, RC, yaT)
                project("up_rwkv", unit["up_rwkv"], yaT, by_a)
            by_b = sb("by_b", [P, NT, D], on=on)
            with ExitStack() as on2:
                yb = sb("yb", [P, NT, SW], on=on2)
                ssd(yb)
                dump("yb", yb)
                ybT = sb("ybT", [P, SW // P, S], on=on2)
                turn_into("yb_turn", yb, SW // P, ybT, scale=lambda j: col("ssd_norm", j))
                project("up_ssd", unit["up_ssd"], ybT, by_b, parts=2)
            merge(by_a, by_b)
            dump("x", x)
        norm("n5", x, [("ffn_norm", 0, hT)])
        with ExitStack() as on:
            gate_rows = sb("gate_rows", [P, NE, S], on=on)
            router(gate_rows)
            experts_stage(gate_rows)
        final_norm()


NAMES = ("x mem mix_norm a_w_in a_conv_w b_w_in b_q_gain kv_norm w_kv_shared k_gain cmp_pos cmp_w1 cmp_w2 rel_bias "
         "mem_norm mem_w_kv mem_q_gain mem_k_gain w_out mlp_norm w_up w_down attn_norm_g_2 w_in_2 b_gate_2 rwkv_mu_2 "
         "rwkv_w0_2 rwkv_w_decay_2 rwkv_a0_2 rwkv_w_a_2 rwkv_w_g_2 rwkv_k_k_2 rwkv_k_a_2 rwkv_r_k_2 rwkv_ln_g_2 "
         "rwkv_ln_b_2 w_up_rwkv_2 ssd_conv_w_2 ssd_conv_b_2 ssd_dt_bias_2 ssd_a_log_2 ssd_d_2 ssd_norm_g_2 w_up_ssd_2 "
         "w_out_2 ffn_norm_g_2 w_router_group_2 b_router_group_2 w_router_expert_2 b_router_expert_2 w_exp_gate_2 "
         "w_exp_up_2 w_exp_down_2 final_norm_g_2").split()


def kernel(**inputs):
    import concourse.bacc as bacc
    from concourse.bass_utils import run_bass_kernel_spmd

    nc = bacc.Bacc("TRN2", target_bir_lowering=False, num_devices=1)
    const, at = constants()
    arrays = {f"in_{n}": np.ascontiguousarray(inputs[n]) for n in NAMES}
    arrays["in_const"] = const
    views = {k[3:]: nc.dram_tensor(k, v.shape, mybir.dt.from_np(v.dtype), kind="ExternalInput").ap()
             for k, v in arrays.items()}
    out = nc.dram_tensor("out_x", (1, S, D), F32, kind="ExternalOutput").ap()
    program(nc, views, out, at)
    r = run_bass_kernel_spmd(nc, [arrays], core_ids=[0])
    return r.results[0]["out_x"]
```

```python
from contextlib import ExitStack, contextmanager

import numpy as np

import concourse.bass as bass
from concourse import mybir

F32 = mybir.dt.float32
F32R = mybir.dt.float32r
I32 = mybir.dt.int32
ALU = mybir.AluOpType
ACT = mybir.ActivationFunctionType
AX = mybir.AxisListType

P = 128
S = 256
NT = S // P
D = 1024
KD = D // P
HD = 64
NEG = -1e30
EPS = 1e-6

CONV_CH = 768
NH = CONV_CH // HD
G = 2
HPG = NH // G
MW = 256
MH = MW // HD
M = 256
FF = 4096
NBK = 32
CMP_L, CMP_S = 32, 16
NC = S // CMP_S - 1
CMP_H = 256

RW = 1024
RH = RW // HD
RC = RW // P
LORA = 64
R_COLS = 3 * RW + 2 * LORA + P
SW = 2048
SH = SW // HD
SG = 4
SN = 128
XBC = SW + 2 * SG * SN
KAPPA = float(np.exp(-0.5))
GN_EPS = 64e-5

NE, NG, EPG, DE = 32, 4, 8, 512
RING = 4
SLOTS = 128
FAR = 1024.0
UC = 512


def bucket_of(dist):
    n = np.maximum(dist, 0)
    nf = np.maximum(n, 1).astype(np.float32)
    large = 16 + (np.log(nf / np.float32(16)) / np.float32(np.log(64.0)) * np.float32(16)).astype(np.int32)
    return np.where(n < 16, n, np.minimum(large, 31))


def constants():
    i = np.arange(P)
    parts = {}
    parts["ident"] = np.eye(P)
    parts["flip"] = np.eye(P)[::-1]
    parts["headones"] = (i[:, None] // HD == i[None, :] // HD)
    parts["strict_incl"] = np.concatenate([i[:, None] < i[None, :], i[:, None] <= i[None, :]], 1)
    level = []
    for b in (1, 2, 4, 8, 16, 32, 64):
        blk = i // b
        lower = (blk[:, None] // 2 == blk[None, :] // 2) & (blk[:, None] % 2 == 1) & (blk[None, :] % 2 == 0)
        level.append(lower.T if b == 1 else lower)
    parts["levels"] = np.concatenate(level, 1)
    y = 255 - np.arange(512)
    hot = np.zeros((P, 512))
    hot[np.where(y >= 0, bucket_of(y), NBK), np.arange(512)] = 1
    parts["hot"] = hot
    parts["headsel"] = np.arange(2)[None, :] == (i // HD)[:, None]
    parts["cmp_rows"] = (i[:, None] + P * np.arange(NT)[None, :]) >= CMP_L - 1
    parts["desc4"] = np.broadcast_to(4.0 - np.arange(4), (P, 4))
    parts["desc8"] = np.broadcast_to(8.0 - np.arange(8), (P, 8))
    parts["ones"] = np.ones((P, P))
    parts["slot_row"] = np.broadcast_to(np.where(i < SLOTS, i, -1), (P, P))
    parts["slot_col"] = np.where(i < SLOTS, i, -1)[:, None]
    parts["noughts"] = np.zeros((P, UC))
    at, n = {}, 0
    for k, v in parts.items():
        at[k] = (n, n + v.shape[1])
        n += v.shape[1]
    return np.concatenate([np.asarray(v, np.float32) for v in parts.values()], 1), at


class Chain:

    def __init__(self, eng, sem):
        self.eng, self.sem, self.n = eng, sem, 0

    def __call__(self, ins):
        self.n += 1
        ins.then_inc(self.sem, 1)
        self.eng.wait_ge(self.sem, self.n)


def three(pe, dst, left, right, start, stop):
    inside = not (start or stop)
    pe.matmul(dst, left[0], right[0], start=start, stop=False, skip_group_check=inside)
    pe.matmul(dst, left[0], right[1], start=False, stop=False, skip_group_check=inside)
    return pe.matmul(dst, left[1], right[0], start=False, stop=stop, skip_group_check=inside)


class Stream:

    def __init__(self, slots, sems):
        self.slots, self.sems = slots, sems
        self.src = []
        self.need = {}
        self.done = {}
        self.issued = 0

    def count(self):
        loads = [0] * RING
        for n, src in enumerate(self.src):
            if src is not None:
                loads[n % RING] += 1
                self.need[n] = 16 * loads[n % RING]

    def view(self, n):
        _, kc, cols = self.src[n]
        return self.slots[:, n % RING, 0:kc * cols].rearrange("p (k c) -> p k c", k=kc)

    def arrived(self, pe, n):
        pe.wait_ge(self.sems[n % RING], self.need[n])
        return self.view(n)

    def load(self, sp, n):
        src, kc, cols = self.src[n]
        before = [u for u in range(n - RING, -1, -RING) if self.src[u] is not None][:1]
        if before and before[0] in self.done:
            sp.wait_ge(*self.done[before[0]])
        sp.dma_start(self.view(n), src).then_inc(self.sems[n % RING], 16)

    def prefetch(self, sp, end):
        while self.issued < min(end + RING, len(self.src)):
            if self.src[self.issued] is not None:
                self.load(sp, self.issued)
            self.issued += 1


def program(nc, a, out, at, dumps=()):
    with ExitStack() as ctx:
        seen = {}

        def sb(name, shape, dt=F32, on=None):
            seen[name] = seen.get(name, 0) + 1
            name = name if seen[name] == 1 else f"{name}_{seen[name]}"
            return (on or ctx).enter_context(nc.sbuf_tensor(name, shape, dt))

        used, cooling = [], []

        def sem(name):
            used.append(nc.alloc_semaphore(name=f"{name}_{len(seen)}_{len(used)}"))
            return used[-1]

        def end_stage():
            for s in cooling:
                nc.release_semaphore(s)
            cooling[:] = used
            for s in used:
                nc.gpsimd.sem_clear(s)
            used.clear()
            stream.done.clear()

        @contextmanager
        def meeting():
            with nc.Block() as block:
                yield block
            end_stage()

        ps = ctx.enter_context(nc.psum_tensor("ps", [P, 8, 512], F32))
        slots = sb("weight_slots", [P, RING, KD * UC])
        n_const = max(e for _, e in at.values())
        const = sb("const", [P, n_const])
        x = sb("x", [P, NT, D])
        hT = sb("hT", [P, KD, S])

        def c_(name):
            lo, hi = at[name]
            return const[:, lo:hi]

        ident = c_("ident")

        def dump(name, t):
            if name in dumps:
                dd = nc.dram_tensor("dump_" + name, list(t.shape), F32, kind="ExternalOutput").ap()
                ds = sem("dump")
                with meeting() as block:
                    @block.sync
                    def _(sp):
                        sp.dma_start(dd, t[tuple(slice(None) for _ in t.shape)]).then_inc(ds, 16)
                        sp.wait_ge(ds, 16)

        stream = Stream(slots, [ctx.enter_context(nc.semaphore(f"weights_landed_{s}")) for s in range(RING)])
        unit = {}

        def kxn(w, r0, rows, c0, cols):
            return (w[r0:r0 + rows, c0:c0 + cols].rearrange("(k p) c -> p k c", p=P), rows // P, cols)

        def plan(name, *views):
            unit[name] = len(stream.src)
            stream.src.extend(views)

        def gap():
            while len(stream.src) % RING:
                stream.src.append(None)

        def columns(w, c0, c1, rows=D):
            return [kxn(w, 0, rows, c, min(UC, c1 - c)) for c in range(c0, c1, UC)]

        def mlp_units(layer):
            v = []
            for j in range(FF // UC):
                v.append(kxn(a["w_up"][layer], 0, D, j * UC, UC))
                v.append(kxn(a["w_down"][layer], j * UC, UC, 0, D))
            return v

        a_w, b_w, w2 = a["a_w_in"][0], a["b_w_in"][0], a["w_in_2"][0]
        Z0 = R_COLS
        X0 = Z0 + SW
        T0 = X0 + XBC
        G0 = T0 + SH
        QG = CONV_CH + 3 * NH
        plan("mem_kv", *[kxn(a["mem_w_kv"][l], 0, D, 0, 2 * MW) for l in range(2)])
        plan("a_in", *columns(a_w, 0, 3 * CONV_CH + MW))
        plan("out0", *columns(a["w_out"][0], 0, D))
        gap()
        plan("mlp0", *mlp_units(0))
        plan("kv", *columns(a["w_kv_shared"], 0, 6 * G * HD))
        plan("cmp1", *[kxn(a["cmp_w1"][i], 0, CMP_L * HD, 0, CMP_H) for i in range(2)])
        plan("b_in", kxn(b_w, 0, D, 0, UC), kxn(b_w, 0, D, UC, QG - UC), kxn(b_w, 0, D, QG, MW))
        plan("out1", *columns(a["w_out"][1], 0, D))
        gap()
        plan("mlp1", *mlp_units(1))
        plan("rwkv", *columns(w2, 0, R_COLS))
        plan("up_rwkv", *columns(a["w_up_rwkv_2"][0], 0, D))
        plan("xbc", *columns(w2, X0, T0))
        plan("dt", kxn(w2, 0, D, T0, SH))
        plan("z", *columns(w2, Z0, X0))
        plan("up_ssd", *[kxn(a["w_up_ssd_2"][0], r * D, D, n * UC, UC) for n in range(2) for r in range(2)])
        plan("gate", *columns(w2, G0, G0 + 2 * D))
        plan("out2", *columns(a["w_out_2"][0], 0, D))
        gap()
        experts = []
        for e in range(NE):
            experts += [kxn(a["w_exp_gate_2"][0, e], 0, D, 0, DE), kxn(a["w_exp_up_2"][0, e], 0, D, 0, DE),
                        kxn(a["w_exp_down_2"][0, e], 0, DE, 0, D)]
        plan("moe", *experts)
        stream.count()

        def stage(name, n_jobs, produce, consume, on_vector=lambda j: j % 2 == 0, uses=(), loads=()):
            full, free_v, free_a = sem(name + "_full"), sem(name + "_free_v"), sem(name + "_free_a")
            chain_v, chain_a = sem(name + "_chain_v"), sem(name + "_chain_a")
            loaded = sem(name + "_loaded")
            n_banks = 8
            bank = lambda j: ps[:, j % n_banks]
            nth = [sum(on_vector(i) == on_vector(j) for i in range(j + 1)) for j in range(n_jobs)]
            with meeting() as block:
                @block.tensor
                def _(pe):
                    for j in range(n_jobs):
                        if j >= n_banks:
                            b = j - n_banks
                            pe.wait_ge(free_v if on_vector(b) else free_a, nth[b])
                        produce(pe, j, bank(j)).then_inc(full, 1)
                    for u, j in dict(uses).items():
                        stream.done[u] = (full, j + 1)

                @block.vector
                def _(dve):
                    chain = Chain(dve, chain_v)
                    for j in range(n_jobs):
                        if on_vector(j):
                            dve.wait_ge(full, j + 1)
                            consume(dve, j, bank(j), chain, True).then_inc(free_v, 1)

                @block.scalar
                def _(act):
                    chain = Chain(act, chain_a)
                    for j in range(n_jobs):
                        if not on_vector(j):
                            act.wait_ge(full, j + 1)
                            consume(act, j, bank(j), chain, False).then_inc(free_a, 1)

                @block.sync
                def _(sp):
                    for dst, src in loads:
                        sp.dma_start(dst, src).then_inc(loaded, 16)
                    if loads:
                        sp.wait_ge(loaded, 16 * len(loads))
                    if uses:
                        stream.prefetch(sp, max(dict(uses)) + 1)

        def copy(eng, vector, dst, src):
            return eng.tensor_copy(dst, src) if vector else eng.activation(dst, src, ACT.Copy)

        def feature_chunk(pe, u, c0, width, dst, src=None):
            w, h = stream.view(u), hT if src is None else src
            for k in range(KD):
                mm = pe.matmul(dst, w[:, k, c0:c0 + width], h[:, k, :], start=(k == 0), stop=(k == KD - 1))
            return mm

        def token_tile(pe, u, c0, width, t, dst, src=None, first=True, last=True):
            w, h = stream.view(u), hT if src is None else src
            kc = stream.src[u][1]
            for k in range(kc):
                mm = pe.matmul(dst, h[:, k, t * P:(t + 1) * P], w[:, k, c0:c0 + width],
                               start=(first and k == 0), stop=(last and k == kc - 1))
            return mm

        rows_of = [
            [("mem_norm", a["mem_norm"]), ("mix_norm", a["mix_norm"]), ("kv_norm", a["kv_norm"]),
             ("mlp_norm", a["mlp_norm"]), ("attn_norm", a["attn_norm_g_2"]), ("ffn_norm", a["ffn_norm_g_2"]),
             ("conv_w", a["a_conv_w"])],
            [("mu", a["rwkv_mu_2"]), ("w0", a["rwkv_w0_2"]), ("a0", a["rwkv_a0_2"]), ("k_k", a["rwkv_k_k_2"]),
             ("k_a", a["rwkv_k_a_2"]), ("r_k", a["rwkv_r_k_2"]), ("ssd_conv_b", a["ssd_conv_b_2"]),
             ("ssd_norm", a["ssd_norm_g_2"])],
            [("ssd_conv_w", a["ssd_conv_w_2"]), ("cmp_pos", a["cmp_pos"])],
        ]
        cols = sb("cols", [P, 3, P])
        col_at = {}
        n_loads = 0
        row_list = []
        for tile, group in enumerate(rows_of):
            r = 0
            for name, v in group:
                size = int(np.prod(v.shape))
                n = size // P
                col_at[name] = (tile, r)
                row_list.append((tile, r, n, bass.AP(v.tensor, v.offset, [[P, n], [1, P]])))
                r += n
            assert r <= P
        row_counts = [sum(n for t, _, n, _ in row_list if t == tile) for tile in range(3)]

        def col(name, i, n=1):
            tile, r = col_at[name]
            return cols[:, tile, r + i:r + i + n]

        gain_rows = [("q_gain", a["b_q_gain"], 64), ("k_gain", a["k_gain"], 192), ("mem_q_gain", a["mem_q_gain"], 128),
                     ("mem_k_gain", a["mem_k_gain"], 128), ("d_skip", a["ssd_d_2"], 32),
                     ("b_rg", a["b_router_group_2"], NG), ("b_re", a["b_router_expert_2"], NE)]
        ssd_cols = sb("ssd_cols", [SH, 4])
        gains = sb("gains", [P, sum(n for _, _, n in gain_rows)])
        g_at, r = {}, 0
        for name, _, n in gain_rows:
            g_at[name] = (r, n)
            r += n

        def everywhere(v, n, off=0):
            return bass.AP(v.tensor, v.offset + off, [[0, P], [1, n]])

        def gain(name, i=0, n=HD):
            lo = g_at[name][0] + i
            return gains[:, lo:lo + n]

        first = ctx.enter_context(ExitStack())
        dist = sb("dist_bias", [P, NH, 3 * P], on=first)
        acs_row = nc.dram_tensor("acs_row", [SH, S], F32, kind="Internal").ap()
        gate_row = nc.dram_tensor("gate_row", [NE, 3, S], F32, kind="Internal").ap()
        dist_row = nc.dram_tensor("dist_row", [NH, 512], F32, kind="Internal").ap()
        cmp2 = sb("cmp_w2", [P, 2, 2, HD], on=first)
        mem_kT = sb("mem_kT", [P, 2, MW // P, M], on=first)
        mem_v = sb("mem_v", [P, 2, M // P, MW], on=first)

        def setup(mem, rows, table, hb):
            landed, bias_out, bias_in = sem("setup_landed"), sem("bias_row_out"), sem("bias_rows_in")
            turned, taken, cleared = sem("setup_turned"), sem("setup_taken"), sem("setup_cleared")
            n = 0
            with meeting() as block:
                @block.gpsimd
                def _(pool):
                    pool.memset(rows[:, :, :], 0.0).then_inc(cleared, 1)

                @block.sync
                def _(sp):
                    nonlocal n
                    for dst, src in [(x[:, :, :], a["x"][0].rearrange("(t p) d -> p t d", p=P)),
                                     (mem[:, :, :], a["mem"][0].rearrange("(t p) d -> p t d", p=P)),
                                     (const[:, :], a["const"])]:
                        sp.dma_start(dst, src).then_inc(landed, 16)
                        n += 1
                    stream.prefetch(sp, 0)
                    sp.wait_ge(cleared, 1)
                    for tile, r, k, src in row_list:
                        sp.dma_start(rows[r:r + k, tile, :], src).then_inc(landed, 16)
                        n += 1
                    sp.wait_ge(taken, 1)
                    sp.dma_start(dist_row, hb[0:NH, :]).then_inc(bias_out, 16)
                    sp.wait_ge(bias_out, 16)
                    sp.dma_start(dist[:, :, :], bass.AP(dist_row.tensor, 0, [[1, P], [512, NH], [1, 3 * P]]))\
                        .then_inc(bias_in, 16)
                    sp.wait_ge(bias_in, 16)

                @block.scalar
                def _(act):
                    nonlocal n
                    for name, v, k in gain_rows:
                        lo = g_at[name][0]
                        act.dma_start(gains[:, lo:lo + k], everywhere(v, k)).then_inc(landed, 16)
                        n += 1
                    for i, v in enumerate((a["ssd_dt_bias_2"], a["ssd_a_log_2"])):
                        act.dma_start(ssd_cols[:, i:i + 1], bass.AP(v.tensor, v.offset, [[1, SH], [1, 1]]))\
                            .then_inc(landed, 16)
                        n += 1
                    act.dma_start(cmp2[:, :, :, :], a["cmp_w2"].rearrange("i (k p) d -> p i k d", p=P))\
                        .then_inc(landed, 16)
                    act.wait_ge(cleared, 2)
                    act.dma_start(table[0:NBK, :], a["rel_bias"]).then_inc(landed, 16)
                    n += 2

                @block.tensor
                def _(pe):
                    pe.wait_ge(cleared, 2)
                    pe.wait_ge(landed, 16 * n)
                    pe.matmul(ps[0:NH, 3, :], table[0:NBK + 1, :], c_("hot")[0:NBK + 1, :],
                              start=True, stop=True).then_inc(turned, 1)
                    for i in range(3):
                        pe.transpose(ps[:, i, 0:P], rows[:, i, :], ident).then_inc(turned, 1)

                @block.vector
                def _(dve):
                    dve.wait_ge(cleared, 1)
                    dve.memset(table[:, :], NEG).then_inc(cleared, 1)
                    dve.wait_ge(turned, 1)
                    dve.tensor_copy(hb[0:NH, :], ps[0:NH, 3, :]).then_inc(taken, 1)
                    dve.wait_ge(turned, 4)
                    for i in range(3):
                        dve.tensor_copy(cols[:, i, :], ps[:, i, 0:P]).then_inc(taken, 1)

        def norm(name, src, outs, scaled=None):
            with ExitStack() as on:
                if scaled is None:
                    scaled = sb(name + "_scaled", [P, NT, D], on=on)
                stat = sb(name + "_stat", [P, 4, NT], on=on)
                squares, roots, scale = sem(name + "_squares"), sem(name + "_roots"), sem(name + "_scale")
                turned, free_v, free_a = sem(name + "_turned"), sem(name + "_free_v"), sem(name + "_free_a")
                with meeting() as block:
                    @block.scalar
                    def _(act):
                        for t in range(NT):
                            act.activation(scaled[:, t, :], src[:, t, :], ACT.Square,
                                           accum_out=stat[:, 0, t:t + 1]).then_inc(squares, 1)
                        act.wait_ge(scale, 1)
                        act.activation(stat[:, 2, :], stat[:, 1, :], ACT.Sqrt).then_inc(roots, 1)
                        for c in range(1, KD, 2):
                            act.wait_ge(turned, c + 1)
                            for gname, g0, dst in outs:
                                last = act.activation(dst[:, c, :], ps[:, c % 8, 0:S], ACT.Copy,
                                                      scale=col(gname, g0 + c))

                    @block.vector
                    def _(dve):
                        dve.wait_ge(squares, NT)
                        dve.tensor_scalar(stat[:, 1, :], stat[:, 0, :], 1.0 / D, EPS, ALU.mult, ALU.add)\
                            .then_inc(scale, 1)
                        dve.wait_ge(roots, 1)
                        dve.reciprocal(stat[:, 3, :], stat[:, 2, :]).then_inc(scale, 1)
                        dve.wait_ge(scale, 2)
                        for t in range(NT):
                            dve.tensor_scalar(scaled[:, t, :], src[:, t, :], stat[:, 3, t:t + 1], None, ALU.mult)\
                                .then_inc(scale, 1)
                        for c in range(0, KD, 2):
                            dve.wait_ge(turned, c + 1)
                            for gname, g0, dst in outs:
                                dve.tensor_scalar(dst[:, c, :], ps[:, c % 8, 0:S], col(gname, g0 + c), None, ALU.mult)

                    @block.tensor
                    def _(pe):
                        pe.wait_ge(scale, 2 + NT)
                        for c in range(KD):
                            for t in range(NT):
                                mm = pe.transpose(ps[:, c % 8, t * P:(t + 1) * P],
                                                  scaled[:, t, c * P:(c + 1) * P], ident)
                            mm.then_inc(turned, 1)

        def head_norm(name, items, copies=()):
            sums, means, roots, scale = (sem(f"{name}_{s}") for s in ("squares", "means", "roots", "scale"))
            with meeting() as block:
                @block.scalar
                def _(act):
                    for dst, src, sq, st, g, k in items:
                        act.activation(sq, src, ACT.Square).then_inc(sums, 1)
                    for n, (dst, src, sq, st, g, k) in enumerate(items):
                        act.wait_ge(means, 2 * n + 2)
                        act.activation(st[:, 1], st[:, 0], ACT.Sqrt).then_inc(roots, 1)

                @block.vector
                def _(dve):
                    for n, (dst, src, sq, st, g, k) in enumerate(items):
                        dve.wait_ge(sums, n + 1)
                        dve.tensor_reduce(st[:, 0], sq, AX.X, ALU.add).then_inc(means, 1)
                        dve.wait_ge(means, 2 * n + 1)
                        dve.tensor_scalar(st[:, 0], st[:, 0], 1.0 / HD / (k * k), EPS / (k * k), ALU.mult, ALU.add)\
                            .then_inc(means, 1)
                    for dst, src in copies:
                        dve.tensor_copy(dst, src)
                    at = 0
                    for n, (dst, src, sq, st, g, k) in enumerate(items):
                        shape = list(src.shape)
                        dve.wait_ge(roots, n + 1)
                        dve.reciprocal(st[:, 0], st[:, 1]).then_inc(scale, 1)
                        dve.wait_ge(scale, at + 1)
                        dve.tensor_tensor(sq, src, st[:, 0].unsqueeze(3).broadcast_to(shape), ALU.mult)\
                            .then_inc(scale, 1)
                        dve.wait_ge(scale, at + 2)
                        for d in dst:
                            dve.tensor_tensor(d, sq, g.unsqueeze(1).unsqueeze(1).broadcast_to(shape), ALU.mult)
                        at += 2

        def heads(v):
            return v.rearrange("p t (h d) -> p t h d", d=HD)

        def memory(memT):
            with ExitStack() as on:
                kv = sb("mem_kv", [P, 2, NT, 2 * MW], on=on)
                kn = sb("mem_kn", [P, 2, NT, MW], on=on)
                sq = sb("mem_sq", [P, 2, NT, MW], on=on)
                st = sb("mem_st", [P, 2, 2, NT, MH], on=on)

                def produce(pe, j, bank):
                    layer, t = divmod(j, NT)
                    u = unit["mem_kv"] + layer
                    if t == 0:
                        stream.arrived(pe, u)
                    return token_tile(pe, u, 0, 2 * MW, t, bank, src=memT)

                def consume(eng, j, bank, chain, vector):
                    return copy(eng, vector, kv[:, j // NT, j % NT, :], bank)

                stage("mem_kv", 2 * NT, produce, consume,
                      uses={unit["mem_kv"] + l: l * NT + 1 for l in range(2)})
                head_norm("mem_k", [([heads(kn[:, l])], heads(kv[:, l, :, 0:MW]), heads(sq[:, l]), st[:, l],
                                     gain("mem_k_gain", l * HD), 1.0) for l in range(2)],
                          copies=[(mem_v[:, l], kv[:, l, :, MW:]) for l in range(2)])

                def turn(pe, j, bank):
                    layer, pair = divmod(j, MW // P)
                    for t in range(NT):
                        mm = pe.transpose(bank[:, t * P:(t + 1) * P], kn[:, layer, t, pair * P:(pair + 1) * P], ident)
                    return mm

                stage("mem_turn", 2 * MW // P, turn,
                      lambda eng, j, bank, chain, vector: copy(eng, vector, mem_kT[:, j // 2, j % 2, :], bank[:, 0:M]))

        def attention(name, groups, sums):
            items = []
            for g, grp in enumerate(groups):
                for h0 in range(0, len(grp["heads"]), grp["per"]):
                    hs = grp["heads"][h0:h0 + grp["per"]]
                    items.append((g, h0, hs, h0 + grp["per"] >= len(grp["heads"])))
            n = len(items)
            logits, top, probs, turned, turned_taken, given, combined = \
                (sem(f"{name}_{s}") for s in ("logits", "top", "probs", "turned", "turned_taken", "given", "combined"))
            chain_sem = sem(name + "_chain")
            exps = [0]
            for g, h0, hs, last in items:
                exps.append(exps[-1] + len(hs))
            with ExitStack() as on:
                nmax = sb(name + "_nmax", [P, 2, 4], on=on)
                probs_sb = sb(name + "_probs", [P, 2, 512], on=on)
                pT = sb(name + "_pT", [P, 2, 4 * P], on=on)
                coef = sb(name + "_coef", [P, 2, 12], on=on)
                part = sb(name + "_part", [P, CONV_CH], on=on)

                def bank_l(i):
                    return ps[:, i % 2]

                def bank_t(i):
                    return ps[:, 2 + i % 2]

                def bank_o(g):
                    return ps[:, 4 + 2 * (g % 2):6 + 2 * (g % 2)].rearrange("p b n -> p (b n)")

                with meeting() as block:
                    @block.tensor
                    def _(pe):
                        def scores(i):
                            g, h0, hs, last = items[i]
                            grp = groups[g]
                            nk = sum(grp["keys"])
                            if i >= 2:
                                pe.wait_ge(probs, exps[i - 1])
                            for n_h, h in enumerate(hs):
                                dst = bank_l(i)[:, n_h * nk:(n_h + 1) * nk]
                                bias = grp["bias"](h) if grp["bias"] else None
                                mm = pe.matmul(dst, grp["q"](h), grp["k"](h), start=True, stop=bias is None)
                                if bias is not None:
                                    mm = pe.matmul(dst, c_("flip"), bias, start=False, stop=True)
                            mm.then_inc(logits, 1)

                        def turn(i):
                            g, h0, hs, last = items[i]
                            grp = groups[g]
                            nk = sum(grp["keys"])
                            pe.wait_ge(probs, exps[i + 1])
                            if i >= 2:
                                pe.wait_ge(turned_taken, i - 1)
                            b = 0
                            for n_h in range(len(hs)):
                                k0 = 0
                                for w in grp["keys"]:
                                    lo = n_h * nk + k0
                                    mm = pe.transpose(bank_t(i)[0:w, b * P:(b + 1) * P],
                                                      probs_sb[:, i % 2, lo:lo + w], ident)
                                    k0 += w
                                    b += 1
                            mm.then_inc(turned, 1)

                        def values(i):
                            g, h0, hs, last = items[i]
                            grp = groups[g]
                            pe.wait_ge(turned_taken, i + 1)
                            if h0 == 0 and g >= 2:
                                pe.wait_ge(combined, g - 1)
                            b = 0
                            for n_h, h in enumerate(hs):
                                at_h = h * HD
                                for kt, w in enumerate(grp["keys"]):
                                    mm = pe.matmul(bank_o(g)[:, at_h:at_h + HD], pT[0:w, i % 2, b * P:(b + 1) * P],
                                                   grp["v"](h, kt), start=(kt == 0), stop=(kt == len(grp["keys"]) - 1))
                                    b += 1
                            mm.then_inc(given, 1)

                        scores(0)
                        for i in range(n):
                            if i + 1 < n:
                                scores(i + 1)
                            turn(i)
                            if i:
                                values(i - 1)
                        values(n - 1)

                    @block.vector
                    def _(dve):
                        chain = Chain(dve, chain_sem)

                        def maxima(i):
                            g, h0, hs, last = items[i]
                            nk = sum(groups[g]["keys"])
                            dve.wait_ge(logits, i + 1)
                            if i >= 2:
                                dve.wait_ge(probs, exps[i - 1])
                            dve.tensor_reduce(nmax[:, i % 2, 0:len(hs)],
                                              bank_l(i)[:, 0:len(hs) * nk].rearrange("p (h k) -> p h k", k=nk),
                                              AX.X, ALU.max, negate=True).then_inc(top, 1)

                        def take(i):
                            g, h0, hs, last = items[i]
                            w, nb = max(groups[g]["keys"]), len(hs) * len(groups[g]["keys"])
                            dve.wait_ge(turned, i + 1)
                            if i >= 2:
                                dve.wait_ge(given, i - 1)
                            dve.tensor_copy(pT[0:w, i % 2, 0:nb * P], bank_t(i)[0:w, 0:nb * P])\
                                .then_inc(turned_taken, 1)

                        def combine(g, i):
                            grp = groups[g]
                            nh = len(grp["heads"])
                            dve.wait_ge(probs, exps[i + 1])
                            k = coef[:, g % 2, 0:nh]
                            chain(dve.reciprocal(k, sums[:, grp["slot"], 0:nh]))
                            for m in grp["factors"]:
                                chain(dve.tensor_tensor(k, k, m, ALU.mult))
                            dve.wait_ge(given, i + 1)
                            o = bank_o(g)[:, 0:nh * HD].rearrange("p (h d) -> p h d", d=HD)
                            kb = k.unsqueeze(2).broadcast_to([P, nh, HD])
                            dst = grp["out"]
                            if grp["add"]:
                                pv = part[:, 0:nh * HD].rearrange("p (h d) -> p h d", d=HD)
                                chain(dve.tensor_tensor(pv, o, kb, ALU.mult))
                                if g:
                                    dve.wait_ge(combined, g)
                                dve.tensor_tensor(dst, dst, pv, ALU.add).then_inc(combined, 1)
                            else:
                                dve.tensor_tensor(dst, o, kb, ALU.mult).then_inc(combined, 1)

                        for i in range(n + 2):
                            if i < n:
                                maxima(i)
                            if 1 <= i <= n:
                                take(i - 1)
                            if i >= 2 and items[i - 2][3]:
                                combine(items[i - 2][0], i - 2)

                    @block.scalar
                    def _(act):
                        for i in range(n):
                            g, h0, hs, last = items[i]
                            nk = sum(groups[g]["keys"])
                            act.wait_ge(top, i + 1)
                            if i >= 2:
                                act.wait_ge(turned, i - 1)
                            for n_h, h in enumerate(hs):
                                act.activation(probs_sb[:, i % 2, n_h * nk:(n_h + 1) * nk],
                                               bank_l(i)[:, n_h * nk:(n_h + 1) * nk], ACT.Exp,
                                               bias=nmax[:, i % 2, n_h:n_h + 1],
                                               accum_out=sums[:, groups[g]["slot"], h:h + 1])\
                                    .then_inc(probs, 1)

        def add_projection(name, u0, src):
            def produce(pe, j, bank):
                half, t = divmod(j, NT)
                if t == 0:
                    stream.arrived(pe, u0 + half)
                return token_tile(pe, u0 + half, 0, UC, t, bank, src=src)

            def consume(eng, j, bank, chain, vector):
                half, t = divmod(j, NT)
                dst = x[:, t, half * UC:(half + 1) * UC]
                return eng.tensor_tensor(dst, dst, bank, ALU.add)

            stage(name, 2 * NT, produce, consume, on_vector=lambda j: True,
                  uses={u0: NT - 1, u0 + 1: 2 * NT - 1})

        def turn_into(name, src, chunks, dst, dst0=0, scale=None):
            def produce(pe, j, bank):
                for t in range(NT):
                    mm = pe.transpose(bank[:, t * P:(t + 1) * P], src[:, t, j * P:(j + 1) * P], ident)
                return mm

            def consume(eng, j, bank, chain, vector):
                if scale is None:
                    return copy(eng, vector, dst[:, dst0 + j, :], bank[:, 0:S])
                if vector:
                    return eng.tensor_scalar(dst[:, dst0 + j, :], bank[:, 0:S], scale(j), None, ALU.mult)
                return eng.activation(dst[:, dst0 + j, :], bank[:, 0:S], ACT.Copy, scale=scale(j))

            stage(name, chunks, produce, consume)

        def close_sums(pe):
            for b in range(4, 8):
                mm = pe.matmul(ps[:, b], c_("noughts")[:, 0:P], c_("noughts"), start=False, stop=True)
            return mm

        def mlp(layer):
            u0 = unit[f"mlp{layer}"]
            n_units = 2 * FF // UC
            trips = n_units // RING
            up_v = a["w_up"][layer].rearrange("(k p) (i b c) -> i b p k c", p=P, b=2, c=UC)
            down_v = a["w_down"][layer].rearrange("(i b k p) c -> i b p k c", p=P, b=2, k=UC // P)
            ups, rect, hid_ready, downs, taken = \
                (sem(f"mlp{layer}_{s}") for s in ("ups", "rectified", "hidden", "downs", "taken"))
            nm = UC // P
            with ExitStack() as on:
                hid = sb("hid", [P, nm, S], on=on)
                rec = sb("rec", [P, nm, S], on=on)

                def up_chunk(m):
                    return ps[:, m // 2, (m % 2) * S:(m % 2 + 1) * S]

                def both(buf, b):
                    return buf[:, 2 * b:2 * b + 2, :].rearrange("p m s -> p (m s)")

                nb = nm // 2

                with meeting() as block:
                    @block.tensor
                    def _(pe):
                        for t in range(NT):
                            for h in range(2):
                                pe.matmul(ps[:, 4 + 2 * t + h], ident, x[:, t, h * UC:(h + 1) * UC],
                                          start=True, stop=False)
                        with pe.Fori(0, trips) as i:
                            for b in range(2):
                                u = u0 + 2 * b
                                w = stream.view(u)
                                pe.wait_ge(stream.sems[u % RING], i * 16 + stream.need[u])
                                for m in range(nm):
                                    for k in range(KD):
                                        mm = pe.matmul(up_chunk(m), w[:, k, m * P:(m + 1) * P], hT[:, k, :],
                                                       start=(k == 0), stop=(k == KD - 1))
                                    if m % 2:
                                        mm.then_inc(ups, 1)
                                u += 1
                                w = stream.view(u)
                                pe.wait_ge(stream.sems[u % RING], i * 16 + stream.need[u])
                                for f in range(nm):
                                    if f % 2 == 0:
                                        pe.wait_ge(hid_ready, i * (2 * nb) + (b * nb + f // 2 + 1))
                                    for t in range(NT):
                                        for h in range(2):
                                            mm = pe.matmul(ps[:, 4 + 2 * t + h], hid[:, f, t * P:(t + 1) * P],
                                                           w[:, f, h * UC:(h + 1) * UC], start=False, stop=False,
                                                           skip_group_check=True)
                                mm.then_inc(downs, 1)
                        close_sums(pe).then_inc(downs, 1)

                    @block.scalar
                    def _(act):
                        with act.Fori(0, trips) as i:
                            for b in range(2):
                                for m in range(nb):
                                    act.wait_ge(ups, i * (2 * nb) + (b * nb + m + 1))
                                    act.activation(both(rec, m), ps[:, m], ACT.Relu).then_inc(rect, 1)

                    @block.vector
                    def _(dve):
                        with dve.Fori(0, trips) as i:
                            for b in range(2):
                                for m in range(nb):
                                    dve.wait_ge(rect, i * (2 * nb) + (b * nb + m + 1))
                                    dve.tensor_tensor(both(hid, m), both(rec, m), both(rec, m), ALU.mult)\
                                        .then_inc(hid_ready, 1)
                        dve.wait_ge(downs, 2 * trips + 1)
                        for t in range(NT):
                            for h in range(2):
                                dve.tensor_copy(x[:, t, h * UC:(h + 1) * UC], ps[:, 4 + 2 * t + h])

                    @block.sync
                    def _(sp):
                        stream.prefetch(sp, u0)
                        with sp.Fori(0, trips - 1) as i:
                            for b in range(2):
                                for kind, v in enumerate((up_v, down_v)):
                                    u = u0 + 2 * b + kind
                                    if kind == 0:
                                        sp.wait_ge(ups, i * (2 * nb) + (b + 1) * nb)
                                    else:
                                        sp.wait_ge(downs, i * 2 + (b + 1))
                                    sp.dma_start(stream.view(u), v[i + 1, b]).then_inc(stream.sems[u % RING], 16)
                        for b in range(2):
                            stream.done[u0 + n_units - RING + 2 * b] = (ups, (2 * trips - 1 + b) * nb)
                            stream.done[u0 + n_units - RING + 2 * b + 1] = (downs, 2 * trips - 1 + b)
                        stream.issued = u0 + n_units
                        stream.prefetch(sp, u0 + n_units)

        def conv_layer():
            with ExitStack() as on:
                z = sb("conv_z", [P, 3 * CONV_CH // P, S], on=on)
                q = sb("conv_q", [P, NT, MW], on=on)
                nconv = CONV_CH // P
                cat = sb("cat", [P, KD, S], on=on)
                u0 = unit["a_in"]
                n_fm = 3 * nconv

                def produce(pe, j, bank):
                    if j < n_fm:
                        if j % 4 == 0:
                            stream.arrived(pe, u0 + j // 4)
                        return feature_chunk(pe, u0 + j // 4, (j % 4) * P, P, bank[:, 0:S])
                    return token_tile(pe, u0 + 4, 2 * P, MW, j - n_fm, bank[:, 0:MW])

                def consume(eng, j, bank, chain, vector):
                    dst = z[:, j, :] if j < n_fm else q[:, j - n_fm, :]
                    return copy(eng, vector, dst, bank[:, 0:S])

                stage("a_in", n_fm + NT, produce, consume,
                      uses={u0: 3, u0 + 1: 7, u0 + 2: 11, u0 + 3: 15, u0 + 4: n_fm + NT - 1})

                conv_step = sem("conv_step")
                with meeting() as block:
                    @block.vector
                    def _(dve):
                        n = 0
                        gb, gc, gu = (z[:, i * nconv:(i + 1) * nconv, :] for i in range(3))
                        dve.tensor_tensor(gc, gc, gu, ALU.mult).then_inc(conv_step, 1)
                        n += 1
                        dve.wait_ge(conv_step, n)
                        for c in range(nconv):
                            dve.tensor_scalar(gu[:, c, :], gc[:, c, :], col("conv_w", 2 * nconv + c), None, ALU.mult)\
                                .then_inc(conv_step, 1)
                        n += nconv
                        dve.wait_ge(conv_step, n)
                        for tap in (1, 0):
                            back = 2 - tap
                            for c in range(nconv):
                                dve.scalar_tensor_tensor(gu[:, c, back:], gc[:, c, 0:S - back],
                                                         col("conv_w", tap * nconv + c), gu[:, c, back:],
                                                         ALU.mult, ALU.add).then_inc(conv_step, 1)
                            n += nconv
                            dve.wait_ge(conv_step, n)
                        dve.tensor_tensor(cat[:, 0:nconv, :], gb, gu, ALU.mult)
                memory_attention(0, q, cat, nconv)
                add_projection("out0", unit["out0"], cat)

        def memory_attention(layer, q, cat, chunk0, more=None, more_norms=(), gates=None):
            with ExitStack() as on:
                qn = sb("mq_n", [P, NT, MW], on=on)
                sq = sb("mq_sq", [P, NT, MW], on=on)
                st = sb("mq_st", [P, 2, NT, MH], on=on)
                qT = sb("mq_T", [P, MW // P, S], on=on)
                ym = sb("ym", [P, NT, MW], on=on)
                sums = sb("mq_sums", [P, NT, MH], on=on)
                head_norm(f"mq{layer}", [([heads(qn)], heads(q), heads(sq), st,
                                          gain("mem_q_gain", layer * HD), HD ** -0.5)])
                turn_into(f"mq_turn{layer}", qn, MW // P, qT)
                groups = []
                for t in range(NT):
                    groups.append(dict(
                        heads=[0, 2, 1, 3], per=2, keys=[P, P], bias=None, slot=t, factors=[], add=False,
                        q=lambda h, t=t: qT[(h % 2) * HD:(h % 2 + 1) * HD, h // 2, t * P:(t + 1) * P],
                        k=lambda h: mem_kT[(h % 2) * HD:(h % 2 + 1) * HD, layer, h // 2, :],
                        v=lambda h, kt: mem_v[:, layer, kt, h * HD:(h + 1) * HD],
                        out=ym[:, t, :].rearrange("p (h d) -> p h d", d=HD)))
                attention(f"mem_attn{layer}", groups, sums)
                turn_into(f"ym_turn{layer}", ym, MW // P, cat, chunk0)

        def shared_buffers(on):
            return dict(
                kT={b: sb(f"{b}_kT", [P, G, S], on=on) for b in ("s", "w")},
                v={b: sb(f"{b}_v", [P, NT, G * HD], on=on) for b in ("s", "w")},
                kcT=sb("c_kT", [P, G, NC], on=on), vc=sb("c_v", [NC, G, HD], on=on))

        def shared_kv(sh, hkv):
            with ExitStack() as on2:
                kv = sb("kv_rest", [P, NT, 4 * G * HD], on=on2)
                pair = sb("cmp_pairs", [P, 2, G, S], on=on2)
                flat = sb("cmp_flat", [P, 2, CMP_L // 2, G * NC], on=on2)
                u0 = unit["kv"]

                def produce(pe, j, bank):
                    if j == 0:
                        stream.arrived(pe, u0)
                    if j == 2 + NT:
                        stream.arrived(pe, u0 + 1)
                    if j < 2:
                        return feature_chunk(pe, u0, j * P, P, bank[:, 0:S], src=hkv)
                    second, t = divmod(j - 2, NT)
                    return token_tile(pe, u0 + second, 0 if second else 2 * P, 2 * P, t, bank[:, 0:2 * P], src=hkv)

                def consume(eng, j, bank, chain, vector):
                    if j < 2:
                        for g in range(G):
                            src = bank[g * HD:(g + 1) * HD, 0:S]
                            eng.tensor_copy(pair[0:HD, j, g, :], src)
                            last = eng.tensor_copy(pair[HD:P, j, g, 0:S - 1], src[:, 1:S])
                            if g == 0:
                                chain(last)
                        return last
                    second, t = divmod(j - 2, NT)
                    return copy(eng, vector, kv[:, t, second * 2 * P:(second + 1) * 2 * P], bank[:, 0:2 * P])

                stage("kv", 2 + 2 * NT, produce, consume, on_vector=lambda j: j < 2 or j % 2 == 0,
                      uses={u0: 1 + NT, u0 + 1: 1 + 2 * NT})

                half = CMP_S // 2
                with meeting() as block:
                    @block.vector
                    def _(dve):
                        for i in range(2):
                            for g in range(G):
                                for part in range(2):
                                    src = pair[:, i, g, part * CMP_S:part * CMP_S + NC * CMP_S]\
                                        .rearrange("p (c l two) -> p l c two", c=NC, two=2)[:, :, :, 0]
                                    pos = col("cmp_pos", i * CMP_L // 2 + part * half, half)
                                    dve.tensor_tensor(flat[:, i, part * half:(part + 1) * half, g * NC:(g + 1) * NC],
                                                      src, pos.unsqueeze(2).broadcast_to([P, half, NC]), ALU.add)

                hidden = sb("cmp_hidden", [G * NC, 2, CMP_H], on=on2)
                u1 = unit["cmp1"]

                def mlp1(pe, j, bank):
                    w = stream.arrived(pe, u1 + j)
                    for k in range(CMP_L // 2):
                        mm = pe.matmul(bank[0:G * NC, 0:CMP_H], flat[:, j, k, :], w[:, k, :],
                                       start=(k == 0), stop=(k == CMP_L // 2 - 1))
                    return mm

                stage("cmp1", 2, mlp1, lambda eng, j, bank, chain, vector:
                      eng.activation(hidden[:, j, :], bank[0:G * NC, 0:CMP_H], ACT.Gelu_apprx_tanh),
                      on_vector=lambda j: False, uses={u1: 0, u1 + 1: 1})
                hiddenT = sb("cmp_hiddenT", [P, 2, 2, G * NC], on=on2)

                def turn(pe, j, bank):
                    for k in range(2):
                        mm = pe.transpose(bank[:, k * P:k * P + G * NC], hidden[:, j, k * P:(k + 1) * P],
                                          ident[0:G * NC, 0:G * NC])
                    return mm

                stage("cmp_turn", 2, turn, lambda eng, j, bank, chain, vector:
                      copy(eng, vector, hiddenT[:, j, :, :],
                           bank[:, 0:2 * P].rearrange("p (k n) -> p k n", k=2)[:, :, 0:G * NC]))
                kc = sb("cmp_k", [NC, 1, G, HD], on=on2)
                dup = sb("kn_dup", [P, 2, NT, G, 2, HD], on=on2)
                cdup = sb("kc_dup", [NC, G, 2, HD], on=on2)

                def mlp2(pe, j, bank):
                    for g in range(G):
                        for k in range(2):
                            mm = pe.matmul(bank[0:NC, g * HD:(g + 1) * HD], hiddenT[:, j, k, g * NC:(g + 1) * NC],
                                           cmp2[:, j, k, :], start=(k == 0), stop=(k == 1))
                    return mm

                stage("cmp2", 2, mlp2, lambda eng, j, bank, chain, vector:
                      eng.tensor_copy(kc[:, 0] if j == 0 else sh["vc"][:, :, :],
                                      bank[0:NC, 0:G * HD].rearrange("p (g d) -> p g d", g=G)),
                      on_vector=lambda j: True)
                sq = sb("kn_sq", [P, 3, NT, G, HD], on=on2)
                st = sb("kn_st", [P, 3, 2, NT, G], on=on2)
                items = [([cdup[:, :, w].unsqueeze(1) for w in range(2)], kc[:, :, :, :], sq[0:NC, 2, 0:1],
                          st[0:NC, 2, :, 0:1], gain("k_gain", 0)[0:NC, :], 1.0)]
                for b in range(2):
                    src = heads(kv[:, :, 2 * b * P:(2 * b + 1) * P])
                    items.append(([dup[:, b, :, :, w] for w in range(2)], src, sq[:, b], st[:, b],
                                  gain("k_gain", (1 + b) * HD), 1.0))
                head_norm("kn", items, copies=[(sh["v"][b][:, :, :], kv[:, :, (2 * n + 1) * P:(2 * n + 2) * P])
                                               for n, b in enumerate(("s", "w"))])

                def turn_keys(pe, j, bank):
                    if j == 2 * G:
                        for g in range(G):
                            mm = pe.transpose(bank[:, g * P:g * P + NC], cdup[:, g].rearrange("p a d -> p (a d)"),
                                              ident[0:NC, 0:NC])
                        return mm
                    b, g = divmod(j, G)
                    for t in range(NT):
                        mm = pe.transpose(bank[:, t * P:(t + 1) * P], dup[:, b, t, g].rearrange("p a d -> p (a d)"),
                                          ident)
                    return mm

                def take_keys(eng, j, bank, chain, vector):
                    if j == 2 * G:
                        return copy(eng, vector, sh["kcT"][:, :, :],
                                    bank[:, 0:G * P].rearrange("p (g n) -> p g n", g=G)[:, :, 0:NC])
                    b, g = divmod(j, G)
                    return copy(eng, vector, sh["kT"]["sw"[b]][:, g, :], bank[:, 0:S])

                stage("kn_turn", 2 * G + 1, turn_keys, take_keys)

        def nsa_layer(sh):
            with ExitStack() as on:
                q = sb("nsa_q", [P, NT, CONV_CH], on=on)
                gates = sb("nsa_gates", [P, NT, NH, 3], on=on)
                mq = sb("nsa_mq", [P, NT, MW], on=on)
                qT = sb("nsa_qT", [P, NH // 2, S], on=on)
                y = sb("nsa_y", [P, NT, CONV_CH], on=on)
                sums = sb("nsa_sums", [P, 3 * NT, NH], on=on)
                cat = sb("cat", [P, KD, S], on=on)
                u0 = unit["b_in"]
                rest = CONV_CH - UC
                with ExitStack() as on2:
                    qn = sb("nsa_qn", [P, NT, CONV_CH], on=on2)
                    sq = sb("nsa_sq", [P, NT, CONV_CH], on=on2)
                    st = sb("nsa_st", [P, 2, NT, NH], on=on2)

                    def produce(pe, j, bank):
                        part, t = divmod(j, NT)
                        width = stream.src[u0 + part][2]
                        if t == 0:
                            stream.arrived(pe, u0 + part)
                        return token_tile(pe, u0 + part, 0, width, t, bank[:, 0:width])

                    def consume(eng, j, bank, chain, vector):
                        part, t = divmod(j, NT)
                        if part == 0:
                            return eng.activation(q[:, t, 0:UC], bank, ACT.Copy)
                        if part == 1:
                            eng.activation(q[:, t, UC:], bank[:, 0:rest], ACT.Copy)
                            return eng.activation(gates[:, t], bank[:, rest:rest + 3 * NH]
                                                  .rearrange("p (h b) -> p h b", b=3), ACT.Sigmoid)
                        return eng.activation(mq[:, t, :], bank[:, 0:MW], ACT.Copy)

                    stage("b_in", 3 * NT, produce, consume, on_vector=lambda j: False,
                          uses={u0 + i: i * NT + 1 for i in range(3)})
                    head_norm("nsa_q", [([heads(qn)], heads(q), heads(sq), st, gain("q_gain"), HD ** -0.5)])
                    turn_into("nsa_qturn", qn, NH // 2, qT)
                groups = []
                for t in range(NT):
                    yt = y[:, t, :].rearrange("p (h d) -> p h d", d=HD)
                    x0 = P * (1 - t)
                    for n, b in enumerate(("c", "s", "w")):
                        grp = dict(
                            heads=[*range(0, NH, 2), *range(1, NH, 2)], slot=t * 3 + n, out=yt, add=n > 0,
                            q=lambda h, t=t: qT[(h % 2) * HD:(h % 2 + 1) * HD, h // 2, t * P:(t + 1) * P],
                            factors=[gates[:, t, :, n]])
                        if b == "c":
                            grp["factors"].append(c_("cmp_rows")[:, t:t + 1].broadcast_to([P, NH]))
                            grp.update(per=3, keys=[NC],
                                       k=lambda h: sh["kcT"][(h % 2) * HD:(h % 2 + 1) * HD, h // HPG, :],
                                       v=lambda h, kt: sh["vc"][:, h // HPG, :],
                                       bias=lambda h, x0=x0: dist[:, h, x0 + CMP_L - 1:x0 + CMP_L + (NC - 1) * CMP_S:CMP_S])
                        else:
                            nk = (t + 1) * P
                            grp.update(per=3 - t, keys=[P] * (t + 1),
                                       k=lambda h, b=b, nk=nk: sh["kT"][b][(h % 2) * HD:(h % 2 + 1) * HD, h // HPG, 0:nk],
                                       v=lambda h, kt, b=b: sh["v"][b][:, kt, (h // HPG) * HD:(h // HPG + 1) * HD],
                                       bias=lambda h, x0=x0, nk=nk: dist[:, h, x0:x0 + nk])
                        groups.append(grp)
                attention("nsa", groups, sums)
                turn_into("nsa_yturn", y, CONV_CH // P, cat)
                memory_attention(1, mq, cat, CONV_CH // P)
                add_projection("out1", unit["out1"], cat)


        def rwkv(ya):
            with ExitStack() as on:
                lora = sb("rw_lora", [P, 2, S], on=on)
                v = sb("rw_v", [P, RC, S], on=on)
                qr = sb("rw_qr", [P, RC, NT, 2 * P], on=on)
                bh = sb("rw_b", [P, RC, S], on=on)
                kh = sb("rw_k", [P, RC, S], on=on)
                kk = sb("rw_kk", [P, RC, S], on=on)
                mid = sb("rw_mid", [P, 4, RC * NT], on=on)
                carry = sb("rw_carry", [P, 2, RC], on=on)
                u0 = unit["rwkv"]
                with ExitStack() as on2:
                    r = sb("rw_r", [P, RC, S], on=on2)
                    k = sb("rw_kraw", [P, RC, S], on=on2)
                    dec = sb("rw_dec", [P, RC, S], on=on2)
                    aa = sb("rw_a", [P, RC, S], on=on2)
                    tmp = sb("rw_tmp", [P, RC, S], on=on2)
                    sums = sb("rw_sums", [P, RC, NT, P + 1], on=on2)
                    w_da = sums[:, :, :, :].rearrange("p c t n -> p (c t n)")[:, 0:RW]
                    shifted = tmp[:, :, :].rearrange("p c s -> p (c s)")[:, 0:2 * (S + 1)]\
                        .rearrange("p (n s) -> p n s", n=2)
                    raw = lambda j: (r, k, v, lora)[j // RC][:, j % RC, :]

                    def produce(pe, j, bank):
                        if j % 4 == 0:
                            stream.arrived(pe, u0 + j // 4)
                        return feature_chunk(pe, u0 + j // 4, (j % 4) * P, P, bank[:, 0:S])

                    def consume(eng, j, bank, chain, vector):
                        if j == 0:
                            chain(eng.memset(shifted[:, :, 0:1], 0.0))
                        sh = shifted[:, j % 2]
                        chain(eng.tensor_scalar(sh[:, 1:], bank[:, 0:S], col("mu", j), None, ALU.mult))
                        chain(eng.tensor_tensor(raw(j), bank[:, 0:S], sh[:, 1:], ALU.subtract))
                        return eng.tensor_tensor(raw(j), raw(j), sh[:, 0:S], ALU.add)

                    n_ch = R_COLS // P
                    stage("rwkv_in", n_ch, produce, consume, on_vector=lambda j: True,
                          uses={u0 + i: min(4 * i + 3, n_ch - 1) for i in range(7)},
                          loads=[(w_da[0:LORA, :], a["rwkv_w_decay_2"][0]), (w_da[LORA:P, :], a["rwkv_w_a_2"][0])])
                    lora_ready = sem("lora_ready")
                    with meeting() as block:
                        @block.scalar
                        def _(act):
                            act.activation(lora[0:LORA, 0, :], lora[0:LORA, 0, :], ACT.Tanh)
                            act.activation(lora[:, 1, :], lora[:, 1, :], ACT.Sigmoid)

                        @block.vector
                        def _(dve):
                            for c in range(RC):
                                dve.tensor_scalar(kk[:, c, :], k[:, c, :], col("k_k", c), None, ALU.mult)

                    def lora_up(pe, j, bank):
                        which, c = divmod(j, RC)
                        lo = which * LORA
                        return pe.matmul(bank[:, 0:S], w_da[lo:lo + LORA, c * P:(c + 1) * P],
                                         lora[lo:lo + LORA, 0, :], start=True, stop=True)

                    stage("lora_up", 2 * RC, lora_up, lambda eng, j, bank, chain, vector:
                          eng.activation((dec, aa)[j // RC][:, j % RC, :], bank[:, 0:S], ACT.Sigmoid,
                                         bias=col(("w0", "a0")[j // RC], j % RC)), on_vector=lambda j: False)

                    flat = lambda z: z[:, :, :].rearrange("p c s -> p (c s)")
                    squares, lengths, roots, made = (sem("kk_" + s) for s in ("squares", "lengths", "roots", "made"))
                    with meeting() as block:
                        @block.scalar
                        def _(act):
                            act.activation(flat(tmp), flat(kk), ACT.Square).then_inc(squares, 1)
                            for b in range(4):
                                act.wait_ge(lengths, b + 1)
                                act.activation(flat(tmp)[:, b * 512:(b + 1) * 512], ps[:, b], ACT.Sqrt).then_inc(roots, 1)

                        @block.tensor
                        def _(pe):
                            pe.wait_ge(squares, 1)
                            for b in range(4):
                                pe.matmul(ps[:, b], c_("headones"), flat(tmp)[:, b * 512:(b + 1) * 512],
                                          start=True, stop=True).then_inc(lengths, 1)

                        @block.vector
                        def _(dve):
                            chain = Chain(dve, made)
                            chain(dve.memset(sums[:, :, :, 0:1], 0.0))
                            for c in range(RC):
                                for t in range(NT):
                                    dve.tensor_tensor_scan(sums[:, c, t, 1:], c_("ones"), dec[:, c, t * P:(t + 1) * P],
                                                           0.0, ALU.mult, ALU.add)
                            dve.wait_ge(roots, 4)
                            chain(dve.tensor_scalar(flat(tmp), flat(tmp), 1e-12, None, ALU.max))
                            chain(dve.reciprocal(flat(dec), flat(tmp)))
                            chain(dve.tensor_tensor(flat(kk), flat(kk), flat(dec), ALU.mult))
                            middle = sums[:, :, :, P // 2].rearrange("p c t -> p (c t)")
                            dve.tensor_scalar(mid[:, 0, :], middle, KAPPA, None, ALU.mult)
                            chain(dve.tensor_scalar(mid[:, 1, :], middle, -KAPPA, None, ALU.mult))
                            chain(dve.tensor_tensor(carry[:, 1, :], sums[:, :, 0, P // 2], sums[:, :, 0, P], ALU.subtract))
                            chain(dve.tensor_tensor(carry[:, 1, :], carry[:, 1, :], sums[:, :, 1, P // 2], ALU.subtract))
                            k_a = col("k_a", 0, RC)
                            chain(dve.tensor_scalar(mid[:, 2, 0:RC], k_a, -1.0, 1.0, ALU.mult, ALU.add))
                            for c in range(RC):
                                dve.tensor_scalar(kh[:, c, :], aa[:, c, :], col("k_a", c), mid[:, 2, c:c + 1],
                                                  ALU.mult, ALU.add)
                            chain(dve.tensor_tensor(flat(bh), flat(kk), flat(aa), ALU.mult))
                            dve.tensor_tensor(flat(kh), flat(kh), flat(k), ALU.mult)

                    exps, scaled = sem("rw_exps"), sem("rw_scaled")
                    with meeting() as block:
                        @block.scalar
                        def _(act):
                            act.activation(carry[:, 0, :], carry[:, 1, :], ACT.Exp, scale=KAPPA)
                            for c in range(RC):
                                for t in range(NT):
                                    n = c * NT + t
                                    act.activation(qr[:, c, t, 0:P], sums[:, c, t, 0:P], ACT.Exp,
                                                   scale=-KAPPA, bias=mid[:, 0, n:n + 1])
                                    act.activation(qr[:, c, t, P:], sums[:, c, t, 1:], ACT.Exp,
                                                   scale=-KAPPA, bias=mid[:, 0, n:n + 1])
                                    act.activation(tmp[:, c, t * P:(t + 1) * P], sums[:, c, t, 1:], ACT.Exp,
                                                   scale=KAPPA, bias=mid[:, 1, n:n + 1]).then_inc(exps, 1)

                        @block.vector
                        def _(dve):
                            for c in range(RC):
                                dve.scalar_tensor_tensor(dec[:, c, :], r[:, c, :], col("r_k", c), kh[:, c, :],
                                                         ALU.mult, ALU.mult).then_inc(scaled, 1)
                            for c in range(RC):
                                dve.wait_ge(scaled, c + 1)
                                dve.wait_ge(exps, NT * (c + 1))
                                tiles = lambda z: z[:, c, :].rearrange("p (t s) -> p t s", t=NT)
                                dve.tensor_tensor(qr[:, c, :, 0:P], qr[:, c, :, 0:P], tiles(kk), ALU.mult)
                                dve.tensor_tensor(qr[:, c, :, P:], qr[:, c, :, P:], tiles(r), ALU.mult)
                                dve.tensor_tensor(bh[:, c, :], bh[:, c, :], tmp[:, c, :], ALU.mult)
                                dve.tensor_tensor(kh[:, c, :], kh[:, c, :], tmp[:, c, :], ALU.mult)
                                dve.wait_ge(scaled, RC)
                    with meeting() as block:
                        @block.vector
                        def _(dve):
                            dve.tensor_copy(flat(kk), flat(dec))
                v_tok = sb("rw_v_tok", [P, NT, RW], on=on)
                b_tok = sb("rw_b_tok", [P, RW], on=on)
                k_tok = sb("rw_k_tok", [P, RW], on=on)
                bonus = sb("rw_bonus", [P, NT, RH], on=on)
                turns = [(v, 0, v_tok[:, 0, :]), (v, 1, v_tok[:, 1, :]), (bh, 0, b_tok), (kh, 0, k_tok)]

                def turn(pe, j, bank):
                    if j == 8:
                        for t in range(NT):
                            for c in range(RC):
                                lo = t * RH + 2 * c
                                mm = pe.matmul(bank[:, lo:lo + 2], kk[:, c, t * P:(t + 1) * P], c_("headsel"),
                                               start=True, stop=True)
                        return mm
                    src, t, _ = turns[j // 2]
                    for i in range(4):
                        mm = pe.transpose(bank[:, i * P:(i + 1) * P], src[:, (j % 2) * 4 + i, t * P:(t + 1) * P], ident)
                    return mm

                def take(eng, j, bank, chain, vector):
                    if j == 8:
                        return copy(eng, vector, bonus[:, :, :], bank[:, 0:NT * RH].rearrange("p (t h) -> p t h", t=NT))
                    return copy(eng, vector, turns[j // 2][2][:, (j % 2) * 512:(j % 2 + 1) * 512], bank)

                stage("rw_turn", 9, turn, take)
                with ExitStack() as on2:
                    rwkv_tiles(on2, qr, bh, kh, v_tok, b_tok, k_tok, carry, ya)
                rwkv_out(ya, v_tok, bonus, lora)

        def rwkv_tiles(on, qr, bh, kh, v_tok, b_tok, k_tok, carry, ya):
            ac = sb("rw_ac", [P, 2, 4, 2 * P], on=on)
            bd = sb("rw_bd", [P, 2, 4, 2 * P], on=on)
            inv = sb("rw_inv", [P, 2, 4, P], on=on)
            invT = sb("rw_invT", [P, 2, 4, P], on=on)
            half = sb("rw_half", [P, 2, 4, P], on=on)
            w = sb("rw_w", [P, 2, P], on=on)
            uu = sb("rw_u", [P, 2, P], on=on)
            state = sb("rw_state", [P, 2, HD], on=on)
            levels = 7
            n_steps = 2 * levels + 6
            made, taken, chain_sem = sem("rw_made"), sem("rw_taken"), sem("rw_chain")
            hp_rows = lambda hp: slice(hp * HD, (hp + 1) * HD)

            def level(i):
                return c_("levels")[:, i * P:(i + 1) * P].unsqueeze(1).broadcast_to([P, 4, P])

            def products(pe, c, p, s):
                bank = lambda b: ps[:, 4 * p + b]
                four = lambda b: bank(b).rearrange("p (u n) -> p u n", u=4)
                hcols = lambda hp: slice((2 * c + hp) * HD, (2 * c + hp + 1) * HD)
                if s == 0:
                    for n, left in enumerate((bh, kh)):
                        for t in range(NT):
                            for hp in range(2):
                                mm = pe.matmul(bank(2 * n + hp)[:, t * 2 * P:(t + 1) * 2 * P],
                                               left[hp_rows(hp), c, t * P:(t + 1) * P], qr[hp_rows(hp), c, t, :],
                                               start=True, stop=True)
                    return mm
                if s == 1:
                    for u in range(4):
                        mm = pe.transpose(four(0)[:, u], invT[:, p, u], ident)
                    return mm
                if s < 2 * levels:
                    for u in range(4):
                        if s % 2 == 0:
                            mm = pe.matmul(four(1)[:, u], ac[:, p, u, 0:P], inv[:, p, u], start=True, stop=True)
                        else:
                            if s < 2 * levels - 1:
                                pe.matmul(four(2)[:, u], invT[:, p, u], half[:, p, u], start=True, stop=True)
                            mm = pe.matmul(four(3)[:, u], half[:, p, u], invT[:, p, u], start=True, stop=True)
                    return mm
                s -= 2 * levels
                for hp in range(2):
                    t = 0 if s < 3 else 1
                    u = 2 * hp + t
                    vt = v_tok[:, t, hcols(hp)]
                    us = uu[:, p, hp * HD:(hp + 1) * HD]
                    cols2 = slice(hp * HD, (hp + 1) * HD)
                    q_, r_ = qr[hp_rows(hp), c, 1, 0:P], qr[hp_rows(hp), c, 1, P:]
                    st = state[hp_rows(hp), p, :]
                    if s == 0:
                        mm = pe.matmul(bank(0)[:, cols2], bd[:, p, u, 0:P], vt, start=True, stop=True)
                    elif s in (1, 4):
                        mm = pe.matmul(bank(2)[:, cols2], invT[:, p, u], w[:, p, cols2], start=True, stop=True)
                    elif s == 2:
                        pe.matmul(bank(0)[:, cols2], ac[:, p, u, P:], us, start=True, stop=False)
                        pe.matmul(bank(0)[:, cols2], bd[:, p, u, P:], vt, start=False, stop=True)
                        pe.matmul(bank(3)[hp_rows(hp), 0:HD], b_tok[:, hcols(hp)], us, start=True, stop=False)
                        mm = pe.matmul(bank(3)[hp_rows(hp), 0:HD], k_tok[:, hcols(hp)], vt, start=False, stop=True)
                    elif s == 3:
                        pe.matmul(bank(hp)[:, 0:HD], q_, st, start=True, stop=False)
                        mm = pe.matmul(bank(hp)[:, 0:HD], bd[:, p, u, 0:P], vt, start=False, stop=True)
                    else:
                        pe.matmul(bank(hp)[:, 0:HD], r_, st, start=True, stop=False)
                        pe.matmul(bank(hp)[:, 0:HD], ac[:, p, u, P:], us, start=False, stop=False)
                        mm = pe.matmul(bank(hp)[:, 0:HD], bd[:, p, u, P:], vt, start=False, stop=True)
                return mm

            def results(dve, chain, c, p, s):
                bank = lambda b: ps[:, 4 * p + b]
                four = lambda b: bank(b).rearrange("p (u n) -> p u n", u=4)
                if s == 0:
                    mask = c_("strict_incl").unsqueeze(1).broadcast_to([P, NT, 2 * P])
                    for n, dst in enumerate((ac, bd)):
                        for hp in range(2):
                            last = dve.tensor_tensor(dst[:, p, 2 * hp:2 * hp + 2, :],
                                                     bank(2 * n + hp).rearrange("p (t n) -> p t n", t=NT), mask, ALU.mult)
                    chain(last)
                    chain(dve.tensor_tensor(half[:, p], ac[:, p, :, 0:P], level(0), ALU.mult))
                    return dve.tensor_tensor(invT[:, p], ident.unsqueeze(1).broadcast_to([P, 4, P]), half[:, p],
                                             ALU.subtract)
                if s == 1:
                    return dve.tensor_copy(inv[:, p], four(0))
                if s < 2 * levels:
                    if s % 2 == 0:
                        return dve.tensor_tensor(half[:, p], four(1), level(s // 2), ALU.mult)
                    if s < 2 * levels - 1:
                        dve.tensor_tensor(inv[:, p], inv[:, p], four(2), ALU.subtract)
                    return dve.tensor_tensor(invT[:, p], invT[:, p], four(3), ALU.subtract)
                s -= 2 * levels
                t = 0 if s < 3 else 1
                if s == 0:
                    return dve.tensor_scalar(w[:, p, :], bank(0)[:, 0:P], -1.0, None, ALU.mult)
                if s in (1, 4):
                    return dve.tensor_copy(uu[:, p, :], bank(2)[:, 0:P])
                if s == 2:
                    dve.tensor_copy(ya[:, 0, c * P:(c + 1) * P], bank(0)[:, 0:P])
                    return dve.tensor_scalar(state[:, p, :], bank(3)[:, 0:HD], carry[:, 0, c:c + 1], None, ALU.mult)
                for hp in range(2):
                    cols2 = slice(hp * HD, (hp + 1) * HD)
                    if s == 3:
                        last = dve.tensor_scalar(w[:, p, cols2], bank(hp)[:, 0:HD], -1.0, None, ALU.mult)
                    else:
                        last = dve.tensor_copy(ya[:, 1, c * P + hp * HD:c * P + (hp + 1) * HD], bank(hp)[:, 0:HD])
                return last

            order = [(2 * i + p, p, s) for i in range(RC // 2) for s in range(n_steps) for p in range(2)]
            with meeting() as block:
                @block.tensor
                def _(pe):
                    for n, (c, p, s) in enumerate(order):
                        if n >= 2:
                            pe.wait_ge(taken, n - 1)
                        products(pe, c, p, s).then_inc(made, 1)

                @block.vector
                def _(dve):
                    chain = Chain(dve, chain_sem)
                    for n, (c, p, s) in enumerate(order):
                        dve.wait_ge(made, n + 1)
                        if n >= 2:
                            dve.wait_ge(taken, n - 1)
                        results(dve, chain, c, p, s).then_inc(taken, 1)

        def rwkv_out(ya, v_tok, bonus, lora):
            with ExitStack() as on:
                w_g = sb("rw_wg", [P, RW], on=on)
                ln = sb("rw_ln", [P, 2, RW], on=on)
                gate = sb("rw_gate", [P, NT, RW], on=on)
                sq = sb("rw_sq", [P, NT, RW], on=on)
                st = sb("rw_gn", [P, 3, NT, RH], on=on)
                landed = sem("rw_out_landed")
                centred, squared, rooted, work = (sem("gn_" + s) for s in ("centred", "squared", "rooted", "work"))
                yh, sh_, vh = heads(ya), heads(sq), heads(v_tok)
                shape = [P, NT, RH, HD]
                wide = lambda z: z.unsqueeze(3).broadcast_to(shape)
                rows = lambda z: z.unsqueeze(1).broadcast_to([P, NT, RW])
                with meeting() as block:
                    @block.sync
                    def _(sp):
                        sp.dma_start(w_g[:, :], a["rwkv_w_g_2"][0]).then_inc(landed, 16)
                        sp.dma_start(ln[:, 0, :], everywhere(a["rwkv_ln_g_2"], RW)).then_inc(landed, 16)
                        sp.dma_start(ln[:, 1, :], everywhere(a["rwkv_ln_b_2"], RW)).then_inc(landed, 16)

                    @block.tensor
                    def _(pe):
                        pe.wait_ge(landed, 48)
                        for t in range(NT):
                            for h in range(2):
                                mm = pe.matmul(ps[:, 2 * t + h], lora[:, 1, t * P:(t + 1) * P],
                                               w_g[:, h * UC:(h + 1) * UC], start=True, stop=True)
                        mm.then_inc(squared, 1)

                    @block.scalar
                    def _(act):
                        act.wait_ge(centred, 1)
                        act.wait_ge(squared, 1)
                        act.activation(sh_, yh, ACT.Square).then_inc(squared, 1)
                        act.activation(gate[:, :, :], ps[:, 0:4].rearrange("p (t b) n -> p t (b n)", t=NT), ACT.Copy)\
                            .then_inc(squared, 1)
                        act.wait_ge(centred, 2)
                        act.activation(st[:, 2], st[:, 1], ACT.Sqrt).then_inc(rooted, 1)

                    @block.vector
                    def _(dve):
                        chain = Chain(dve, work)
                        chain(dve.tensor_reduce(st[:, 0], yh, AX.X, ALU.add))
                        chain(dve.tensor_scalar(st[:, 0], st[:, 0], 1.0 / HD, None, ALU.mult))
                        dve.tensor_tensor(yh, yh, wide(st[:, 0]), ALU.subtract).then_inc(centred, 1)
                        dve.wait_ge(squared, 2)
                        chain(dve.tensor_reduce(st[:, 1], sh_, AX.X, ALU.add))
                        dve.tensor_scalar(st[:, 1], st[:, 1], 1.0 / HD, GN_EPS, ALU.mult, ALU.add).then_inc(centred, 1)
                        dve.wait_ge(rooted, 1)
                        chain(dve.reciprocal(st[:, 0], st[:, 2]))
                        chain(dve.tensor_tensor(yh, yh, wide(st[:, 0]), ALU.mult))
                        dve.wait_ge(landed, 48)
                        chain(dve.tensor_tensor(ya[:, :, :], ya[:, :, :], rows(ln[:, 0, :]), ALU.mult))
                        chain(dve.tensor_tensor(ya[:, :, :], ya[:, :, :], rows(ln[:, 1, :]), ALU.add))
                        chain(dve.tensor_tensor(sh_, vh, wide(bonus[:, :, :]), ALU.mult))
                        chain(dve.tensor_tensor(yh, yh, sh_, ALU.add))
                        dve.wait_ge(squared, 3)
                        dve.tensor_tensor(ya[:, :, :], ya[:, :, :], gate[:, :, :], ALU.mult)

        def ssd(u_out):
            HG = SH // SG
            GW = SW // SG
            with ExitStack() as on:
                bc = sb("ssd_bc", [P, 2 * SG, S], on=on)
                xs = sb("ssd_x", [P, NT, SW], on=on)
                dts = sb("ssd_dt", [SH, 6, S], on=on)
                dt_tok = sb("ssd_dt_tok", [P, 2, NT, SH], on=on)
                u0, ud = unit["xbc"], unit["dt"]
                with ExitStack() as on2:
                    xT = sb("ssd_xT", [P, SW // P, S], on=on2)
                    nx, nb = SW // P, 2 * SG
                    part = lambda j: xT[:, j, :] if j < nx else bc[:, j - nx, :]

                    def produce(pe, j, bank):
                        if j == nx + nb:
                            stream.arrived(pe, ud)
                            return feature_chunk(pe, ud, 0, SH, bank[0:SH, 0:S])
                        if j % 4 == 0:
                            stream.arrived(pe, u0 + j // 4)
                        return feature_chunk(pe, u0 + j // 4, (j % 4) * P, P, bank[:, 0:S])

                    def consume(eng, j, bank, chain, vector):
                        if j == nx + nb:
                            return eng.tensor_scalar(dts[:, 0, :], bank[0:SH, 0:S], ssd_cols[:, 0:1], None, ALU.add)
                        d = part(j)
                        chain(eng.tensor_scalar(d, bank[:, 0:S], col("ssd_conv_w", 3 * (nx + nb) + j),
                                                col("ssd_conv_b", j), ALU.mult, ALU.add))
                        for tap in (2, 1, 0):
                            back = 3 - tap
                            last = eng.scalar_tensor_tensor(d[:, back:], bank[:, 0:S - back],
                                                            col("ssd_conv_w", tap * (nx + nb) + j), d[:, back:],
                                                            ALU.mult, ALU.add)
                            if tap:
                                chain(last)
                        return last

                    stage("xbc", nx + nb + 1, produce, consume, on_vector=lambda j: True,
                          uses={**{u0 + i: 4 * i + 3 for i in range(6)}, ud: nx + nb})

                    work, acted = sem("dt_work"), sem("dt_acted")
                    z_, e_, u_, d_, l_, out_ = (dts[:, i, :] for i in range(6))
                    with meeting() as block:
                        @block.scalar
                        def _(act):
                            act.activation(e_, z_, ACT.Abs).then_inc(acted, 1)
                            act.wait_ge(acted, 1)
                            act.activation(e_, e_, ACT.Exp, scale=-1.0).then_inc(acted, 1)
                            act.activation(ssd_cols[:, 2:3], ssd_cols[:, 1:2], ACT.Exp).then_inc(acted, 1)
                            act.wait_ge(work, 1)
                            act.activation(l_, u_, ACT.Ln).then_inc(acted, 1)
                            for i in range(0, nx, 4):
                                act.activation(xT[:, i:i + 4, :], xT[:, i:i + 4, :], ACT.Silu)
                            for i in range(0, nb, 4):
                                act.activation(bc[:, i:i + 4, :], bc[:, i:i + 4, :], ACT.Silu)

                        @block.vector
                        def _(dve):
                            chain = Chain(dve, work)
                            dve.wait_ge(acted, 3)
                            chain(dve.tensor_scalar(u_, e_, 1.0, None, ALU.add))
                            chain(dve.tensor_scalar(d_, u_, -1.0, None, ALU.add))
                            chain(dve.tensor_scalar(out_, d_, 0.0, None, ALU.is_equal))
                            chain(dve.tensor_tensor(out_, out_, e_, ALU.mult))
                            chain(dve.tensor_scalar(d_, d_, 1e-30, None, ALU.max))
                            dve.wait_ge(acted, 4)
                            chain(dve.reciprocal(u_, d_))
                            chain(dve.tensor_tensor(e_, e_, u_, ALU.mult))
                            chain(dve.tensor_tensor(e_, e_, l_, ALU.mult))
                            chain(dve.tensor_tensor(e_, e_, out_, ALU.add))
                            chain(dve.tensor_scalar(z_, z_, 0.0, None, ALU.max))
                            chain(dve.tensor_tensor(z_, z_, e_, ALU.add))
                            chain(dve.tensor_scalar(d_, z_, ssd_cols[:, 2:3], -1.0, ALU.mult, ALU.mult))
                            chain(dve.memset(l_, 1.0))
                            dve.tensor_tensor_scan(u_, l_, d_, 0.0, ALU.mult, ALU.add)

                    def turn(pe, j, bank):
                        if j == 8:
                            for i, src in enumerate((z_, u_)):
                                for t in range(NT):
                                    lo = (i * NT + t) * SH
                                    mm = pe.transpose(bank[:, lo:lo + SH], src[:, t * P:(t + 1) * P], ident[0:SH, 0:SH])
                            return mm
                        t, i4 = divmod(j, 4)
                        for i in range(4):
                            mm = pe.transpose(bank[:, i * P:(i + 1) * P], xT[:, i4 * 4 + i, t * P:(t + 1) * P], ident)
                        return mm

                    def take(eng, j, bank, chain, vector):
                        if j == 8:
                            return copy(eng, vector, dt_tok[:, :, :, :],
                                        bank[:, 0:2 * NT * SH].rearrange("p (i t h) -> p i t h", i=2, t=NT))
                        t, i4 = divmod(j, 4)
                        return copy(eng, vector, xs[:, t, i4 * 512:(i4 + 1) * 512], bank)

                    stage("ssd_turn", 9, turn, take, loads=[(acs_row, u_)])

                uz = unit["z"]

                def produce_z(pe, j, bank):
                    n, t = divmod(j, NT)
                    if t == 0:
                        stream.arrived(pe, uz + n)
                    return token_tile(pe, uz + n, 0, UC, t, bank)

                stage("z", 4 * NT, produce_z, lambda eng, j, bank, chain, vector:
                      eng.activation(u_out[:, j % NT, (j // NT) * UC:(j // NT + 1) * UC], bank, ACT.Silu),
                      on_vector=lambda j: False, uses={uz + n: n * NT + 1 for n in range(4)})

                acs = sb("ssd_acs", [P, 2, HG, S], on=on)
                cb = sb("ssd_cb", [P, SG, 3 * P], on=on)
                xdt = sb("ssd_xdt", [P, 2, NT, GW], on=on)
                seg = sb("ssd_seg", [P, 2, 3 * P], on=on)
                dec = sb("ssd_dec", [P, 2, 3 * P], on=on)
                mix = sb("ssd_mix", [P, 2, 3 * P], on=on)
                xd = sb("ssd_xd", [P, 2, GW], on=on)
                cb_made, cb_taken, rows_in, segs, decs, mixes, xdts, given, finished, chain_sem = \
                    (sem("ssd_" + s) for s in ("cb_made", "cb_taken", "rows_in", "segs", "decs", "mixes", "xdts",
                                               "given", "finished", "chain"))
                rows_in2 = sem("ssd_rows_in2")
                incl = c_("strict_incl")[:, P:]
                per_head = lambda z: z.rearrange("p (h d) -> p h d", d=HD)
                wide = lambda z: z.unsqueeze(2).broadcast_to([P, HG, HD])
                with meeting() as block:
                    @block.sync
                    def _(sp):
                        for g in range(SG):
                            if g >= 2:
                                sp.wait_ge(segs, (g - 1) * HG)
                            sp.dma_start(acs[:, g % 2, :, :], bass.AP(acs_row.tensor, g * HG * S, [[0, P], [1, HG * S]])
                                         .rearrange("p (h s) -> p h s", h=HG)).then_inc((rows_in, rows_in2)[g % 2], 16)

                    @block.tensor
                    def _(pe):
                        for g in range(SG):
                            pe.matmul(ps[:, g, 0:S], bc[:, g, 0:P], bc[:, SG + g, :], start=True, stop=True)
                            pe.matmul(ps[:, g, S:3 * P], bc[:, g, P:], bc[:, SG + g, P:], start=True, stop=True)\
                                .then_inc(cb_made, 1)
                        for g in range(SG):
                            if g >= 2:
                                pe.wait_ge(finished, g - 1)
                            pe.wait_ge(xdts, g + 1)
                            for hg in range(HG):
                                h = g * HG + hg
                                pe.wait_ge(mixes, h + 1)
                                o = [ps[:, 4 + 2 * (g % 2) + t, hg * HD:(hg + 1) * HD] for t in range(NT)]
                                xv = [xdt[:, g % 2, t, hg * HD:(hg + 1) * HD] for t in range(NT)]
                                pe.matmul(o[0], mix[:, h % 2, 0:P], xv[0], start=True, stop=True)
                                pe.matmul(o[1], mix[:, h % 2, P:2 * P], xv[0], start=True, stop=False)
                                pe.matmul(o[1], mix[:, h % 2, 2 * P:], xv[1], start=False, stop=True).then_inc(given, 1)

                    @block.scalar
                    def _(act):
                        for h in range(SH):
                            act.wait_ge(segs, h + 1)
                            if h >= 2:
                                act.wait_ge(mixes, h - 1)
                            act.activation(dec[:, h % 2, :], seg[:, h % 2, :], ACT.Exp).then_inc(decs, 1)

                    @block.vector
                    def _(dve):
                        chain = Chain(dve, chain_sem)
                        for g in range(SG):
                            dve.wait_ge(cb_made, g + 1)
                            dve.tensor_tensor(cb[:, g, 0:P], ps[:, g, 0:P], incl, ALU.mult)
                            dve.tensor_copy(cb[:, g, P:2 * P], ps[:, g, P:2 * P])
                            dve.tensor_tensor(cb[:, g, 2 * P:], ps[:, g, 2 * P:3 * P], incl, ALU.mult)\
                                .then_inc(cb_taken, 1)

                        def differences(h):
                            g, hg = divmod(h, HG)
                            if hg == 0:
                                dve.wait_ge((rows_in, rows_in2)[g % 2], 16 * (g // 2 + 1))
                            if h >= 2:
                                dve.wait_ge(decs, h - 1)
                            dve.tensor_scalar(seg[:, h % 2, 0:S], acs[:, g % 2, hg, :], dt_tok[:, 1, 0, h:h + 1], 0.0,
                                              ALU.subtract, ALU.min)
                            dve.tensor_scalar(seg[:, h % 2, S:], acs[:, g % 2, hg, P:], dt_tok[:, 1, 1, h:h + 1], 0.0,
                                              ALU.subtract, ALU.min).then_inc(segs, 1)

                        def weigh(h):
                            dve.wait_ge(decs, h + 1)
                            if h >= 2:
                                dve.wait_ge(given, h - 1)
                            dve.tensor_tensor(mix[:, h % 2, :], dec[:, h % 2, :], cb[:, h // HG, :], ALU.mult)\
                                .then_inc(mixes, 1)

                        def inputs(g):
                            if g >= 2:
                                dve.wait_ge(given, (g - 1) * HG)
                            for t in range(NT):
                                last = dve.tensor_tensor(per_head(xdt[:, g % 2, t, :]),
                                                         per_head(xs[:, t, g * GW:(g + 1) * GW]),
                                                         wide(dt_tok[:, 0, t, g * HG:(g + 1) * HG]), ALU.mult)
                            last.then_inc(xdts, 1)

                        def finish(g):
                            dve.wait_ge(given, (g + 1) * HG)
                            for t in range(NT):
                                cols_g = slice(g * GW, (g + 1) * GW)
                                chain(dve.tensor_tensor(per_head(xd[:, t, :]), per_head(xs[:, t, cols_g]),
                                                        wide(gain("d_skip", g * HG, HG)), ALU.mult))
                                chain(dve.tensor_tensor(xd[:, t, :], xd[:, t, :], ps[:, 4 + 2 * (g % 2) + t], ALU.add))
                                last = dve.tensor_tensor(u_out[:, t, cols_g], u_out[:, t, cols_g], xd[:, t, :], ALU.mult)
                            last.then_inc(finished, 1)

                        dve.wait_ge(cb_taken, SG)
                        differences(0)
                        for h in range(SH):
                            if h % HG == 0:
                                inputs(h // HG)
                            if h + 1 < SH:
                                differences(h + 1)
                            weigh(h)
                            if h % HG == 1 and h >= HG:
                                finish(h // HG - 1)
                        finish(SG - 1)

                sums, scaled, rooted = sem("sn_sums"), sem("sn_scaled"), sem("sn_rooted")
                st = sb("ssd_st", [P, 3, NT, SG], on=on)
                junk = xs
                with meeting() as block:
                    @block.scalar
                    def _(act):
                        for t in range(NT):
                            for g in range(SG):
                                act.activation(junk[:, t, g * GW:(g + 1) * GW], u_out[:, t, g * GW:(g + 1) * GW],
                                               ACT.Square, accum_out=st[:, 0, t, g:g + 1]).then_inc(sums, 1)
                        act.wait_ge(scaled, 1)
                        act.activation(st[:, 2], st[:, 1], ACT.Sqrt).then_inc(rooted, 1)

                    @block.vector
                    def _(dve):
                        dve.wait_ge(sums, NT * SG)
                        dve.tensor_scalar(st[:, 1], st[:, 0], 1.0 / GW, EPS, ALU.mult, ALU.add).then_inc(scaled, 1)
                        dve.wait_ge(rooted, 1)
                        dve.reciprocal(st[:, 0], st[:, 2]).then_inc(scaled, 1)
                        dve.wait_ge(scaled, 2)
                        for t in range(NT):
                            v = u_out[:, t, :].rearrange("p (g n) -> p g n", g=SG)
                            dve.tensor_tensor(v, v, st[:, 0, t, :].unsqueeze(2).broadcast_to([P, SG, GW]), ALU.mult)

        def project(name, u0, src, dst, parts=1):
            def produce(pe, j, bank):
                half, t = divmod(j, NT)
                for r in range(parts):
                    u = u0 + half * parts + r
                    if t == 0:
                        stream.arrived(pe, u)
                    mm = token_tile(pe, u, 0, UC, t, bank, src=src[:, r * KD:(r + 1) * KD, :],
                                    first=r == 0, last=r == parts - 1)
                return mm

            stage(name, 2 * NT, produce, lambda eng, j, bank, chain, vector:
                  copy(eng, vector, dst[:, j % NT, (j // NT) * UC:(j // NT + 1) * UC], bank),
                  uses={u0 + half * parts + r: half * NT + 1 for half in range(2) for r in range(parts)})

        def merge(by_a, by_b):
            with ExitStack() as on:
                gates = sb("merge_gates", [P, NT, 2 * D], on=on)
                bias = sb("merge_bias", [P, 2 * D], on=on)
                landed = sem("gate_bias_landed")
                with meeting() as block:
                    @block.sync
                    def _(sp):
                        sp.dma_start(bias[:, :], everywhere(a["b_gate_2"], 2 * D)).then_inc(landed, 16)
                        sp.wait_ge(landed, 16)
                ug = unit["gate"]

                def produce(pe, j, bank):
                    n, t = divmod(j, NT)
                    if t == 0:
                        stream.arrived(pe, ug + n)
                    return token_tile(pe, ug + n, 0, UC, t, bank)

                stage("gate", 4 * NT, produce, lambda eng, j, bank, chain, vector:
                      eng.tensor_tensor(gates[:, j % NT, (j // NT) * UC:(j // NT + 1) * UC], bank,
                                        bias[:, (j // NT) * UC:(j // NT + 1) * UC], ALU.add),
                      on_vector=lambda j: True, uses={ug + n: n * NT + 1 for n in range(4)})
                opened, work = sem("gates_opened"), sem("merge_work")
                with meeting() as block:
                    @block.scalar
                    def _(act):
                        for i in range(2):
                            act.activation(gates[:, :, i * D:(i + 1) * D], gates[:, :, i * D:(i + 1) * D], ACT.Sigmoid)\
                                .then_inc(opened, 1)

                    @block.vector
                    def _(dve):
                        chain = Chain(dve, work)
                        for i, src in enumerate((by_a, by_b)):
                            dve.wait_ge(opened, i + 1)
                            chain(dve.tensor_tensor(src[:, :, :], src[:, :, :], gates[:, :, i * D:(i + 1) * D], ALU.mult))
                        dve.tensor_tensor(by_a[:, :, :], by_a[:, :, :], by_b[:, :, :], ALU.add)
            with ExitStack() as on:
                mT = sb("mergedT", [P, KD, S], on=on)
                turn_into("merge_turn", by_a, KD, mT)
                add_projection("out2", unit["out2"], mT)

        def router(flag, scaled, h_tok, rank):
            NR = NG + NE
            with ExitStack() as on:
                wr = sb("w_router", [P, KD, NR], on=on)
                lg = sb("router_logits", [P, NT, NR], on=on)
                gsel = sb("r_gsel", [P, NT, NG], on=on)
                t4 = sb("r_t4", [P, NT, NG], on=on)
                el = sb("r_el", [P, NT, EPG, NG], on=on)
                pr = sb("r_pr", [P, NT, EPG], on=on)
                left = sb("r_left", [P, NT, EPG], on=on)
                one = sb("r_one", [P, 2, NT, EPG], on=on)
                t8 = sb("r_t8", [P, NT, EPG], on=on)
                s1 = sb("r_s1", [P, 8, NT], on=on)
                dense = sb("r_dense", [P, NT, NG, EPG], on=on)
                mask = sb("r_mask", [P, NT, NG, EPG], on=on)
                late = sb("r_late", [P, NT, NE], on=on)
                late_any = sb("r_late_any", [P, 1], on=on)
                rows = sb("r_rows", [NE, 3, S], on=on)
                row = sb("r_gain", [P, D], on=on)
                landed = sem("router_landed")
                with meeting() as block:
                    @block.sync
                    def _(sp):
                        for lo, w in ((0, a["w_router_group_2"][0]), (NG, a["w_router_expert_2"][0])):
                            n = w.shape[1]
                            sp.dma_start(wr[:, :, lo:lo + n], w.rearrange("(k p) c -> p k c", p=P)).then_inc(landed, 16)
                        sp.dma_start(row[:, :], everywhere(a["ffn_norm_g_2"], D)).then_inc(landed, 16)
                        sp.wait_ge(landed, 48)

                def produce(pe, j, bank):
                    for k in range(KD):
                        mm = pe.matmul(bank[:, 0:NR], hT[:, k, j * P:(j + 1) * P], wr[:, k, :], start=(k == 0),
                                       stop=(k == KD - 1))
                    return mm

                stage("router", NT, produce, lambda eng, j, bank, chain, vector:
                      eng.tensor_tensor(lg[:, j, :], bank[:, 0:NR], gains[:, g_at["b_rg"][0]:g_at["b_rg"][0] + NR],
                                        ALU.add), on_vector=lambda j: True)
                work, asked, acted = sem("r_work"), sem("r_asked"), sem("r_acted")
                gl = lg[:, :, 0:NG]
                shape4, shape8 = [P, NT, NG], [P, NT, EPG]
                over = lambda v, shape: v.unsqueeze(2).broadcast_to(shape)
                with meeting() as block:
                    @block.scalar
                    def _(act):
                        act.wait_ge(asked, 1)
                        act.activation(t4[:, :, :], t4[:, :, :], ACT.Exp).then_inc(acted, 1)
                        act.wait_ge(asked, 2)
                        act.activation(pr[:, :, :], pr[:, :, :], ACT.Exp).then_inc(acted, 1)

                    @block.vector
                    def _(dve):
                        chain = Chain(dve, work)

                        def first_max(dst, src, top, desc, shape, scratch, s_top):
                            chain(dve.tensor_reduce(top, src, AX.X, ALU.max))
                            chain(dve.tensor_tensor(dst, src, over(top, shape), ALU.is_equal))
                            chain(dve.tensor_tensor(dst, dst, desc.unsqueeze(1).broadcast_to(shape), ALU.mult))
                            chain(dve.tensor_reduce(s_top, dst, AX.X, ALU.max))
                            chain(dve.tensor_tensor(dst, dst, over(s_top, shape), ALU.is_equal))

                        first_max(gsel[:, :, :], gl, s1[:, 0, :], c_("desc4"), shape4, None, s1[:, 1, :])
                        dve.tensor_tensor(t4[:, :, :], gl, over(s1[:, 0, :], shape4), ALU.subtract).then_inc(asked, 1)
                        for t in range(NT):
                            chain(dve.tensor_tensor(el[:, t], lg[:, t, NG:].rearrange("p (g e) -> p e g", g=NG),
                                                    gsel[:, t, :].unsqueeze(1).broadcast_to([P, EPG, NG]), ALU.mult))
                        chain(dve.tensor_reduce(left[:, :, :], el[:, :, :, :], AX.X, ALU.add))
                        chain(dve.tensor_reduce(s1[:, 2, :], left[:, :, :], AX.X, ALU.max))
                        dve.tensor_tensor(pr[:, :, :], left[:, :, :], over(s1[:, 2, :], shape8), ALU.subtract)\
                            .then_inc(asked, 1)
                        dve.wait_ge(acted, 1)
                        chain(dve.tensor_reduce(s1[:, 3, :], t4[:, :, :], AX.X, ALU.add))
                        dve.wait_ge(acted, 2)
                        chain(dve.tensor_reduce(s1[:, 4, :], pr[:, :, :], AX.X, ALU.add))
                        chain(dve.reciprocal(s1[:, 5, :], s1[:, 4, :]))
                        chain(dve.tensor_tensor(pr[:, :, :], pr[:, :, :], over(s1[:, 5, :], shape8), ALU.mult))
                        first_max(one[:, 0], pr[:, :, :], s1[:, 0, :], c_("desc8"), shape8, None, s1[:, 1, :])
                        chain(dve.tensor_scalar(t8[:, :, :], one[:, 0], -2.0, None, ALU.mult))
                        chain(dve.tensor_tensor(left[:, :, :], pr[:, :, :], t8[:, :, :], ALU.add))
                        first_max(one[:, 1], left[:, :, :], s1[:, 2, :], c_("desc8"), shape8, None, s1[:, 1, :])
                        chain(dve.tensor_tensor(s1[:, 4, :], s1[:, 0, :], s1[:, 2, :], ALU.add))
                        chain(dve.tensor_tensor(s1[:, 4, :], s1[:, 4, :], s1[:, 3, :], ALU.mult))
                        chain(dve.reciprocal(s1[:, 5, :], s1[:, 4, :]))
                        chain(dve.tensor_tensor(one[:, 0], one[:, 0], one[:, 1], ALU.add))
                        for t in range(NT):
                            chain(dve.tensor_tensor(mask[:, t], one[:, 0, t, :].unsqueeze(1).broadcast_to([P, NG, EPG]),
                                              gsel[:, t, :].unsqueeze(2).broadcast_to([P, NG, EPG]), ALU.mult))
                        chain(dve.tensor_tensor(one[:, 0], one[:, 0], pr[:, :, :], ALU.mult))
                        chain(dve.tensor_tensor(one[:, 0], one[:, 0], over(s1[:, 5, :], shape8), ALU.mult))
                        for t in range(NT):
                            dve.tensor_tensor(dense[:, t], one[:, 0, t, :].unsqueeze(1).broadcast_to([P, NG, EPG]),
                                              gsel[:, t, :].unsqueeze(2).broadcast_to([P, NG, EPG]), ALU.mult)

                flat = lambda v, t: v[:, t].rearrange("p g e -> p (g e)")
                counted, ranked, turned, split, taken, stored, work2 = \
                    (sem("r_" + n) for n in ("counted", "ranked", "turned", "split", "taken", "rows_stored", "work2"))
                before = c_("strict_incl")[:, 0:P]
                with meeting() as block:
                    @block.tensor
                    def _(pe):
                        pe.matmul(ps[:, 0, 0:NE], before, flat(mask, 0), start=True, stop=True)
                        pe.matmul(ps[:, 0, NE:2 * NE], c_("ones"), flat(mask, 0), start=True, stop=False)
                        pe.matmul(ps[:, 0, NE:2 * NE], before, flat(mask, 1), start=False, stop=True)\
                            .then_inc(counted, 1)
                        pe.wait_ge(ranked, 3)
                        for n, src in enumerate((rank[:, :, :], dense[:, :].rearrange("p t g e -> p t (g e)"), late[:, :, :])):
                            for t in range(NT):
                                mm = pe.transpose(ps[0:NE, 1 + n, t * P:(t + 1) * P], src[:, t], ident)
                            mm.then_inc(turned, 1)
                        pe.wait_ge(ranked, 4)
                        pe.matmul(ps[0:1, 4, 0:1], c_("ones")[:, 0:1], late_any[:, :], start=True, stop=True)\
                            .then_inc(turned, 1)

                    @block.scalar
                    def _(act):
                        act.wait_ge(split, 1)
                        act.activation(h_tok[0][:, :, :], scaled[:, :, :], ACT.Copy).then_inc(split, 1)

                    @block.vector
                    def _(dve):
                        chain = Chain(dve, work2)
                        dve.wait_ge(counted, 1)
                        r_ = rank[:, :, :].rearrange("p t e -> p (t e)")
                        m_ = mask[:, :].rearrange("p t g e -> p (t g e)")
                        d_ = dense[:, :].rearrange("p t g e -> p (t g e)")
                        l_ = late[:, :, :].rearrange("p t e -> p (t e)")
                        chain(dve.tensor_scalar(r_, ps[:, 0, 0:2 * NE], -FAR, None, ALU.add))
                        chain(dve.tensor_scalar(l_, r_, SLOTS - FAR, None, ALU.is_ge))
                        chain(dve.tensor_tensor(r_, r_, m_, ALU.mult))
                        dve.tensor_scalar(r_, r_, FAR, None, ALU.add).then_inc(ranked, 1)
                        dve.tensor_tensor(l_, l_, d_, ALU.mult).then_inc(ranked, 1)
                        dve.wait_ge(ranked, 2)
                        dve.tensor_reduce(late_any[:, :], l_, AX.X, ALU.max).then_inc(ranked, 1)
                        dve.wait_ge(ranked, 3)
                        dve.tensor_scalar(late_any[:, :], late_any[:, :], 0.0, None, ALU.is_gt).then_inc(ranked, 1)
                        dve.tensor_tensor(scaled[:, :, :], scaled[:, :, :],
                                          row[:, :].unsqueeze(1).broadcast_to([P, NT, D]), ALU.mult).then_inc(split, 1)
                        for n in range(3):
                            dve.wait_ge(turned, n + 1)
                            dve.tensor_copy(rows[:, n, :], ps[0:NE, 1 + n, 0:S]).then_inc(taken, 1)
                        dve.wait_ge(turned, 4)
                        dve.tensor_copy(flag[:, :], ps[0:1, 4, 0:1])
                        dve.wait_ge(split, 2)
                        dve.tensor_tensor(h_tok[1][:, :, :], scaled[:, :, :], h_tok[0][:, :, :].bitcast(F32), ALU.subtract)

                    @block.sync
                    def _(sp):
                        sp.wait_ge(taken, 3)
                        sp.dma_start(gate_row, rows[:, :, :]).then_inc(stored, 16)
                        sp.wait_ge(stored, 16)

        def experts_stage(h_tok, rank_col):
            u0 = unit["moe"]
            assert u0 % RING == 0
            body = 4
            trips = NE // body
            pieces = 6
            SPLIT = 4
            assert (body * pieces) % SPLIT == 0
            views = [a["w_exp_gate_2"][0].rearrange("(i b) (k p) c -> i b p k c", b=body, p=P),
                     a["w_exp_up_2"][0].rearrange("(i b) (k p) c -> i b p k c", b=body, p=P),
                     a["w_exp_down_2"][0].rearrange("(i b) (k p) c -> i b p k c", b=body, p=P)]
            rows_v = gate_row.rearrange("(i b) r s -> i b (r s)", b=body)
            nm = DE // P
            with ExitStack() as on:
                def two(name, shape):
                    return [sb(f"moe_{name}_{part}", shape, F32R, on=on) for part in ("hi", "lo")]

                w_split = two("w", [P, SPLIT, KD * UC // 2])
                h_sel = two("h", [P, KD, P])
                hid_T = two("hidT", [P, nm, P])
                y = two("y", [P, D])
                sel = sb("moe_sel", [P, NT, P], F32R, on=on)
                sel_T = sb("moe_selT", [P, 2, S], F32R, on=on)
                rows = sb("moe_rows", [P, 2, 2, S], on=on)
                gated = sb("moe_gated", [P, S], on=on)
                slot_gate = sb("moe_slot_gate", [P, 2], on=on)
                silu = sb("moe_silu", [P, DE], on=on)
                hid = sb("moe_hid", [P, DE], on=on)
                acc = lambda t, h: ps[:, 4 + 2 * t + h]
                flat = lambda v: v[:, :, :].rearrange("p c s -> p (c s)")
                wide = ps[:, 0:2].rearrange("p b c -> p (b c)")
                wide_y = ps[:, 2:4].rearrange("p b c -> p (b c)")

                def piece_slot(buf, j):
                    kc = 2 if j % pieces >= 4 else 4
                    return buf[:, j % SPLIT, :].rearrange("p (k c) -> p k c", k=kc)

                def raw_piece(j):
                    kc = 2 if j % pieces >= 4 else 4
                    return stream.view(u0 + j // 2)[:, (j % 2) * kc:(j % 2 + 1) * kc, :]

                def nth(i, per, n):
                    return i * per + n

                with meeting() as block:
                    @block.scalar
                    def _(act):
                        for half in range(2):
                            act.activation(y[0][:, half * UC:(half + 1) * UC], c_("noughts"), ACT.Copy)
                            act.activation(y[1][:, half * UC:(half + 1) * UC], c_("noughts"), ACT.Copy)
                        act.activation(sel_T[:, 1, :], c_("noughts")[:, 0:S], ACT.Copy)

                names = ("selected", "gathered", "h_hi", "h_lo", "used", "opened", "prepared", "hidden",
                         "turned", "hid_hi", "hid_lo", "w_hi", "w_lo", "y_hi", "y_lo", "closed")
                (selected, gathered, h_hi, h_lo, used, opened, prepared, hidden, turned, hid_hi, hid_lo, w_hi,
                 w_lo, y_hi, y_lo, closed) = (sem("moe_" + s) for s in names)
                rows_in = [sem("moe_rows_in0"), sem("moe_rows_in1")]

                with meeting() as block:
                    @block.tensor
                    def _(pe):
                        def gather(i, b):
                            pe.wait_ge(selected, nth(i, body, b + 1))
                            for c in range(KD):
                                dst = ps[:, c // 4, (c % 4) * P:(c % 4 + 1) * P]
                                for t in range(NT):
                                    for part in range(2):
                                        mm = pe.matmul(dst, h_tok[part][:, t, c * P:(c + 1) * P], sel[:, t, :],
                                                       start=(t == 0 and part == 0), stop=(t == NT - 1 and part == 1))
                            mm.then_inc(gathered, 1)

                        def scatter(i, n):
                            pe.wait_ge(y_lo, nth(i, body, n))
                            pe.wait_ge(y_hi, nth(i, body, n))
                            for t in range(NT):
                                for h in range(2):
                                    for part in range(2):
                                        mm = pe.matmul(acc(t, h), sel_T[:, (n + 1) % 2, t * P:(t + 1) * P],
                                                       y[part][:, h * UC:(h + 1) * UC], start=False, stop=False,
                                                       skip_group_check=True)
                            return mm

                        def product(i, b, kind):
                            for half in range(2):
                                j = b * pieces + 2 * kind + half
                                w = [piece_slot(p, j) for p in w_split]
                                pe.wait_ge(w_lo, nth(i, body * pieces, j + 1))
                                for k in range(4):
                                    c = 4 * half + k
                                    mm = three(pe, ps[:, kind], [p[:, c, :] for p in h_sel], [p[:, k, :] for p in w],
                                               start=(c == 0), stop=(c == KD - 1))
                                mm.then_inc(used, 1)

                        def expert(i, b, last=False):
                            pe.wait_ge(h_lo, nth(i, body, b + 1))
                            product(i, b, 0)
                            product(i, b, 1)
                            scatter(i, b)
                            pe.wait_ge(hidden, nth(i, body, b + 1))
                            for m in range(nm):
                                mm = pe.transpose(ps[:, 2, m * P:(m + 1) * P], hid[:, m * P:(m + 1) * P], ident)
                            mm.then_inc(turned, 1)
                            if not last:
                                gather(i, b + 1)
                            pe.wait_ge(hid_lo, nth(i, body, b + 1))
                            for half in range(2):
                                j = b * pieces + 4 + half
                                w = [piece_slot(p, j) for p in w_split]
                                pe.wait_ge(w_lo, nth(i, body * pieces, j + 1))
                                for h in range(2):
                                    for k in range(2):
                                        f = 2 * half + k
                                        mm = three(pe, ps[:, 2 + h], [p[:, f, :] for p in hid_T],
                                                   [p[:, k, h * UC:(h + 1) * UC] for p in w],
                                                   start=(f == 0), stop=(f == nm - 1))
                                mm.then_inc(used, 1)

                        for t in range(NT):
                            for h in range(2):
                                pe.matmul(acc(t, h), ident, x[:, t, h * UC:(h + 1) * UC], start=True, stop=False)
                        gather(0, 0)
                        with pe.Fori(0, trips - 1) as i:
                            for b in range(body):
                                expert(i, b)
                        for b in range(body):
                            expert(trips - 1, b, last=b == body - 1)
                        scatter(trips - 1, body)
                        close_sums(pe).then_inc(closed, 1)

                    @block.scalar
                    def _(act):
                        def split(i, j):
                            u = u0 + j // 2
                            if j % 2 == 0:
                                trip_loads = 3 * body // RING
                                act.wait_ge(stream.sems[u % RING],
                                            i * (16 * trip_loads) + (16 * (j // 2 // RING) + stream.need[u0 + u % RING]))
                            if j >= SPLIT:
                                act.wait_ge(used, nth(i, body * pieces, j + 1 - SPLIT))
                            act.activation(piece_slot(w_split[0], j % (body * pieces)), raw_piece(j % (body * pieces)),
                                           ACT.Copy).then_inc(w_hi, 1)

                        def tokens_split(i, b):
                            act.wait_ge(gathered, nth(i, body, b + 1))
                            act.activation(flat(h_sel[0]), wide, ACT.Copy).then_inc(h_hi, 1)

                        def expert(i, b, last=False):
                            j = b * pieces
                            after = (lambda n: None) if last else (lambda n: split(i, j + SPLIT + n))
                            split(i, j + SPLIT)
                            act.wait_ge(used, nth(i, body * pieces, j + 2))
                            act.wait_ge(hidden, nth(i, body, b))
                            act.activation(silu[:, :], ps[:, 0], ACT.Silu).then_inc(opened, 1)
                            split(i, j + SPLIT + 1)
                            after(2)
                            act.wait_ge(turned, nth(i, body, b + 1))
                            act.activation(flat(hid_T[0]), ps[:, 2], ACT.Copy).then_inc(hid_hi, 1)
                            if not last:
                                tokens_split(i, b + 1)
                            after(3)
                            after(4)
                            act.wait_ge(used, nth(i, body * pieces, j + 6))
                            act.activation(y[0][:, :], wide_y, ACT.Copy).then_inc(y_hi, 1)
                            after(5)

                        for j in range(SPLIT):
                            split(0, j)
                        tokens_split(0, 0)
                        with act.Fori(0, trips - 1) as i:
                            for b in range(body):
                                expert(i, b)
                        for b in range(body):
                            expert(trips - 1, b, last=b == body - 1)

                    @block.vector
                    def _(dve):
                        def split(i, j):
                            dve.wait_ge(w_hi, nth(i, body * pieces, j + 1))
                            jj = j % (body * pieces)
                            dve.tensor_tensor(piece_slot(w_split[1], jj), raw_piece(jj),
                                              piece_slot(w_split[0], jj).bitcast(F32), ALU.subtract).then_inc(w_lo, 1)

                        def tokens_split(i, b):
                            dve.wait_ge(h_hi, nth(i, body, b + 1))
                            dve.tensor_tensor(flat(h_sel[1]), wide, flat(h_sel[0]).bitcast(F32), ALU.subtract)\
                                .then_inc(h_lo, 1)

                        def select(i, b):
                            if b:
                                dve.wait_ge(gathered, nth(i, body, b))
                            ranks = rank_col[:, :, bass.ds(i * body + b, 1)]
                            for t in range(NT):
                                last = dve.tensor_scalar(sel[:, t, :], c_("slot_row"), ranks[:, t, :], None, ALU.is_equal)
                            last.then_inc(selected, 1)

                        def prepare(i, b):
                            dve.wait_ge(rows_in[b % 2], nth(i, 16 * body // 2, 16 * (b // 2 + 1)))
                            dve.wait_ge(turned, nth(i, body, b))
                            slot = c_("slot_col")
                            dve.tensor_scalar(sel_T[:, b % 2, :], rows[:, b % 2, 0, :], slot, None, ALU.is_equal)
                            dve.scalar_tensor_tensor(gated[:, :], rows[:, b % 2, 0, :], slot, rows[:, b % 2, 1, :],
                                                     ALU.is_equal, ALU.mult, accum_out=slot_gate[:, b % 2:b % 2 + 1])\
                                .then_inc(prepared, 1)

                        def expert(i, b, last=False):
                            j = b * pieces
                            after = (lambda n: None) if last else (lambda n: split(i, j + SPLIT + n))
                            prepare(i, b)
                            if not last:
                                select(i, b + 1)
                            split(i, j + SPLIT)
                            split(i, j + SPLIT + 1)
                            after(2)
                            dve.wait_ge(opened, nth(i, body, b + 1))
                            dve.wait_ge(prepared, nth(i, body, b + 1))
                            dve.wait_ge(used, nth(i, body * pieces, j + 4))
                            dve.scalar_tensor_tensor(hid[:, :], silu[:, :], slot_gate[:, b % 2:b % 2 + 1], ps[:, 1],
                                                     ALU.mult, ALU.mult).then_inc(hidden, 1)
                            dve.wait_ge(hid_hi, nth(i, body, b + 1))
                            dve.tensor_tensor(flat(hid_T[1]), ps[:, 2], flat(hid_T[0]).bitcast(F32), ALU.subtract)\
                                .then_inc(hid_lo, 1)
                            if not last:
                                tokens_split(i, b + 1)
                            after(3)
                            after(4)
                            dve.wait_ge(y_hi, nth(i, body, b + 1))
                            dve.tensor_tensor(y[1][:, :], wide_y, y[0][:, :].bitcast(F32), ALU.subtract)\
                                .then_inc(y_lo, 1)
                            after(5)

                        select(0, 0)
                        for j in range(SPLIT):
                            split(0, j)
                        tokens_split(0, 0)
                        with dve.Fori(0, trips - 1) as i:
                            for b in range(body):
                                expert(i, b)
                        for b in range(body):
                            expert(trips - 1, b, last=b == body - 1)
                        dve.wait_ge(closed, 1)
                        for t in range(NT):
                            for h in range(2):
                                dve.tensor_copy(x[:, t, h * UC:(h + 1) * UC], acc(t, h))

                    @block.sync
                    def _(sp):
                        stream.prefetch(sp, u0)

                        def load(n, i):
                            j, m = (i, n - RING) if n >= RING else (i - 1, n - RING + 3 * body)
                            sp.wait_ge(w_lo, j * (body * pieces) + 2 * (m + 1))
                            sp.dma_start(stream.view(u0 + n), views[n % 3][i, n // 3])\
                                .then_inc(stream.sems[n % RING], 16)

                        def load_rows(b, i):
                            if b >= 2:
                                sp.wait_ge(prepared, i * body + (b - 1))
                            elif not isinstance(i, int) or i > 0:
                                sp.wait_ge(prepared, (i - 1) * body + (b - 1 + body))
                            sp.dma_start(rows[:, b % 2, :, :].rearrange("p r s -> p (r s)"),
                                         rows_v[i, b][0:2 * S].unsqueeze(0).broadcast_to([P, 2 * S]))\
                                .then_inc(rows_in[b % 2], 16)

                        load_rows(0, 0)
                        load_rows(1, 0)

                        def turn(i, last=False):
                            for b in range(body):
                                for n in range(RING + 3 * b, RING + 3 * b + 3):
                                    if n < 3 * body:
                                        load(n, i)
                                    elif not last:
                                        load(n - 3 * body, i + 1)
                                if b + 2 < body:
                                    load_rows(b + 2, i)
                                elif not last:
                                    load_rows(b + 2 - body, i + 1)

                        with sp.Fori(0, trips - 1) as i:
                            turn(i)
                        turn(trips - 1, last=True)

        def late_experts(flag):
            body = 4
            trips = NE // body
            per = 3 * body // RING
            views = [a["w_exp_gate_2"][0].rearrange("(i b) (k p) c -> i b p k c", b=body, p=P),
                     a["w_exp_up_2"][0].rearrange("(i b) (k p) c -> i b p k c", b=body, p=P),
                     a["w_exp_down_2"][0].rearrange("(i b) (k p) c -> i b p k c", b=body, p=P)]
            grown, opened, hid_ready, downs, weighed, rows_landed = \
                (sem("late_" + s) for s in ("grown", "opened", "hidden", "downs", "weighed", "rows_landed"))
            landed = [sem(f"late_landed_{s}") for s in range(RING)]
            nm = DE // P
            nb = nm // 2

            def unit_view(n):
                kc = 4 if n % 3 == 2 else KD
                return slots[:, n % RING, :].rearrange("p (k c) -> p k c", k=kc)

            with ExitStack() as on:
                gates = sb("late_gates", [P, NE, S], on=on)
                hid = sb("late_hid", [P, nm, S], on=on)
                act_ = sb("late_act", [P, nm, S], on=on)
                both = lambda buf, b: buf[:, 2 * b:2 * b + 2, :].rearrange("p m s -> p (m s)")

                def any_late(eng):
                    return eng.value_load(flag[0:1, 0:1], min_val=0, max_val=P) > 0

                with meeting() as block:
                    @block.tensor
                    def _(pe):
                        with pe.If(any_late(pe)):
                            for t in range(NT):
                                for h in range(2):
                                    pe.matmul(ps[:, 4 + 2 * t + h], ident, x[:, t, h * UC:(h + 1) * UC],
                                              start=True, stop=False)
                            with pe.Fori(0, trips) as i:
                                for b in range(body):
                                    for kind in range(2):
                                        n = 3 * b + kind
                                        w = unit_view(n)
                                        pe.wait_ge(landed[n % RING], i * (16 * per) + 16 * (n // RING + 1))
                                        for m in range(nm):
                                            dst = ps[:, 2 * kind + m // 2, (m % 2) * S:(m % 2 + 1) * S]
                                            for k in range(KD):
                                                mm = pe.matmul(dst, w[:, k, m * P:(m + 1) * P], hT[:, k, :],
                                                               start=(k == 0), stop=(k == KD - 1))
                                            if m % 2:
                                                mm.then_inc(grown, 1)
                                    n = 3 * b + 2
                                    w = unit_view(n)
                                    pe.wait_ge(landed[n % RING], i * (16 * per) + 16 * (n // RING + 1))
                                    for f in range(nm):
                                        if f % 2 == 0:
                                            pe.wait_ge(hid_ready, i * (body * nb) + (b * nb + f // 2 + 1))
                                        for t in range(NT):
                                            for h in range(2):
                                                mm = pe.matmul(ps[:, 4 + 2 * t + h], hid[:, f, t * P:(t + 1) * P],
                                                               w[:, f, h * UC:(h + 1) * UC], start=False, stop=False,
                                                               skip_group_check=True)
                                    mm.then_inc(downs, 1)
                            close_sums(pe).then_inc(downs, 1)

                    @block.scalar
                    def _(act):
                        with act.If(any_late(act)):
                            with act.Fori(0, trips) as i:
                                for b in range(body):
                                    for m in range(nb):
                                        act.wait_ge(grown, i * (body * 2 * nb) + (b * 2 * nb + m + 1))
                                        act.activation(both(act_, m), ps[:, m], ACT.Silu).then_inc(opened, 1)

                    @block.vector
                    def _(dve):
                        with dve.If(any_late(dve)):
                            dve.wait_ge(rows_landed, 16)
                            with dve.Fori(0, trips) as i:
                                rows_i = gates[:, bass.ds(i * body, body), :]
                                for b in range(body):
                                    for m in range(nb):
                                        dve.wait_ge(opened, i * (body * nb) + (b * nb + m + 1))
                                        dve.tensor_tensor(act_[:, 2 * m:2 * m + 2, :], act_[:, 2 * m:2 * m + 2, :],
                                                          rows_i[:, b, :].unsqueeze(1).broadcast_to([P, 2, S]),
                                                          ALU.mult).then_inc(weighed, 1)
                                        dve.wait_ge(weighed, i * (body * nb) + (b * nb + m + 1))
                                        dve.wait_ge(grown, i * (body * 2 * nb) + (b * 2 * nb + nb + m + 1))
                                        dve.tensor_tensor(both(hid, m), both(act_, m), ps[:, 2 + m], ALU.mult)\
                                            .then_inc(hid_ready, 1)
                            dve.wait_ge(downs, body * trips + 1)
                            for t in range(NT):
                                for h in range(2):
                                    dve.tensor_copy(x[:, t, h * UC:(h + 1) * UC], ps[:, 4 + 2 * t + h])

                    @block.sync
                    def _(sp):
                        def load(n, i):
                            m = n - RING
                            if m < 0 and isinstance(i, int):
                                pass
                            else:
                                b, kind = divmod(m % (3 * body), 3)
                                j = i if m >= 0 else i - 1
                                if kind == 2:
                                    sp.wait_ge(downs, j * body + (b + 1))
                                else:
                                    sp.wait_ge(grown, j * (body * 2 * nb) + (b * 2 * nb + (kind + 1) * nb))
                            sp.dma_start(unit_view(n), views[n % 3][i, n // 3]).then_inc(landed[n % RING], 16)

                        with sp.If(any_late(sp)):
                            sp.dma_start(gates[:, :, :], bass.AP(gate_row.tensor, 2 * S, [[0, P], [3 * S, NE], [1, S]]))\
                                .then_inc(rows_landed, 16)
                            for n in range(RING):
                                load(n, 0)
                            with sp.Fori(0, trips - 1) as i:
                                for n in range(RING, 3 * body):
                                    load(n, i)
                                for n in range(RING):
                                    load(n, i + 1)
                            for n in range(RING, 3 * body):
                                load(n, trips - 1)

        def final_norm():
            with ExitStack() as on:
                row = sb("final_gain", [P, D], on=on)
                sq = sb("final_sq", [P, D], on=on)
                st = sb("final_st", [P, 4, NT], on=on)
                y = sb("final_y", [P, NT, D], on=on)
                landed, sums, scaled, rooted, done = (sem("final_" + s) for s in ("landed", "sums", "scaled", "rooted", "done"))
                stored = sem("stored")
                with meeting() as block:
                    @block.sync
                    def _(sp):
                        sp.dma_start(row[:, :], everywhere(a["final_norm_g_2"], D)).then_inc(landed, 16)
                        for t in range(NT):
                            sp.wait_ge(done, t + 1)
                            sp.dma_start(out[0, t * P:(t + 1) * P, :], y[:, t, :]).then_inc(stored, 16)
                        sp.wait_ge(stored, 16 * NT)

                    @block.scalar
                    def _(act):
                        for t in range(NT):
                            if t:
                                act.wait_ge(sums, t)
                            act.activation(sq[:, :], x[:, t, :], ACT.Square, accum_out=st[:, 0, t:t + 1])\
                                .then_inc(sums, 1)
                        act.wait_ge(scaled, 1)
                        act.activation(st[:, 2, :], st[:, 1, :], ACT.Sqrt).then_inc(rooted, 1)

                    @block.vector
                    def _(dve):
                        dve.wait_ge(sums, NT)
                        dve.tensor_scalar(st[:, 1, :], st[:, 0, :], 1.0 / D, EPS, ALU.mult, ALU.add).then_inc(scaled, 1)
                        dve.wait_ge(rooted, 1)
                        dve.reciprocal(st[:, 3, :], st[:, 2, :]).then_inc(scaled, 1)
                        dve.wait_ge(scaled, 2)
                        dve.wait_ge(landed, 16)
                        for t in range(NT):
                            dve.scalar_tensor_tensor(y[:, t, :], x[:, t, :], st[:, 3, t:t + 1], row[:, :],
                                                     ALU.mult, ALU.mult).then_inc(done, 1)

        with ExitStack() as on:
            mem = sb("mem", [P, NT, D], on=on)
            with ExitStack() as on2:
                rows = sb("rows", [P, 3, P], on=on2)
                table = sb("table", [NBK + 1, NH], on=on2)
                hb = sb("dist_rows", [NH, 512], on=on2)
                setup(mem, rows, table, hb)
            norm("mem", mem, [("mem_norm", 0, hT)])
            memory(hT)
        norm("n0", x, [("mix_norm", 0, hT)])
        conv_layer()
        norm("n1", x, [("mlp_norm", 0, hT)])
        mlp(0)
        with ExitStack() as on:
            sh = shared_buffers(on)
            with ExitStack() as on2:
                hkv = sb("hkv", [P, KD, S], on=on2)
                norm("n2", x, [("kv_norm", 0, hkv), ("mix_norm", KD, hT)])
                shared_kv(sh, hkv)
            nsa_layer(sh)
        norm("n3", x, [("mlp_norm", KD, hT)])
        mlp(1)
        first.close()
        with ExitStack() as on:
            by_a = sb("by_a", [P, NT, D], on=on)
            norm("n4", x, [("attn_norm", 0, hT)])
            with ExitStack() as on2:
                rwkv(by_a)
                dump("ya", by_a)
                yaT = sb("yaT", [P, RC, S], on=on2)
                turn_into("ya_turn", by_a, RC, yaT)
                project("up_rwkv", unit["up_rwkv"], yaT, by_a)
            by_b = sb("by_b", [P, NT, D], on=on)
            with ExitStack() as on2:
                yb = sb("yb", [P, NT, SW], on=on2)
                ssd(yb)
                dump("yb", yb)
                ybT = sb("ybT", [P, SW // P, S], on=on2)
                turn_into("yb_turn", yb, SW // P, ybT, scale=lambda j: col("ssd_norm", j))
                project("up_ssd", unit["up_ssd"], ybT, by_b, parts=2)
            merge(by_a, by_b)
            dump("x", x)
        with ExitStack() as on:
            flag = sb("late_flag", [1, 1], I32, on=on)
            with ExitStack() as on2:
                rank = sb("rank", [P, NT, NE], on=on2)
                h_tok = [sb("h_tok_" + part, [P, NT, D], F32R, on=on2) for part in ("hi", "lo")]
                with ExitStack() as on3:
                    scaled = sb("n5_scaled", [P, NT, D], on=on3)
                    norm("n5", x, [("ffn_norm", 0, hT)], scaled)
                    router(flag, scaled, h_tok, rank)
                experts_stage(h_tok, rank)
            late_experts(flag)
        final_norm()


NAMES = ("x mem mix_norm a_w_in a_conv_w b_w_in b_q_gain kv_norm w_kv_shared k_gain cmp_pos cmp_w1 cmp_w2 rel_bias "
         "mem_norm mem_w_kv mem_q_gain mem_k_gain w_out mlp_norm w_up w_down attn_norm_g_2 w_in_2 b_gate_2 rwkv_mu_2 "
         "rwkv_w0_2 rwkv_w_decay_2 rwkv_a0_2 rwkv_w_a_2 rwkv_w_g_2 rwkv_k_k_2 rwkv_k_a_2 rwkv_r_k_2 rwkv_ln_g_2 "
         "rwkv_ln_b_2 w_up_rwkv_2 ssd_conv_w_2 ssd_conv_b_2 ssd_dt_bias_2 ssd_a_log_2 ssd_d_2 ssd_norm_g_2 w_up_ssd_2 "
         "w_out_2 ffn_norm_g_2 w_router_group_2 b_router_group_2 w_router_expert_2 b_router_expert_2 w_exp_gate_2 "
         "w_exp_up_2 w_exp_down_2 final_norm_g_2").split()


def kernel(**inputs):
    import concourse.bacc as bacc
    from concourse.bass_utils import run_bass_kernel_spmd

    nc = bacc.Bacc("TRN2", target_bir_lowering=False, num_devices=1)
    const, at = constants()
    arrays = {f"in_{n}": np.ascontiguousarray(inputs[n]) for n in NAMES}
    arrays["in_const"] = const
    views = {k[3:]: nc.dram_tensor(k, v.shape, mybir.dt.from_np(v.dtype), kind="ExternalInput").ap()
             for k, v in arrays.items()}
    out = nc.dram_tensor("out_x", (1, S, D), F32, kind="ExternalOutput").ap()
    program(nc, views, out, at)
    r = run_bass_kernel_spmd(nc, [arrays], core_ids=[0])
    return r.results[0]["out_x"]
```

```python
from contextlib import ExitStack, contextmanager

import numpy as np

import concourse.bass as bass
from concourse import mybir

F32 = mybir.dt.float32
F32R = mybir.dt.float32r
BF16 = mybir.dt.bfloat16
I32 = mybir.dt.int32
ALU = mybir.AluOpType
ACT = mybir.ActivationFunctionType
AX = mybir.AxisListType

P = 128
S = 256
NT = S // P
D = 1024
KD = D // P
HD = 64
NEG = -1e30
EPS = 1e-6

CONV_CH = 768
NH = CONV_CH // HD
G = 2
HPG = NH // G
MW = 256
MH = MW // HD
M = 256
FF = 4096
NBK = 32
CMP_L, CMP_S = 32, 16
NC = S // CMP_S - 1
CMP_H = 256

RW = 1024
RH = RW // HD
RC = RW // P
LORA = 64
R_COLS = 3 * RW + 2 * LORA + P
SW = 2048
SH = SW // HD
SG = 4
SN = 128
XBC = SW + 2 * SG * SN
KAPPA = float(np.exp(-0.5))
GN_EPS = 64e-5

NE, NG, EPG, DE = 32, 4, 8, 512
RING = 4
SLOTS = 128
FAR = 1024.0
UC = 512


def bucket_of(dist):
    n = np.maximum(dist, 0)
    nf = np.maximum(n, 1).astype(np.float32)
    large = 16 + (np.log(nf / np.float32(16)) / np.float32(np.log(64.0)) * np.float32(16)).astype(np.int32)
    return np.where(n < 16, n, np.minimum(large, 31))


def constants():
    i = np.arange(P)
    parts = {}
    parts["ident"] = np.eye(P)
    parts["flip"] = np.eye(P)[::-1]
    parts["headones"] = (i[:, None] // HD == i[None, :] // HD)
    parts["strict_incl"] = np.concatenate([i[:, None] < i[None, :], i[:, None] <= i[None, :]], 1)
    level = []
    for b in (1, 2, 4, 8, 16, 32, 64):
        blk = i // b
        lower = (blk[:, None] // 2 == blk[None, :] // 2) & (blk[:, None] % 2 == 1) & (blk[None, :] % 2 == 0)
        level.append(lower.T if b == 1 else lower)
    parts["levels"] = np.concatenate(level, 1)
    y = 255 - np.arange(512)
    hot = np.zeros((P, 512))
    hot[np.where(y >= 0, bucket_of(y), NBK), np.arange(512)] = 1
    parts["hot"] = hot
    parts["headsel"] = np.arange(2)[None, :] == (i // HD)[:, None]
    parts["cmp_rows"] = (i[:, None] + P * np.arange(NT)[None, :]) >= CMP_L - 1
    parts["desc4"] = np.broadcast_to(4.0 - np.arange(4), (P, 4))
    parts["desc8"] = np.broadcast_to(8.0 - np.arange(8), (P, 8))
    parts["ones"] = np.ones((P, P))
    parts["slot_row"] = np.broadcast_to(np.where(i < SLOTS, i, -1), (P, P))
    parts["slot_col"] = np.where(i < SLOTS, i, -1)[:, None]
    parts["noughts"] = np.zeros((P, UC))
    at, n = {}, 0
    for k, v in parts.items():
        at[k] = (n, n + v.shape[1])
        n += v.shape[1]
    return np.concatenate([np.asarray(v, np.float32) for v in parts.values()], 1), at


class Chain:

    def __init__(self, eng, sem):
        self.eng, self.sem, self.n = eng, sem, 0

    def __call__(self, ins):
        self.n += 1
        ins.then_inc(self.sem, 1)
        self.eng.wait_ge(self.sem, self.n)


def three(pe, dst, left, right, start, stop):
    inside = not (start or stop)
    pe.matmul(dst, left[0], right[0], start=start, stop=False, skip_group_check=inside)
    pe.matmul(dst, left[0], right[1], start=False, stop=False, skip_group_check=inside)
    return pe.matmul(dst, left[1], right[0], start=False, stop=stop, skip_group_check=inside)


class Stream:

    def __init__(self, slots, sems):
        self.slots, self.sems = slots, sems
        self.src = []
        self.need = {}
        self.done = {}
        self.issued = 0

    def count(self):
        loads = [0] * RING
        for n, src in enumerate(self.src):
            if src is not None:
                loads[n % RING] += 1
                self.need[n] = 16 * loads[n % RING]

    def view(self, n):
        _, kc, cols = self.src[n]
        return self.slots[:, n % RING, 0:kc * cols].rearrange("p (k c) -> p k c", k=kc)

    def arrived(self, pe, n):
        pe.wait_ge(self.sems[n % RING], self.need[n])
        return self.view(n)

    def load(self, sp, n):
        src, kc, cols = self.src[n]
        before = [u for u in range(n - RING, -1, -RING) if self.src[u] is not None][:1]
        if before and before[0] in self.done:
            sp.wait_ge(*self.done[before[0]])
        sp.dma_start(self.view(n), src).then_inc(self.sems[n % RING], 16)

    def prefetch(self, sp, end):
        while self.issued < min(end + RING, len(self.src)):
            if self.src[self.issued] is not None:
                self.load(sp, self.issued)
            self.issued += 1


def program(nc, a, out, at, dumps=()):
    with ExitStack() as ctx:
        seen = {}

        def sb(name, shape, dt=F32, on=None):
            seen[name] = seen.get(name, 0) + 1
            name = name if seen[name] == 1 else f"{name}_{seen[name]}"
            return (on or ctx).enter_context(nc.sbuf_tensor(name, shape, dt))

        used, cooling = [], []

        def sem(name):
            used.append(nc.alloc_semaphore(name=f"{name}_{len(seen)}_{len(used)}"))
            return used[-1]

        def end_stage():
            for s in cooling:
                nc.release_semaphore(s)
            cooling[:] = used
            for s in used:
                nc.gpsimd.sem_clear(s)
            used.clear()
            stream.done.clear()

        @contextmanager
        def meeting():
            with nc.Block() as block:
                yield block
            end_stage()

        ps = ctx.enter_context(nc.psum_tensor("ps", [P, 8, 512], F32))
        slots = sb("weight_slots", [P, RING, KD * UC])
        n_const = max(e for _, e in at.values())
        const = sb("const", [P, n_const])
        x = sb("x", [P, NT, D])
        hT = sb("hT", [P, KD, S])

        def c_(name):
            lo, hi = at[name]
            return const[:, lo:hi]

        ident = c_("ident")

        def dump(name, t):
            if name in dumps:
                dd = nc.dram_tensor("dump_" + name, list(t.shape), F32, kind="ExternalOutput").ap()
                ds = sem("dump")
                with meeting() as block:
                    @block.sync
                    def _(sp):
                        sp.dma_start(dd, t[tuple(slice(None) for _ in t.shape)]).then_inc(ds, 16)
                        sp.wait_ge(ds, 16)

        stream = Stream(slots, [ctx.enter_context(nc.semaphore(f"weights_landed_{s}")) for s in range(RING)])
        unit = {}

        def kxn(w, r0, rows, c0, cols):
            return (w[r0:r0 + rows, c0:c0 + cols].rearrange("(k p) c -> p k c", p=P), rows // P, cols)

        def plan(name, *views):
            unit[name] = len(stream.src)
            stream.src.extend(views)

        def gap():
            while len(stream.src) % RING:
                stream.src.append(None)

        def columns(w, c0, c1, rows=D):
            return [kxn(w, 0, rows, c, min(UC, c1 - c)) for c in range(c0, c1, UC)]

        def mlp_units(layer):
            v = []
            for j in range(FF // UC):
                v.append(kxn(a["w_up"][layer], 0, D, j * UC, UC))
                v.append(kxn(a["w_down"][layer], j * UC, UC, 0, D))
            return v

        a_w, b_w, w2 = a["a_w_in"][0], a["b_w_in"][0], a["w_in_2"][0]
        Z0 = R_COLS
        X0 = Z0 + SW
        T0 = X0 + XBC
        G0 = T0 + SH
        QG = CONV_CH + 3 * NH
        plan("mem_kv", *[kxn(a["mem_w_kv"][l], 0, D, 0, 2 * MW) for l in range(2)])
        plan("a_in", *columns(a_w, 0, 3 * CONV_CH + MW))
        plan("out0", *columns(a["w_out"][0], 0, D))
        gap()
        plan("mlp0", *mlp_units(0))
        plan("kv", *columns(a["w_kv_shared"], 0, 6 * G * HD))
        plan("cmp1", *[kxn(a["cmp_w1"][i], 0, CMP_L * HD, 0, CMP_H) for i in range(2)])
        plan("b_in", kxn(b_w, 0, D, 0, UC), kxn(b_w, 0, D, UC, QG - UC), kxn(b_w, 0, D, QG, MW))
        plan("out1", *columns(a["w_out"][1], 0, D))
        gap()
        plan("mlp1", *mlp_units(1))
        plan("rwkv", *columns(w2, 0, R_COLS))
        plan("up_rwkv", *columns(a["w_up_rwkv_2"][0], 0, D))
        plan("xbc", *columns(w2, X0, T0))
        plan("dt", kxn(w2, 0, D, T0, SH))
        plan("z", *columns(w2, Z0, X0))
        plan("up_ssd", *[kxn(a["w_up_ssd_2"][0], r * D, D, n * UC, UC) for n in range(2) for r in range(2)])
        plan("gate", *columns(w2, G0, G0 + 2 * D))
        plan("out2", *columns(a["w_out_2"][0], 0, D))
        gap()
        experts = []
        for e in range(NE):
            experts += [kxn(a["w_exp_gate_2"][0, e], 0, D, 0, DE), kxn(a["w_exp_up_2"][0, e], 0, D, 0, DE),
                        kxn(a["w_exp_down_2"][0, e], 0, DE, 0, D)]
        plan("moe", *experts)
        stream.count()

        def stage(name, n_jobs, produce, consume, on_vector=lambda j: j % 2 == 0, uses=(), loads=()):
            full, free_v, free_a = sem(name + "_full"), sem(name + "_free_v"), sem(name + "_free_a")
            chain_v, chain_a = sem(name + "_chain_v"), sem(name + "_chain_a")
            loaded = sem(name + "_loaded")
            n_banks = 8
            bank = lambda j: ps[:, j % n_banks]
            nth = [sum(on_vector(i) == on_vector(j) for i in range(j + 1)) for j in range(n_jobs)]
            with meeting() as block:
                @block.tensor
                def _(pe):
                    for j in range(n_jobs):
                        if j >= n_banks:
                            b = j - n_banks
                            pe.wait_ge(free_v if on_vector(b) else free_a, nth[b])
                        produce(pe, j, bank(j)).then_inc(full, 1)
                    for u, j in dict(uses).items():
                        stream.done[u] = (full, j + 1)

                @block.vector
                def _(dve):
                    chain = Chain(dve, chain_v)
                    for j in range(n_jobs):
                        if on_vector(j):
                            dve.wait_ge(full, j + 1)
                            consume(dve, j, bank(j), chain, True).then_inc(free_v, 1)

                @block.scalar
                def _(act):
                    chain = Chain(act, chain_a)
                    for j in range(n_jobs):
                        if not on_vector(j):
                            act.wait_ge(full, j + 1)
                            consume(act, j, bank(j), chain, False).then_inc(free_a, 1)

                @block.sync
                def _(sp):
                    for dst, src in loads:
                        sp.dma_start(dst, src).then_inc(loaded, 16)
                    if uses:
                        stream.prefetch(sp, max(dict(uses)) + 1)
                    if loads:
                        sp.wait_ge(loaded, 16 * len(loads))

        def split_stage(name, units, consume, src, pair=None, depth=3, on_vector=lambda j: j % 2 == 0, loads=(),
                        act_then=None, dve_then=None):
            full, used, free_v, free_a = (sem(f"{name}_{s}") for s in ("full", "used", "free_v", "free_a"))
            w_hi, w_lo, h_hi, h_lo = (sem(f"{name}_{s}") for s in ("w_hi", "w_lo", "h_hi", "h_lo"))
            chain_v, chain_a, loaded = sem(name + "_chain_v"), sem(name + "_chain_a"), sem(name + "_loaded")
            followed = sem(name + "_followed")
            half_chunks = KD // 2
            n_banks = 8
            bank = lambda j: ps[:, j % n_banks]
            nth = lambda j: sum(on_vector(i) == on_vector(j) for i in range(j + 1))
            n_pieces = 2 * len(units)
            groups = sorted({first + h * half_chunks for _, first, _ in units for h in range(2)})
            whole = [], []
            n_full = n_used = 0
            for _, _, products in units:
                n_used += 1
                whole[1].append((used, n_used))
                done = [p[0] for p in products if p[6]]
                whole[0].append(done)
                n_full += len(done)
                n_used += not done
                whole[1].append((full, n_full) if done else (used, n_used))
            with ExitStack() as on:
                own = pair is None
                if own:
                    pair = [sb(f"{name}_h_{part}", [P, len(groups) * half_chunks, S], F32R, on=on)
                            for part in ("hi", "lo")]
                w_split = [sb(f"{name}_w_{part}", [P, depth, half_chunks * UC], F32R, on=on) for part in ("hi", "lo")]

                def piece(n):
                    u = units[n // 2][0]
                    raw = stream.view(u)[:, (n % 2) * half_chunks:(n % 2 + 1) * half_chunks, :]
                    cols = stream.src[u][2]
                    return raw, [p[:, n % depth, 0:half_chunks * cols].rearrange("p (k c) -> p k c", c=cols)
                                 for p in w_split]

                def steps(n):
                    return [slice(0, half_chunks // 2), slice(half_chunks // 2, half_chunks)] if n == 0 \
                        else [slice(0, half_chunks)]

                def programme(split_w, split_h, empty, later=None):
                    for n in range(min(depth, n_pieces)):
                        for s in steps(n):
                            if own and n < len(groups):
                                split_h(n, s)
                            split_w(n, s)
                    if own:
                        for g in range(depth, len(groups)):
                            split_h(g, slice(0, half_chunks))
                    for n in range(len(units)):
                        for p in (2 * n + depth, 2 * n + 1 + depth):
                            if p < n_pieces:
                                split_w(p, slice(0, half_chunks))
                        for j in whole[0][n]:
                            empty(j)
                        if later:
                            for j in whole[0][n - 1] if n else ():
                                later(j)
                    if later:
                        for j in whole[0][-1]:
                            later(j)

                with meeting() as block:
                    @block.tensor
                    def _(pe):
                        for n, (u, first_chunk, products) in enumerate(units):
                            for half in range(2):
                                _, w = piece(2 * n + half)
                                for step, (job, kind, c0, width, t, first, last) in \
                                        [(s, p) for s in steps(2 * n + half) for p in products]:
                                    if job == products[0][0]:
                                        whole_piece = step.stop == half_chunks
                                        pe.wait_ge(w_lo, 2 * n + half + 2 if whole_piece else 1)
                                        if own:
                                            g = groups.index(first_chunk + half * half_chunks)
                                            pe.wait_ge(h_lo, g + 2 if whole_piece else 1)
                                    if half == 0 and first and job >= n_banks:
                                        b = job - n_banks
                                        pe.wait_ge(free_v if on_vector(b) else free_a, nth(b))
                                    for k in range(step.start, step.stop):
                                        c = first_chunk + half * half_chunks + k
                                        begin = first and half == 0 and k == 0
                                        end = last and half == 1 and k == half_chunks - 1
                                        wk = [p[:, k, c0:c0 + width] for p in w]
                                        if kind == "feature":
                                            mm = three(pe, bank(job)[:, 0:S], wk, [p[:, c, :] for p in pair],
                                                       start=begin, stop=end)
                                        else:
                                            mm = three(pe, bank(job)[:, 0:width],
                                                       [p[:, c, t * P:(t + 1) * P] for p in pair], wk,
                                                       start=begin, stop=end)
                                    if last and half == 1:
                                        mm.then_inc(full, 1)
                                if half == 0 or not products[-1][6]:
                                    mm.then_inc(used, 1)

                    @block.scalar
                    def _(act):
                        chain = Chain(act, chain_a)

                        def split_w(n, s):
                            u = units[n // 2][0]
                            act.wait_ge(stream.sems[u % RING], stream.need[u])
                            if n >= depth:
                                act.wait_ge(*whole[1][n - depth])
                            raw, w = piece(n)
                            act.activation(w[0][:, s, :], raw[:, s, :], ACT.Copy).then_inc(w_hi, 1)

                        def split_h(g, s):
                            c = slice(groups[g] + s.start, groups[g] + s.stop)
                            act.activation(pair[0][:, c, :], src[:, c, :], ACT.Copy).then_inc(h_hi, 1)

                        def empty(j):
                            if not on_vector(j):
                                act.wait_ge(full, j + 1)
                                consume(act, j, bank(j), chain, False).then_inc(free_a, 1)
                            if act_then:
                                act.wait_ge(free_v, nth(j))
                                act_then(act, j).then_inc(followed, 1)

                        programme(split_w, split_h, empty)

                    @block.vector
                    def _(dve):
                        chain = Chain(dve, chain_v)

                        def split_w(n, s):
                            dve.wait_ge(w_hi, n + 2 if s.stop == half_chunks else 1)
                            raw, w = piece(n)
                            dve.tensor_tensor(w[1][:, s, :], raw[:, s, :], w[0][:, s, :].bitcast(F32), ALU.subtract)\
                                .then_inc(w_lo, 1)

                        def split_h(g, s):
                            dve.wait_ge(h_hi, g + 2 if s.stop == half_chunks else 1)
                            c = slice(groups[g] + s.start, groups[g] + s.stop)
                            dve.tensor_tensor(pair[1][:, c, :], src[:, c, :], pair[0][:, c, :].bitcast(F32),
                                              ALU.subtract).then_inc(h_lo, 1)

                        def empty(j):
                            if on_vector(j):
                                dve.wait_ge(full, j + 1)
                                consume(dve, j, bank(j), chain, True).then_inc(free_v, 1)

                        def later(j):
                            dve.wait_ge(followed, j + 1)
                            dve_then(dve, j, chain)

                        programme(split_w, split_h, empty, later if dve_then else None)

                    @block.sync
                    def _(sp):
                        for dst, source in loads:
                            sp.dma_start(dst, source).then_inc(loaded, 16)
                        for n, (u, _, _) in enumerate(units):
                            stream.done[u] = (w_lo, 2 * (n + 1) + 1)
                        stream.prefetch(sp, units[-1][0] + 1)
                        if loads:
                            sp.wait_ge(loaded, 16 * len(loads))

        def feature_products(u0, n_chunks):
            products = [(j, "feature", (j % 4) * P, P, None, True, True) for j in range(n_chunks)]
            return [(u0 + j // 4, 0, products[j:j + 4]) for j in range(0, n_chunks, 4)]

        def token_products(u0, n_units, width=UC):
            return [(u0 + n, 0, [(n * NT + t, "token", 0, width, t, True, True) for t in range(NT)])
                    for n in range(n_units)]

        def copy(eng, vector, dst, src):
            return eng.tensor_copy(dst, src) if vector else eng.activation(dst, src, ACT.Copy)

        def feature_chunk(pe, u, c0, width, dst, src=None):
            w, h = stream.view(u), hT if src is None else src
            for k in range(KD):
                mm = pe.matmul(dst, w[:, k, c0:c0 + width], h[:, k, :], start=(k == 0), stop=(k == KD - 1))
            return mm

        def token_tile(pe, u, c0, width, t, dst, src=None, first=True, last=True):
            w, h = stream.view(u), hT if src is None else src
            kc = stream.src[u][1]
            for k in range(kc):
                mm = pe.matmul(dst, h[:, k, t * P:(t + 1) * P], w[:, k, c0:c0 + width],
                               start=(first and k == 0), stop=(last and k == kc - 1))
            return mm

        rows_of = [
            [("mem_norm", a["mem_norm"]), ("mix_norm", a["mix_norm"]), ("kv_norm", a["kv_norm"]),
             ("mlp_norm", a["mlp_norm"]), ("attn_norm", a["attn_norm_g_2"]), ("ffn_norm", a["ffn_norm_g_2"]),
             ("conv_w", a["a_conv_w"])],
            [("mu", a["rwkv_mu_2"]), ("w0", a["rwkv_w0_2"]), ("a0", a["rwkv_a0_2"]), ("k_k", a["rwkv_k_k_2"]),
             ("k_a", a["rwkv_k_a_2"]), ("r_k", a["rwkv_r_k_2"]), ("ssd_conv_b", a["ssd_conv_b_2"]),
             ("ssd_norm", a["ssd_norm_g_2"])],
            [("ssd_conv_w", a["ssd_conv_w_2"]), ("cmp_pos", a["cmp_pos"])],
        ]
        cols = sb("cols", [P, 3, P])
        col_at = {}
        n_loads = 0
        row_list = []
        for tile, group in enumerate(rows_of):
            r = 0
            for name, v in group:
                size = int(np.prod(v.shape))
                n = size // P
                col_at[name] = (tile, r)
                row_list.append((tile, r, n, bass.AP(v.tensor, v.offset, [[P, n], [1, P]])))
                r += n
            assert r <= P
        row_counts = [sum(n for t, _, n, _ in row_list if t == tile) for tile in range(3)]

        def col(name, i, n=1):
            tile, r = col_at[name]
            return cols[:, tile, r + i:r + i + n]

        gain_rows = [("q_gain", a["b_q_gain"], 64), ("k_gain", a["k_gain"], 192), ("mem_q_gain", a["mem_q_gain"], 128),
                     ("mem_k_gain", a["mem_k_gain"], 128), ("d_skip", a["ssd_d_2"], 32),
                     ("b_rg", a["b_router_group_2"], NG), ("b_re", a["b_router_expert_2"], NE)]
        ssd_cols = sb("ssd_cols", [SH, 4])
        gains = sb("gains", [P, sum(n for _, _, n in gain_rows)])
        g_at, r = {}, 0
        for name, _, n in gain_rows:
            g_at[name] = (r, n)
            r += n

        def everywhere(v, n, off=0):
            return bass.AP(v.tensor, v.offset + off, [[0, P], [1, n]])

        def gain(name, i=0, n=HD):
            lo = g_at[name][0] + i
            return gains[:, lo:lo + n]

        first = ctx.enter_context(ExitStack())
        acs_row = nc.dram_tensor("acs_row", [SH, S], F32, kind="Internal").ap()
        gate_row = nc.dram_tensor("gate_row", [NE, 3, S], F32, kind="Internal").ap()
        dist_row = nc.dram_tensor("dist_row", [NH, 512], F32, kind="Internal").ap()
        cmp2 = sb("cmp_w2", [P, 2, 2, HD], on=first)
        mem_kT = sb("mem_kT", [P, 2, MW // P, M], on=first)
        mem_v = sb("mem_v", [P, 2, M // P, MW], on=first)

        x_landed = ctx.enter_context(nc.semaphore("x_landed"))
        bias_out = ctx.enter_context(nc.semaphore("bias_row_out"))

        def late_loads():
            with meeting() as block:
                @block.sync
                def _(sp):
                    sp.wait_ge(x_landed, 16)
                    sp.wait_ge(bias_out, 16)

        def setup(mem, rows, table, hb):
            landed = sem("setup_landed")
            turned, taken, cleared = sem("setup_turned"), sem("setup_taken"), sem("setup_cleared")
            n = 0
            with meeting() as block:
                @block.gpsimd
                def _(pool):
                    pool.memset(rows[:, :, :], 0.0).then_inc(cleared, 1)

                @block.sync
                def _(sp):
                    nonlocal n
                    for dst, src in [(mem[:, :, :], a["mem"][0].rearrange("(t p) d -> p t d", p=P)),
                                     (const[:, :], a["const"])]:
                        sp.dma_start(dst, src).then_inc(landed, 16)
                        n += 1
                    sp.wait_ge(cleared, 1)
                    for tile, r, k, src in row_list:
                        sp.dma_start(rows[r:r + k, tile, :], src).then_inc(landed, 16)
                        n += 1
                    stream.load(sp, 0)
                    stream.issued = 1
                    sp.dma_start(x[:, :, :], a["x"][0].rearrange("(t p) d -> p t d", p=P)).then_inc(x_landed, 16)
                    stream.prefetch(sp, 0)
                    sp.wait_ge(taken, 1)
                    sp.dma_start(dist_row, hb[0:NH, :]).then_inc(bias_out, 16)

                @block.scalar
                def _(act):
                    nonlocal n
                    for name, v, k in gain_rows:
                        lo = g_at[name][0]
                        act.dma_start(gains[:, lo:lo + k], everywhere(v, k)).then_inc(landed, 16)
                        n += 1
                    for i, v in enumerate((a["ssd_dt_bias_2"], a["ssd_a_log_2"])):
                        act.dma_start(ssd_cols[:, i:i + 1], bass.AP(v.tensor, v.offset, [[1, SH], [1, 1]]))\
                            .then_inc(landed, 16)
                        n += 1
                    act.dma_start(cmp2[:, :, :, :], a["cmp_w2"].rearrange("i (k p) d -> p i k d", p=P))\
                        .then_inc(landed, 16)
                    act.wait_ge(cleared, 2)
                    act.dma_start(table[0:NBK, :], a["rel_bias"]).then_inc(landed, 16)
                    n += 2

                @block.tensor
                def _(pe):
                    pe.wait_ge(cleared, 2)
                    pe.wait_ge(landed, 16 * n)
                    pe.matmul(ps[0:NH, 3, :], table[0:NBK + 1, :], c_("hot")[0:NBK + 1, :],
                              start=True, stop=True).then_inc(turned, 1)
                    for i in range(3):
                        pe.transpose(ps[:, i, 0:P], rows[:, i, :], ident).then_inc(turned, 1)

                @block.vector
                def _(dve):
                    dve.wait_ge(cleared, 1)
                    dve.memset(table[:, :], NEG).then_inc(cleared, 1)
                    dve.wait_ge(turned, 1)
                    dve.tensor_copy(hb[0:NH, :], ps[0:NH, 3, :]).then_inc(taken, 1)
                    dve.wait_ge(turned, 4)
                    for i in range(3):
                        dve.tensor_copy(cols[:, i, :], ps[:, i, 0:P]).then_inc(taken, 1)

        def norm(name, src, outs, scaled=None):
            with ExitStack() as on:
                if scaled is None:
                    scaled = sb(name + "_scaled", [P, NT, D], on=on)
                stat = sb(name + "_stat", [P, 4, NT], on=on)
                squares, roots, scale = sem(name + "_squares"), sem(name + "_roots"), sem(name + "_scale")
                turned, led = sem(name + "_turned"), sem(name + "_led")
                in_parts = [o for o in outs if isinstance(o[2], list)]
                plain = [o for o in outs if not isinstance(o[2], list)]
                with meeting() as block:
                    @block.scalar
                    def _(act):
                        act.activation(scaled[:, 0, :], src[:, 0, :], ACT.Square,
                                       accum_out=stat[:, 0, 0:1]).then_inc(squares, 1)
                        act.wait_ge(scale, 1)
                        act.activation(stat[:, 2, :], stat[:, 1, :], ACT.Sqrt).then_inc(roots, 1)
                        for c in range(KD):
                            if in_parts or c % 2:
                                act.wait_ge(turned, c + 1)
                            for gname, g0, (hi, lo) in in_parts:
                                act.activation(hi[:, c, :], ps[:, c, 0:S], ACT.Copy, scale=col(gname, g0 + c))\
                                    .then_inc(led, 1)
                            if c % 2:
                                for gname, g0, dst in plain:
                                    act.activation(dst[:, c, :], ps[:, c, 0:S], ACT.Copy, scale=col(gname, g0 + c))

                    @block.vector
                    def _(dve):
                        dve.scalar_tensor_tensor(scaled[:, 1, :], src[:, 1, :], 1.0, src[:, 1, :], ALU.mult, ALU.mult,
                                                 accum_out=stat[:, 0, 1:2]).then_inc(squares, 1)
                        dve.wait_ge(squares, NT)
                        dve.tensor_scalar(stat[:, 1, :], stat[:, 0, :], 1.0 / D, EPS, ALU.mult, ALU.add)\
                            .then_inc(scale, 1)
                        dve.wait_ge(roots, 1)
                        dve.reciprocal(stat[:, 3, :], stat[:, 2, :]).then_inc(scale, 1)
                        dve.wait_ge(scale, 2)
                        for t in range(NT):
                            dve.tensor_scalar(scaled[:, t, :], src[:, t, :], stat[:, 3, t:t + 1], None, ALU.mult)\
                                .then_inc(scale, 1)
                        for c in range(KD):
                            if c % 2 == 0:
                                dve.wait_ge(turned, c + 1)
                                for gname, g0, dst in plain:
                                    dve.tensor_scalar(dst[:, c, :], ps[:, c, 0:S], col(gname, g0 + c), None, ALU.mult)
                            for n, (gname, g0, (hi, lo)) in enumerate(in_parts):
                                dve.wait_ge(led, c * len(in_parts) + n + 1)
                                dve.scalar_tensor_tensor(lo[:, c, :], ps[:, c, 0:S], col(gname, g0 + c),
                                                         hi[:, c, :].bitcast(F32), ALU.mult, ALU.subtract)

                    @block.tensor
                    def _(pe):
                        for t in range(NT):
                            pe.wait_ge(scale, 3 + t)
                            for c in range(KD):
                                mm = pe.transpose(ps[:, c, t * P:(t + 1) * P], scaled[:, t, c * P:(c + 1) * P], ident)
                                if t == NT - 1:
                                    mm.then_inc(turned, 1)

        def head_norm(name, items, copies=()):
            sums, means, roots, scale = (sem(f"{name}_{s}") for s in ("squares", "means", "roots", "scale"))
            with meeting() as block:
                @block.scalar
                def _(act):
                    for dst, src, sq, st, g, k in items:
                        act.activation(sq, src, ACT.Square).then_inc(sums, 1)
                    for n, (dst, src, sq, st, g, k) in enumerate(items):
                        act.wait_ge(means, 2 * n + 2)
                        act.activation(st[:, 1], st[:, 0], ACT.Sqrt).then_inc(roots, 1)

                @block.vector
                def _(dve):
                    for n, (dst, src, sq, st, g, k) in enumerate(items):
                        dve.wait_ge(sums, n + 1)
                        dve.tensor_reduce(st[:, 0], sq, AX.X, ALU.add).then_inc(means, 1)
                        dve.wait_ge(means, 2 * n + 1)
                        dve.tensor_scalar(st[:, 0], st[:, 0], 1.0 / HD / (k * k), EPS / (k * k), ALU.mult, ALU.add)\
                            .then_inc(means, 1)
                    for dst, src in copies:
                        dve.tensor_copy(dst, src)
                    at = 0
                    for n, (dst, src, sq, st, g, k) in enumerate(items):
                        shape = list(src.shape)
                        dve.wait_ge(roots, n + 1)
                        dve.reciprocal(st[:, 0], st[:, 1]).then_inc(scale, 1)
                        dve.wait_ge(scale, at + 1)
                        dve.tensor_tensor(sq, src, st[:, 0].unsqueeze(3).broadcast_to(shape), ALU.mult)\
                            .then_inc(scale, 1)
                        dve.wait_ge(scale, at + 2)
                        for d in dst:
                            dve.tensor_tensor(d, sq, g.unsqueeze(1).unsqueeze(1).broadcast_to(shape), ALU.mult)
                        at += 2

        def heads(v):
            return v.rearrange("p t (h d) -> p t h d", d=HD)

        def memory(memT):
            with ExitStack() as on:
                kv = sb("mem_kv", [P, 2, NT, 2 * MW], on=on)
                kn = sb("mem_kn", [P, 2, NT, MW], on=on)
                sq = sb("mem_sq", [P, 2, NT, MW], on=on)
                st = sb("mem_st", [P, 2, 2, NT, MH], on=on)

                def produce(pe, j, bank):
                    layer, t = divmod(j, NT)
                    u = unit["mem_kv"] + layer
                    if t == 0:
                        stream.arrived(pe, u)
                    return token_tile(pe, u, 0, 2 * MW, t, bank, src=memT)

                def consume(eng, j, bank, chain, vector):
                    return copy(eng, vector, kv[:, j // NT, j % NT, :], bank)

                stage("mem_kv", 2 * NT, produce, consume,
                      uses={unit["mem_kv"] + l: l * NT + 1 for l in range(2)})
                head_norm("mem_k", [([heads(kn[:, l])], heads(kv[:, l, :, 0:MW]), heads(sq[:, l]), st[:, l],
                                     gain("mem_k_gain", l * HD), 1.0) for l in range(2)],
                          copies=[(mem_v[:, l], kv[:, l, :, MW:]) for l in range(2)])

                def turn(pe, j, bank):
                    layer, pair = divmod(j, MW // P)
                    for t in range(NT):
                        mm = pe.transpose(bank[:, t * P:(t + 1) * P], kn[:, layer, t, pair * P:(pair + 1) * P], ident)
                    return mm

                stage("mem_turn", 2 * MW // P, turn,
                      lambda eng, j, bank, chain, vector: copy(eng, vector, mem_kT[:, j // 2, j % 2, :], bank[:, 0:M]))

        def attention(name, groups, sums):
            items = []
            for g, grp in enumerate(groups):
                for h0 in range(0, len(grp["heads"]), grp["per"]):
                    hs = grp["heads"][h0:h0 + grp["per"]]
                    items.append((g, h0, hs, h0 + grp["per"] >= len(grp["heads"])))
            n = len(items)
            logits, top, probs, turned, turned_taken, given, combined = \
                (sem(f"{name}_{s}") for s in ("logits", "top", "probs", "turned", "turned_taken", "given", "combined"))
            chain_sem = sem(name + "_chain")
            exps = [0]
            for g, h0, hs, last in items:
                exps.append(exps[-1] + len(hs))
            with ExitStack() as on:
                nmax = sb(name + "_nmax", [P, 2, 4], on=on)
                probs_sb = sb(name + "_probs", [P, 2, 512], on=on)
                pT = sb(name + "_pT", [P, 2, 4 * P], on=on)
                coef = sb(name + "_coef", [P, 2, 12], on=on)
                part = sb(name + "_part", [P, CONV_CH], on=on)

                def bank_l(i):
                    return ps[:, i % 2]

                def bank_t(i):
                    return ps[:, 2 + i % 2]

                def bank_o(g):
                    return ps[:, 4 + 2 * (g % 2):6 + 2 * (g % 2)].rearrange("p b n -> p (b n)")

                with meeting() as block:
                    @block.tensor
                    def _(pe):
                        def scores(i):
                            g, h0, hs, last = items[i]
                            grp = groups[g]
                            nk = sum(grp["keys"])
                            if i >= 2:
                                pe.wait_ge(probs, exps[i - 1])
                            for n_h, h in enumerate(hs):
                                dst = bank_l(i)[:, n_h * nk:(n_h + 1) * nk]
                                bias = grp["bias"](h) if grp["bias"] else None
                                mm = pe.matmul(dst, grp["q"](h), grp["k"](h), start=True, stop=bias is None)
                                if bias is not None:
                                    mm = pe.matmul(dst, c_("flip"), bias, start=False, stop=True)
                            mm.then_inc(logits, 1)

                        def turn(i):
                            g, h0, hs, last = items[i]
                            grp = groups[g]
                            nk = sum(grp["keys"])
                            pe.wait_ge(probs, exps[i + 1])
                            if i >= 2:
                                pe.wait_ge(turned_taken, i - 1)
                            b = 0
                            for n_h in range(len(hs)):
                                k0 = 0
                                for w in grp["keys"]:
                                    lo = n_h * nk + k0
                                    mm = pe.transpose(bank_t(i)[0:w, b * P:(b + 1) * P],
                                                      probs_sb[:, i % 2, lo:lo + w], ident)
                                    k0 += w
                                    b += 1
                            mm.then_inc(turned, 1)

                        def values(i):
                            g, h0, hs, last = items[i]
                            grp = groups[g]
                            pe.wait_ge(turned_taken, i + 1)
                            if h0 == 0 and g >= 2:
                                pe.wait_ge(combined, g - 1)
                            b = 0
                            for n_h, h in enumerate(hs):
                                at_h = h * HD
                                for kt, w in enumerate(grp["keys"]):
                                    mm = pe.matmul(bank_o(g)[:, at_h:at_h + HD], pT[0:w, i % 2, b * P:(b + 1) * P],
                                                   grp["v"](h, kt), start=(kt == 0), stop=(kt == len(grp["keys"]) - 1))
                                    b += 1
                            mm.then_inc(given, 1)

                        scores(0)
                        for i in range(n):
                            if i + 1 < n:
                                scores(i + 1)
                            turn(i)
                            if i:
                                values(i - 1)
                        values(n - 1)

                    @block.vector
                    def _(dve):
                        chain = Chain(dve, chain_sem)

                        def maxima(i):
                            g, h0, hs, last = items[i]
                            nk = sum(groups[g]["keys"])
                            dve.wait_ge(logits, i + 1)
                            if i >= 2:
                                dve.wait_ge(probs, exps[i - 1])
                            dve.tensor_reduce(nmax[:, i % 2, 0:len(hs)],
                                              bank_l(i)[:, 0:len(hs) * nk].rearrange("p (h k) -> p h k", k=nk),
                                              AX.X, ALU.max, negate=True).then_inc(top, 1)

                        def take(i):
                            g, h0, hs, last = items[i]
                            w, nb = max(groups[g]["keys"]), len(hs) * len(groups[g]["keys"])
                            dve.wait_ge(turned, i + 1)
                            if i >= 2:
                                dve.wait_ge(given, i - 1)
                            dve.tensor_copy(pT[0:w, i % 2, 0:nb * P], bank_t(i)[0:w, 0:nb * P])\
                                .then_inc(turned_taken, 1)

                        def combine(g, i):
                            grp = groups[g]
                            nh = len(grp["heads"])
                            dve.wait_ge(probs, exps[i + 1])
                            k = coef[:, g % 2, 0:nh]
                            chain(dve.reciprocal(k, sums[:, grp["slot"], 0:nh]))
                            for m in grp["factors"]:
                                chain(dve.tensor_tensor(k, k, m, ALU.mult))
                            dve.wait_ge(given, i + 1)
                            o = bank_o(g)[:, 0:nh * HD].rearrange("p (h d) -> p h d", d=HD)
                            kb = k.unsqueeze(2).broadcast_to([P, nh, HD])
                            dst = grp["out"]
                            if grp["add"]:
                                pv = part[:, 0:nh * HD].rearrange("p (h d) -> p h d", d=HD)
                                chain(dve.tensor_tensor(pv, o, kb, ALU.mult))
                                if g:
                                    dve.wait_ge(combined, g)
                                dve.tensor_tensor(dst, dst, pv, ALU.add).then_inc(combined, 1)
                            else:
                                dve.tensor_tensor(dst, o, kb, ALU.mult).then_inc(combined, 1)

                        for i in range(n + 2):
                            if i < n:
                                maxima(i)
                            if 1 <= i <= n:
                                take(i - 1)
                            if i >= 2 and items[i - 2][3]:
                                combine(items[i - 2][0], i - 2)

                    @block.scalar
                    def _(act):
                        for i in range(n):
                            g, h0, hs, last = items[i]
                            nk = sum(groups[g]["keys"])
                            act.wait_ge(top, i + 1)
                            if i >= 2:
                                act.wait_ge(turned, i - 1)
                            for n_h, h in enumerate(hs):
                                act.activation(probs_sb[:, i % 2, n_h * nk:(n_h + 1) * nk],
                                               bank_l(i)[:, n_h * nk:(n_h + 1) * nk], ACT.Exp,
                                               bias=nmax[:, i % 2, n_h:n_h + 1],
                                               accum_out=sums[:, groups[g]["slot"], h:h + 1])\
                                    .then_inc(probs, 1)

        def add_projection(name, u0, src):
            def consume(eng, j, bank, chain, vector):
                half, t = divmod(j, NT)
                dst = x[:, t, half * UC:(half + 1) * UC]
                return eng.tensor_tensor(dst, dst, bank, ALU.add)

            split_stage(name, token_products(u0, 2), consume, src, on_vector=lambda j: True, depth=2)

        def turn_into(name, src, chunks, dst, dst0=0, scale=None):
            def produce(pe, j, bank):
                for t in range(NT):
                    mm = pe.transpose(bank[:, t * P:(t + 1) * P], src[:, t, j * P:(j + 1) * P], ident)
                return mm

            def consume(eng, j, bank, chain, vector):
                if scale is None:
                    return copy(eng, vector, dst[:, dst0 + j, :], bank[:, 0:S])
                if vector:
                    return eng.tensor_scalar(dst[:, dst0 + j, :], bank[:, 0:S], scale(j), None, ALU.mult)
                return eng.activation(dst[:, dst0 + j, :], bank[:, 0:S], ACT.Copy, scale=scale(j))

            stage(name, chunks, produce, consume)

        def turn_into_pair(name, src, chunks, pair, scale=None):
            turned, led, left = sem(name + "_turned"), sem(name + "_hi"), sem(name + "_lo")
            with meeting() as block:
                @block.tensor
                def _(pe):
                    for c in range(chunks):
                        if c >= 8:
                            pe.wait_ge(left, c - 7)
                        for t in range(NT):
                            mm = pe.transpose(ps[:, c % 8, t * P:(t + 1) * P], src[:, t, c * P:(c + 1) * P], ident)
                        mm.then_inc(turned, 1)

                @block.scalar
                def _(act):
                    for c in range(chunks):
                        act.wait_ge(turned, c + 1)
                        act.activation(pair[0][:, c, :], ps[:, c % 8, 0:S], ACT.Copy, scale=scale(c) if scale else 1.0)\
                            .then_inc(led, 1)

                @block.vector
                def _(dve):
                    for c in range(chunks):
                        dve.wait_ge(led, c + 1)
                        dve.scalar_tensor_tensor(pair[1][:, c, :], ps[:, c % 8, 0:S], scale(c) if scale else 1.0,
                                                 pair[0][:, c, :].bitcast(F32), ALU.mult, ALU.subtract)\
                            .then_inc(left, 1)

        def close_sums(pe):
            for b in range(4, 8):
                mm = pe.matmul(ps[:, b], c_("noughts")[:, 0:P], c_("noughts"), start=False, stop=True)
            return mm

        def mlp(layer, h_pair):
            u0 = unit[f"mlp{layer}"]
            assert u0 % RING == 0
            n_units = 2 * FF // UC
            body = 2
            trips = n_units // RING
            pieces = 4
            SPLIT = 4
            up_v = a["w_up"][layer].rearrange("(k p) (i b c) -> i b p k c", p=P, b=2, c=UC)
            down_v = a["w_down"][layer].rearrange("(i b k p) c -> i b p k c", p=P, b=2, k=UC // P)
            ups, rect, squared, hid_hi, hid_lo, downs, closed, w_hi, w_lo = \
                (sem(f"mlp{layer}_{s}") for s in ("ups", "rectified", "squared", "hid_hi", "hid_lo", "downs",
                                                  "closed", "w_hi", "w_lo"))
            nm = UC // P
            nb = nm // 2
            with ExitStack() as on:
                w_split = [sb("mlp_w_" + part, [P, SPLIT, KD * UC // 2], F32R, on=on) for part in ("hi", "lo")]
                hid = [sb("mlp_hid_" + part, [P, nm, S], F32R, on=on) for part in ("hi", "lo")]
                rec = sb("mlp_rec", [P, nm, S], on=on)
                acc = lambda t, h: ps[:, 4 + 2 * t + h]

                def piece_slot(buf, j):
                    return buf[:, j % SPLIT, :].rearrange("p (k c) -> p k c", k=4 if j % pieces < 2 else 2)

                def raw_piece(j):
                    kc = 4 if j % pieces < 2 else 2
                    return stream.view(u0 + j // 2)[:, (j % 2) * kc:(j % 2 + 1) * kc, :]

                def both(buf, b):
                    return buf[:, 2 * b:2 * b + 2, :].rearrange("p m s -> p (m s)")

                with meeting() as block:
                    @block.tensor
                    def _(pe):
                        for t in range(NT):
                            for h in range(2):
                                pe.matmul(acc(t, h), ident, x[:, t, h * UC:(h + 1) * UC], start=True, stop=False)
                        with pe.Fori(0, trips) as i:
                            for b in range(body):
                                w = [[piece_slot(p, b * pieces + half) for p in w_split] for half in range(2)]
                                pe.wait_ge(w_lo, i * (body * pieces) + (b * pieces + 2))
                                for m in range(nm):
                                    dst = ps[:, m // 2, (m % 2) * S:(m % 2 + 1) * S]
                                    for k in range(KD):
                                        mm = three(pe, dst, [p[:, k % 4, m * P:(m + 1) * P] for p in w[k // 4]],
                                                   [p[:, k, :] for p in h_pair], start=(k == 0), stop=(k == KD - 1))
                                    if m % 2:
                                        mm.then_inc(ups, 1)
                                for half in range(2):
                                    j = b * pieces + 2 + half
                                    w = [piece_slot(p, j) for p in w_split]
                                    pe.wait_ge(w_lo, i * (body * pieces) + (j + 1))
                                    pe.wait_ge(hid_lo, i * (body * nb) + (b * nb + half + 1))
                                    for k in range(2):
                                        f = 2 * half + k
                                        for t in range(NT):
                                            for h in range(2):
                                                mm = three(pe, acc(t, h), [p[:, f, t * P:(t + 1) * P] for p in hid],
                                                           [p[:, k, h * UC:(h + 1) * UC] for p in w],
                                                           start=False, stop=False)
                                    mm.then_inc(downs, 1)
                        close_sums(pe).then_inc(closed, 1)

                    @block.scalar
                    def _(act):
                        def split(i, j, free=None):
                            jj = j % (body * pieces)
                            u = u0 + jj // 2
                            if j % 2 == 0:
                                act.wait_ge(stream.sems[u % RING],
                                            i * 16 + (16 * (j // (body * pieces)) + stream.need[u]))
                            if free is not None:
                                act.wait_ge(*free)
                            act.activation(piece_slot(w_split[0], jj), raw_piece(jj), ACT.Copy).then_inc(w_hi, 1)

                        def turn(i, b, last=False):
                            for m in range(nb):
                                done = i * (body * nb) + (b * nb + m + 1)
                                act.wait_ge(ups, done)
                                act.activation(both(rec, m), ps[:, m], ACT.Relu).then_inc(rect, 1)
                                act.wait_ge(squared, done)
                                act.activation(both(hid[0], m), both(rec, m), ACT.Copy).then_inc(hid_hi, 1)
                            if not last:
                                j = (b + 1) * pieces
                                split(i, j)
                                split(i, j + 1)
                                split(i, j + 2, (downs, i * (2 * body) + (2 * b + 1)))
                                split(i, j + 3, (downs, i * (2 * body) + (2 * b + 2)))

                        for j in range(SPLIT):
                            split(0, j)
                        with act.Fori(0, trips - 1) as i:
                            for b in range(body):
                                turn(i, b)
                        for b in range(body):
                            turn(trips - 1, b, last=b == body - 1)

                    @block.vector
                    def _(dve):
                        def split(i, j):
                            jj = j % (body * pieces)
                            dve.wait_ge(w_hi, i * (body * pieces) + (j + 1))
                            dve.tensor_tensor(piece_slot(w_split[1], jj), raw_piece(jj),
                                              piece_slot(w_split[0], jj).bitcast(F32), ALU.subtract).then_inc(w_lo, 1)

                        def turn(i, b, last=False):
                            for m in range(nb):
                                done = i * (body * nb) + (b * nb + m + 1)
                                dve.wait_ge(rect, done)
                                dve.tensor_tensor(both(rec, m), both(rec, m), both(rec, m), ALU.mult)\
                                    .then_inc(squared, 1)
                                dve.wait_ge(hid_hi, done)
                                dve.tensor_tensor(both(hid[1], m), both(rec, m), both(hid[0], m).bitcast(F32),
                                                  ALU.subtract).then_inc(hid_lo, 1)
                            if not last:
                                for j in range((b + 1) * pieces, (b + 2) * pieces):
                                    split(i, j)

                        for j in range(SPLIT):
                            split(0, j)
                        with dve.Fori(0, trips - 1) as i:
                            for b in range(body):
                                turn(i, b)
                        for b in range(body):
                            turn(trips - 1, b, last=b == body - 1)
                        dve.wait_ge(closed, 1)
                        for t in range(NT):
                            for h in range(2):
                                dve.tensor_copy(x[:, t, h * UC:(h + 1) * UC], acc(t, h))

                    @block.sync
                    def _(sp):
                        stream.prefetch(sp, u0)
                        with sp.Fori(0, trips - 1) as i:
                            for n in range(RING):
                                sp.wait_ge(w_lo, i * (body * pieces) + 2 * (n + 1))
                                sp.dma_start(stream.view(u0 + n), (up_v, down_v)[n % 2][i + 1, n // 2])\
                                    .then_inc(stream.sems[n], 16)
                        for n in range(RING):
                            stream.done[u0 + n_units - RING + n] = (w_lo, (trips - 1) * body * pieces + 2 * (n + 1))
                        stream.issued = u0 + n_units
                        stream.prefetch(sp, u0 + n_units)

        def conv_layer():
            with ExitStack() as on:
                z = sb("conv_z", [P, 3 * CONV_CH // P, S], on=on)
                q = sb("conv_q", [P, NT, MW], on=on)
                nconv = CONV_CH // P
                cat = sb("cat", [P, KD, S], on=on)
                u0 = unit["a_in"]
                n_fm = 3 * nconv

                products = [(j, "feature", (j % 4) * P, P, None, True, True) for j in range(n_fm)]
                products += [(n_fm + t, "token", 2 * P, MW, t, True, True) for t in range(NT)]
                units = [(u0 + n, 0, products[4 * n:4 * n + 4]) for n in range(5)]

                def consume(eng, j, bank, chain, vector):
                    dst = z[:, j, :] if j < n_fm else q[:, j - n_fm, :]
                    return copy(eng, vector, dst, bank[:, 0:S])

                split_stage("a_in", units, consume, hT)

                conv_step = sem("conv_step")
                with meeting() as block:
                    @block.vector
                    def _(dve):
                        n = 0
                        gb, gc, gu = (z[:, i * nconv:(i + 1) * nconv, :] for i in range(3))
                        dve.tensor_tensor(gc, gc, gu, ALU.mult).then_inc(conv_step, 1)
                        n += 1
                        dve.wait_ge(conv_step, n)
                        for c in range(nconv):
                            dve.tensor_scalar(gu[:, c, :], gc[:, c, :], col("conv_w", 2 * nconv + c), None, ALU.mult)\
                                .then_inc(conv_step, 1)
                        n += nconv
                        dve.wait_ge(conv_step, n)
                        for tap in (1, 0):
                            back = 2 - tap
                            for c in range(nconv):
                                dve.scalar_tensor_tensor(gu[:, c, back:], gc[:, c, 0:S - back],
                                                         col("conv_w", tap * nconv + c), gu[:, c, back:],
                                                         ALU.mult, ALU.add).then_inc(conv_step, 1)
                            n += nconv
                            dve.wait_ge(conv_step, n)
                        dve.tensor_tensor(cat[:, 0:nconv, :], gb, gu, ALU.mult)
                memory_attention(0, q, cat, nconv)
                add_projection("out0", unit["out0"], cat)

        def memory_attention(layer, q, cat, chunk0, more=None, more_norms=(), gates=None):
            with ExitStack() as on:
                qn = sb("mq_n", [P, NT, MW], on=on)
                sq = sb("mq_sq", [P, NT, MW], on=on)
                st = sb("mq_st", [P, 2, NT, MH], on=on)
                qT = sb("mq_T", [P, MW // P, S], on=on)
                ym = sb("ym", [P, NT, MW], on=on)
                sums = sb("mq_sums", [P, NT, MH], on=on)
                head_norm(f"mq{layer}", [([heads(qn)], heads(q), heads(sq), st,
                                          gain("mem_q_gain", layer * HD), HD ** -0.5)])
                turn_into(f"mq_turn{layer}", qn, MW // P, qT)
                groups = []
                for t in range(NT):
                    groups.append(dict(
                        heads=[0, 2, 1, 3], per=2, keys=[P, P], bias=None, slot=t, factors=[], add=False,
                        q=lambda h, t=t: qT[(h % 2) * HD:(h % 2 + 1) * HD, h // 2, t * P:(t + 1) * P],
                        k=lambda h: mem_kT[(h % 2) * HD:(h % 2 + 1) * HD, layer, h // 2, :],
                        v=lambda h, kt: mem_v[:, layer, kt, h * HD:(h + 1) * HD],
                        out=ym[:, t, :].rearrange("p (h d) -> p h d", d=HD)))
                attention(f"mem_attn{layer}", groups, sums)
                turn_into(f"ym_turn{layer}", ym, MW // P, cat, chunk0)

        def shared_buffers(on):
            return dict(
                kT={b: sb(f"{b}_kT", [P, G, S], on=on) for b in ("s", "w")},
                v={b: sb(f"{b}_v", [P, NT, G * HD], on=on) for b in ("s", "w")},
                kcT=sb("c_kT", [P, G, NC], on=on), vc=sb("c_v", [NC, G, HD], on=on))

        def shared_kv(sh, hkv):
            with ExitStack() as on2:
                kv = sb("kv_rest", [P, NT, 4 * G * HD], on=on2)
                pair = sb("cmp_pairs", [P, 2, G, S], on=on2)
                flat = sb("cmp_flat", [P, 2, CMP_L // 2, G * NC], on=on2)
                u0 = unit["kv"]

                def produce(pe, j, bank):
                    if j == 0:
                        stream.arrived(pe, u0)
                    if j == 2 + NT:
                        stream.arrived(pe, u0 + 1)
                    if j < 2:
                        return feature_chunk(pe, u0, j * P, P, bank[:, 0:S], src=hkv)
                    second, t = divmod(j - 2, NT)
                    return token_tile(pe, u0 + second, 0 if second else 2 * P, 2 * P, t, bank[:, 0:2 * P], src=hkv)

                def consume(eng, j, bank, chain, vector):
                    if j < 2:
                        for g in range(G):
                            src = bank[g * HD:(g + 1) * HD, 0:S]
                            eng.tensor_copy(pair[0:HD, j, g, :], src)
                            last = eng.tensor_copy(pair[HD:P, j, g, 0:S - 1], src[:, 1:S])
                            if g == 0:
                                chain(last)
                        return last
                    second, t = divmod(j - 2, NT)
                    return copy(eng, vector, kv[:, t, second * 2 * P:(second + 1) * 2 * P], bank[:, 0:2 * P])

                stage("kv", 2 + 2 * NT, produce, consume, on_vector=lambda j: j < 2 or j % 2 == 0,
                      uses={u0: 1 + NT, u0 + 1: 1 + 2 * NT})

                half = CMP_S // 2
                with meeting() as block:
                    @block.vector
                    def _(dve):
                        for i in range(2):
                            for g in range(G):
                                for part in range(2):
                                    src = pair[:, i, g, part * CMP_S:part * CMP_S + NC * CMP_S]\
                                        .rearrange("p (c l two) -> p l c two", c=NC, two=2)[:, :, :, 0]
                                    pos = col("cmp_pos", i * CMP_L // 2 + part * half, half)
                                    dve.tensor_tensor(flat[:, i, part * half:(part + 1) * half, g * NC:(g + 1) * NC],
                                                      src, pos.unsqueeze(2).broadcast_to([P, half, NC]), ALU.add)

                hidden = sb("cmp_hidden", [G * NC, 2, CMP_H], on=on2)
                u1 = unit["cmp1"]

                def mlp1(pe, j, bank):
                    w = stream.arrived(pe, u1 + j)
                    for k in range(CMP_L // 2):
                        mm = pe.matmul(bank[0:G * NC, 0:CMP_H], flat[:, j, k, :], w[:, k, :],
                                       start=(k == 0), stop=(k == CMP_L // 2 - 1))
                    return mm

                stage("cmp1", 2, mlp1, lambda eng, j, bank, chain, vector:
                      eng.activation(hidden[:, j, :], bank[0:G * NC, 0:CMP_H], ACT.Gelu_apprx_tanh),
                      on_vector=lambda j: False, uses={u1: 0, u1 + 1: 1})
                hiddenT = sb("cmp_hiddenT", [P, 2, 2, G * NC], on=on2)

                def turn(pe, j, bank):
                    for k in range(2):
                        mm = pe.transpose(bank[:, k * P:k * P + G * NC], hidden[:, j, k * P:(k + 1) * P],
                                          ident[0:G * NC, 0:G * NC])
                    return mm

                stage("cmp_turn", 2, turn, lambda eng, j, bank, chain, vector:
                      copy(eng, vector, hiddenT[:, j, :, :],
                           bank[:, 0:2 * P].rearrange("p (k n) -> p k n", k=2)[:, :, 0:G * NC]))
                kc = sb("cmp_k", [NC, 1, G, HD], on=on2)
                dup = sb("kn_dup", [P, 2, NT, G, 2, HD], on=on2)
                cdup = sb("kc_dup", [NC, G, 2, HD], on=on2)

                def mlp2(pe, j, bank):
                    for g in range(G):
                        for k in range(2):
                            mm = pe.matmul(bank[0:NC, g * HD:(g + 1) * HD], hiddenT[:, j, k, g * NC:(g + 1) * NC],
                                           cmp2[:, j, k, :], start=(k == 0), stop=(k == 1))
                    return mm

                stage("cmp2", 2, mlp2, lambda eng, j, bank, chain, vector:
                      eng.tensor_copy(kc[:, 0] if j == 0 else sh["vc"][:, :, :],
                                      bank[0:NC, 0:G * HD].rearrange("p (g d) -> p g d", g=G)),
                      on_vector=lambda j: True)
                sq = sb("kn_sq", [P, 3, NT, G, HD], on=on2)
                st = sb("kn_st", [P, 3, 2, NT, G], on=on2)
                items = [([cdup[:, :, w].unsqueeze(1) for w in range(2)], kc[:, :, :, :], sq[0:NC, 2, 0:1],
                          st[0:NC, 2, :, 0:1], gain("k_gain", 0)[0:NC, :], 1.0)]
                for b in range(2):
                    src = heads(kv[:, :, 2 * b * P:(2 * b + 1) * P])
                    items.append(([dup[:, b, :, :, w] for w in range(2)], src, sq[:, b], st[:, b],
                                  gain("k_gain", (1 + b) * HD), 1.0))
                head_norm("kn", items, copies=[(sh["v"][b][:, :, :], kv[:, :, (2 * n + 1) * P:(2 * n + 2) * P])
                                               for n, b in enumerate(("s", "w"))])

                def turn_keys(pe, j, bank):
                    if j == 2 * G:
                        for g in range(G):
                            mm = pe.transpose(bank[:, g * P:g * P + NC], cdup[:, g].rearrange("p a d -> p (a d)"),
                                              ident[0:NC, 0:NC])
                        return mm
                    b, g = divmod(j, G)
                    for t in range(NT):
                        mm = pe.transpose(bank[:, t * P:(t + 1) * P], dup[:, b, t, g].rearrange("p a d -> p (a d)"),
                                          ident)
                    return mm

                def take_keys(eng, j, bank, chain, vector):
                    if j == 2 * G:
                        return copy(eng, vector, sh["kcT"][:, :, :],
                                    bank[:, 0:G * P].rearrange("p (g n) -> p g n", g=G)[:, :, 0:NC])
                    b, g = divmod(j, G)
                    return copy(eng, vector, sh["kT"]["sw"[b]][:, g, :], bank[:, 0:S])

                stage("kn_turn", 2 * G + 1, turn_keys, take_keys)

        def nsa_layer(sh):
            with ExitStack() as on:
                dist = sb("dist_bias", [P, NH, 3 * P], on=on)
                q = sb("nsa_q", [P, NT, CONV_CH], on=on)
                gates = sb("nsa_gates", [P, NT, NH, 3], on=on)
                mq = sb("nsa_mq", [P, NT, MW], on=on)
                qT = sb("nsa_qT", [P, NH // 2, S], on=on)
                y = sb("nsa_y", [P, NT, CONV_CH], on=on)
                sums = sb("nsa_sums", [P, 3 * NT, NH], on=on)
                cat = sb("cat", [P, KD, S], on=on)
                u0 = unit["b_in"]
                rest = CONV_CH - UC
                with ExitStack() as on2:
                    qn = sb("nsa_qn", [P, NT, CONV_CH], on=on2)
                    sq = sb("nsa_sq", [P, NT, CONV_CH], on=on2)
                    st = sb("nsa_st", [P, 2, NT, NH], on=on2)

                    def produce(pe, j, bank):
                        part, t = divmod(j, NT)
                        width = stream.src[u0 + part][2]
                        if t == 0:
                            stream.arrived(pe, u0 + part)
                        return token_tile(pe, u0 + part, 0, width, t, bank[:, 0:width])

                    def consume(eng, j, bank, chain, vector):
                        part, t = divmod(j, NT)
                        if part == 0:
                            return eng.activation(q[:, t, 0:UC], bank, ACT.Copy)
                        if part == 1:
                            eng.activation(q[:, t, UC:], bank[:, 0:rest], ACT.Copy)
                            return eng.activation(gates[:, t], bank[:, rest:rest + 3 * NH]
                                                  .rearrange("p (h b) -> p h b", b=3), ACT.Sigmoid)
                        return eng.activation(mq[:, t, :], bank[:, 0:MW], ACT.Copy)

                    stage("b_in", 3 * NT, produce, consume, on_vector=lambda j: False,
                          loads=[(dist[:, :, :], bass.AP(dist_row.tensor, 0, [[1, P], [512, NH], [1, 3 * P]]))],
                          uses={u0 + i: i * NT + 1 for i in range(3)})
                    head_norm("nsa_q", [([heads(qn)], heads(q), heads(sq), st, gain("q_gain"), HD ** -0.5)])
                    turn_into("nsa_qturn", qn, NH // 2, qT)
                groups = []
                for t in range(NT):
                    yt = y[:, t, :].rearrange("p (h d) -> p h d", d=HD)
                    x0 = P * (1 - t)
                    for n, b in enumerate(("c", "s", "w")):
                        grp = dict(
                            heads=[*range(0, NH, 2), *range(1, NH, 2)], slot=t * 3 + n, out=yt, add=n > 0,
                            q=lambda h, t=t: qT[(h % 2) * HD:(h % 2 + 1) * HD, h // 2, t * P:(t + 1) * P],
                            factors=[gates[:, t, :, n]])
                        if b == "c":
                            grp["factors"].append(c_("cmp_rows")[:, t:t + 1].broadcast_to([P, NH]))
                            grp.update(per=3, keys=[NC],
                                       k=lambda h: sh["kcT"][(h % 2) * HD:(h % 2 + 1) * HD, h // HPG, :],
                                       v=lambda h, kt: sh["vc"][:, h // HPG, :],
                                       bias=lambda h, x0=x0: dist[:, h, x0 + CMP_L - 1:x0 + CMP_L + (NC - 1) * CMP_S:CMP_S])
                        else:
                            nk = (t + 1) * P
                            grp.update(per=3 - t, keys=[P] * (t + 1),
                                       k=lambda h, b=b, nk=nk: sh["kT"][b][(h % 2) * HD:(h % 2 + 1) * HD, h // HPG, 0:nk],
                                       v=lambda h, kt, b=b: sh["v"][b][:, kt, (h // HPG) * HD:(h // HPG + 1) * HD],
                                       bias=lambda h, x0=x0, nk=nk: dist[:, h, x0:x0 + nk])
                        groups.append(grp)
                attention("nsa", groups, sums)
                turn_into("nsa_yturn", y, CONV_CH // P, cat)
                memory_attention(1, mq, cat, CONV_CH // P)
                add_projection("out1", unit["out1"], cat)


        def rwkv(ya):
            with ExitStack() as on:
                lora = sb("rw_lora", [P, 2, S], on=on)
                v = sb("rw_v", [P, RC, S], on=on)
                r = sb("rw_r", [P, RC, S], on=on)
                k = sb("rw_kraw", [P, RC, S], on=on)
                u0 = unit["rwkv"]
                with ExitStack() as on2:
                    shifted = sb("rw_shifted", [P, 2, S + 1], on=on2)
                    raw = lambda j: (r, k, v, lora)[j // RC][:, j % RC, :]

                    def consume(eng, j, bank, chain, vector):
                        if j == 0:
                            chain(eng.memset(shifted[:, :, 0:1], 0.0))
                        sh = shifted[:, j % 2]
                        chain(eng.tensor_scalar(sh[:, 1:], bank[:, 0:S], col("mu", j), None, ALU.mult))
                        chain(eng.tensor_tensor(raw(j), bank[:, 0:S], sh[:, 1:], ALU.subtract))
                        return eng.tensor_tensor(raw(j), raw(j), sh[:, 0:S], ALU.add)

                    n_ch = R_COLS // P
                    split_stage("rwkv_in", feature_products(u0, n_ch), consume, hT, on_vector=lambda j: True)
                qr = sb("rw_qr", [P, RC, NT, 2 * P], on=on)
                bh = sb("rw_b", [P, RC, S], on=on)
                kh = sb("rw_k", [P, RC, S], on=on)
                kk = sb("rw_kk", [P, RC, S], on=on)
                mid = sb("rw_mid", [P, 4, RC * NT], on=on)
                carry = sb("rw_carry", [P, 2, RC], on=on)
                with ExitStack() as on2:
                    dec = sb("rw_dec", [P, RC, S], on=on2)
                    aa = sb("rw_a", [P, RC, S], on=on2)
                    tmp = sb("rw_tmp", [P, RC, S], on=on2)
                    sums = sb("rw_sums", [P, RC, NT, P + 1], on=on2)
                    w_da = sums[:, :, :, :].rearrange("p c t n -> p (c t n)")[:, 0:RW]
                    landed = sem("lora_weights_landed")
                    with meeting() as block:
                        @block.sync
                        def _(sp):
                            sp.dma_start(w_da[0:LORA, :], a["rwkv_w_decay_2"][0]).then_inc(landed, 16)
                            sp.dma_start(w_da[LORA:P, :], a["rwkv_w_a_2"][0]).then_inc(landed, 16)
                            sp.wait_ge(landed, 32)

                        @block.scalar
                        def _(act):
                            act.activation(lora[0:LORA, 0, :], lora[0:LORA, 0, :], ACT.Tanh)
                            act.activation(lora[:, 1, :], lora[:, 1, :], ACT.Sigmoid)

                        @block.vector
                        def _(dve):
                            for c in range(RC):
                                dve.tensor_scalar(kk[:, c, :], k[:, c, :], col("k_k", c), None, ALU.mult)

                    def lora_up(pe, j, bank):
                        which, c = divmod(j, RC)
                        lo = which * LORA
                        return pe.matmul(bank[:, 0:S], w_da[lo:lo + LORA, c * P:(c + 1) * P],
                                         lora[lo:lo + LORA, 0, :], start=True, stop=True)

                    stage("lora_up", 2 * RC, lora_up, lambda eng, j, bank, chain, vector:
                          eng.activation((dec, aa)[j // RC][:, j % RC, :], bank[:, 0:S], ACT.Sigmoid,
                                         bias=col(("w0", "a0")[j // RC], j % RC)), on_vector=lambda j: False)

                    flat = lambda z: z[:, :, :].rearrange("p c s -> p (c s)")
                    squares, lengths, roots, made, made_k = \
                        (sem("kk_" + s) for s in ("squares", "lengths", "roots", "made", "made_k"))
                    with meeting() as block:
                        @block.scalar
                        def _(act):
                            act.activation(flat(tmp), flat(kk), ACT.Square).then_inc(squares, 1)
                            for b in range(4):
                                act.wait_ge(lengths, b + 1)
                                act.activation(flat(tmp)[:, b * 512:(b + 1) * 512], ps[:, b], ACT.Sqrt).then_inc(roots, 1)

                        @block.tensor
                        def _(pe):
                            pe.wait_ge(squares, 1)
                            for b in range(4):
                                pe.matmul(ps[:, b], c_("headones"), flat(tmp)[:, b * 512:(b + 1) * 512],
                                          start=True, stop=True).then_inc(lengths, 1)

                        @block.vector
                        def _(dve):
                            chain = Chain(dve, made)
                            chain(dve.memset(sums[:, :, :, 0:1], 0.0))
                            for c in range(RC):
                                for t in range(NT):
                                    dve.tensor_tensor_scan(sums[:, c, t, 1:], c_("ones"), dec[:, c, t * P:(t + 1) * P],
                                                           0.0, ALU.mult, ALU.add)
                            dve.wait_ge(roots, 4)
                            chain(dve.tensor_scalar(flat(tmp), flat(tmp), 1e-12, None, ALU.max))
                            chain(dve.reciprocal(flat(dec), flat(tmp)))
                            chain(dve.tensor_tensor(flat(kk), flat(kk), flat(dec), ALU.mult))
                            middle = sums[:, :, :, P // 2].rearrange("p c t -> p (c t)")
                            dve.tensor_scalar(mid[:, 0, :], middle, KAPPA, None, ALU.mult)
                            chain(dve.tensor_scalar(mid[:, 1, :], middle, -KAPPA, None, ALU.mult))
                            chain(dve.tensor_tensor(carry[:, 1, :], sums[:, :, 0, P // 2], sums[:, :, 0, P], ALU.subtract))
                            chain(dve.tensor_tensor(carry[:, 1, :], carry[:, 1, :], sums[:, :, 1, P // 2], ALU.subtract))
                            dve.tensor_tensor(flat(bh), flat(kk), flat(aa), ALU.mult)

                        @block.gpsimd
                        def _(pool):
                            chain = Chain(pool, made_k)
                            chain(pool.tensor_scalar(mid[:, 2, 0:RC], col("k_a", 0, RC), -1.0, 1.0, ALU.mult, ALU.add))
                            for c in range(RC):
                                last = pool.tensor_scalar(kh[:, c, :], aa[:, c, :], col("k_a", c), mid[:, 2, c:c + 1],
                                                          ALU.mult, ALU.add)
                            chain(last)
                            pool.tensor_tensor(flat(kh), flat(kh), flat(k), ALU.mult)

                    exps, scaled = sem("rw_exps"), sem("rw_scaled")
                    with meeting() as block:
                        @block.scalar
                        def _(act):
                            act.activation(carry[:, 0, :], carry[:, 1, :], ACT.Exp, scale=KAPPA)
                            for c in range(RC):
                                for t in range(NT):
                                    n = c * NT + t
                                    act.activation(qr[:, c, t, 0:P], sums[:, c, t, 0:P], ACT.Exp,
                                                   scale=-KAPPA, bias=mid[:, 0, n:n + 1])
                                    act.activation(qr[:, c, t, P:], sums[:, c, t, 1:], ACT.Exp,
                                                   scale=-KAPPA, bias=mid[:, 0, n:n + 1])
                                    act.activation(tmp[:, c, t * P:(t + 1) * P], sums[:, c, t, 1:], ACT.Exp,
                                                   scale=KAPPA, bias=mid[:, 1, n:n + 1]).then_inc(exps, 1)

                        @block.vector
                        def _(dve):
                            for c in range(RC):
                                dve.scalar_tensor_tensor(dec[:, c, :], r[:, c, :], col("r_k", c), kh[:, c, :],
                                                         ALU.mult, ALU.mult).then_inc(scaled, 1)
                            for c in range(RC):
                                dve.wait_ge(scaled, c + 1)
                                dve.wait_ge(exps, NT * (c + 1))
                                tiles = lambda z: z[:, c, :].rearrange("p (t s) -> p t s", t=NT)
                                dve.tensor_tensor(qr[:, c, :, 0:P], qr[:, c, :, 0:P], tiles(kk), ALU.mult)
                                dve.tensor_tensor(qr[:, c, :, P:], qr[:, c, :, P:], tiles(r), ALU.mult)
                                dve.tensor_tensor(bh[:, c, :], bh[:, c, :], tmp[:, c, :], ALU.mult)
                                dve.tensor_tensor(kh[:, c, :], kh[:, c, :], tmp[:, c, :], ALU.mult)
                                dve.wait_ge(scaled, RC)
                    with meeting() as block:
                        @block.vector
                        def _(dve):
                            dve.tensor_copy(flat(kk), flat(dec))
                v_tok = r[:, :, :].rearrange("p c s -> p (c s)").rearrange("p (t n) -> p t n", t=NT)
                b_tok, k_tok = (k[:, :, :].rearrange("p c s -> p (c s)")[:, i * RW:(i + 1) * RW] for i in range(2))
                bonus = sb("rw_bonus", [P, NT, RH], on=on)
                turns = [(v, 0, v_tok[:, 0, :]), (v, 1, v_tok[:, 1, :]), (bh, 0, b_tok), (kh, 0, k_tok)]

                def turn(pe, j, bank):
                    if j == 8:
                        for t in range(NT):
                            for c in range(RC):
                                lo = t * RH + 2 * c
                                mm = pe.matmul(bank[:, lo:lo + 2], kk[:, c, t * P:(t + 1) * P], c_("headsel"),
                                               start=True, stop=True)
                        return mm
                    src, t, _ = turns[j // 2]
                    for i in range(4):
                        mm = pe.transpose(bank[:, i * P:(i + 1) * P], src[:, (j % 2) * 4 + i, t * P:(t + 1) * P], ident)
                    return mm

                def take(eng, j, bank, chain, vector):
                    if j == 8:
                        return copy(eng, vector, bonus[:, :, :], bank[:, 0:NT * RH].rearrange("p (t h) -> p t h", t=NT))
                    return copy(eng, vector, turns[j // 2][2][:, (j % 2) * 512:(j % 2 + 1) * 512], bank)

                stage("rw_turn", 9, turn, take)
                with ExitStack() as on2:
                    rwkv_tiles(on2, qr, bh, kh, v_tok, b_tok, k_tok, carry, ya)
                rwkv_out(ya, v_tok, bonus, lora)

        def rwkv_tiles(on, qr, bh, kh, v_tok, b_tok, k_tok, carry, ya):
            ac = sb("rw_ac", [P, 2, 4, 2 * P], on=on)
            bd = sb("rw_bd", [P, 2, 4, 2 * P], on=on)
            inv = sb("rw_inv", [P, 2, 4, P], on=on)
            invT = sb("rw_invT", [P, 2, 4, P], on=on)
            half = sb("rw_half", [P, 2, 4, P], on=on)
            w = sb("rw_w", [P, 2, P], on=on)
            uu = sb("rw_u", [P, 2, P], on=on)
            state = sb("rw_state", [P, 2, HD], on=on)
            levels = 7
            n_steps = 2 * levels + 6
            made, taken, chain_sem = sem("rw_made"), sem("rw_taken"), sem("rw_chain")
            hp_rows = lambda hp: slice(hp * HD, (hp + 1) * HD)

            def level(i):
                return c_("levels")[:, i * P:(i + 1) * P].unsqueeze(1).broadcast_to([P, 4, P])

            def products(pe, c, p, s):
                bank = lambda b: ps[:, 4 * p + b]
                four = lambda b: bank(b).rearrange("p (u n) -> p u n", u=4)
                hcols = lambda hp: slice((2 * c + hp) * HD, (2 * c + hp + 1) * HD)
                if s == 0:
                    for n, left in enumerate((bh, kh)):
                        for t in range(NT):
                            for hp in range(2):
                                mm = pe.matmul(bank(2 * n + hp)[:, t * 2 * P:(t + 1) * 2 * P],
                                               left[hp_rows(hp), c, t * P:(t + 1) * P], qr[hp_rows(hp), c, t, :],
                                               start=True, stop=True)
                    return mm
                if s == 1:
                    for u in range(4):
                        mm = pe.transpose(four(0)[:, u], invT[:, p, u], ident)
                    return mm
                if s < 2 * levels:
                    for u in range(4):
                        if s % 2 == 0:
                            mm = pe.matmul(four(1)[:, u], ac[:, p, u, 0:P], inv[:, p, u], start=True, stop=True)
                        else:
                            if s < 2 * levels - 1:
                                pe.matmul(four(2)[:, u], invT[:, p, u], half[:, p, u], start=True, stop=True)
                            mm = pe.matmul(four(3)[:, u], half[:, p, u], invT[:, p, u], start=True, stop=True)
                    return mm
                s -= 2 * levels
                for hp in range(2):
                    t = 0 if s < 3 else 1
                    u = 2 * hp + t
                    vt = v_tok[:, t, hcols(hp)]
                    us = uu[:, p, hp * HD:(hp + 1) * HD]
                    cols2 = slice(hp * HD, (hp + 1) * HD)
                    q_, r_ = qr[hp_rows(hp), c, 1, 0:P], qr[hp_rows(hp), c, 1, P:]
                    st = state[hp_rows(hp), p, :]
                    if s == 0:
                        mm = pe.matmul(bank(0)[:, cols2], bd[:, p, u, 0:P], vt, start=True, stop=True)
                    elif s in (1, 4):
                        mm = pe.matmul(bank(2)[:, cols2], invT[:, p, u], w[:, p, cols2], start=True, stop=True)
                    elif s == 2:
                        pe.matmul(bank(0)[:, cols2], ac[:, p, u, P:], us, start=True, stop=False)
                        pe.matmul(bank(0)[:, cols2], bd[:, p, u, P:], vt, start=False, stop=True)
                        pe.matmul(bank(3)[hp_rows(hp), 0:HD], b_tok[:, hcols(hp)], us, start=True, stop=False)
                        mm = pe.matmul(bank(3)[hp_rows(hp), 0:HD], k_tok[:, hcols(hp)], vt, start=False, stop=True)
                    elif s == 3:
                        pe.matmul(bank(hp)[:, 0:HD], q_, st, start=True, stop=False)
                        mm = pe.matmul(bank(hp)[:, 0:HD], bd[:, p, u, 0:P], vt, start=False, stop=True)
                    else:
                        pe.matmul(bank(hp)[:, 0:HD], r_, st, start=True, stop=False)
                        pe.matmul(bank(hp)[:, 0:HD], ac[:, p, u, P:], us, start=False, stop=False)
                        mm = pe.matmul(bank(hp)[:, 0:HD], bd[:, p, u, P:], vt, start=False, stop=True)
                return mm

            def results(dve, chain, c, p, s):
                bank = lambda b: ps[:, 4 * p + b]
                four = lambda b: bank(b).rearrange("p (u n) -> p u n", u=4)
                if s == 0:
                    mask = c_("strict_incl").unsqueeze(1).broadcast_to([P, NT, 2 * P])
                    for n, dst in enumerate((ac, bd)):
                        for hp in range(2):
                            last = dve.tensor_tensor(dst[:, p, 2 * hp:2 * hp + 2, :],
                                                     bank(2 * n + hp).rearrange("p (t n) -> p t n", t=NT), mask, ALU.mult)
                    chain(last)
                    chain(dve.tensor_tensor(half[:, p], ac[:, p, :, 0:P], level(0), ALU.mult))
                    return dve.tensor_tensor(invT[:, p], ident.unsqueeze(1).broadcast_to([P, 4, P]), half[:, p],
                                             ALU.subtract)
                if s == 1:
                    return dve.tensor_copy(inv[:, p], four(0))
                if s < 2 * levels:
                    if s % 2 == 0:
                        return dve.tensor_tensor(half[:, p], four(1), level(s // 2), ALU.mult)
                    if s < 2 * levels - 1:
                        dve.tensor_tensor(inv[:, p], inv[:, p], four(2), ALU.subtract)
                    return dve.tensor_tensor(invT[:, p], invT[:, p], four(3), ALU.subtract)
                s -= 2 * levels
                t = 0 if s < 3 else 1
                if s == 0:
                    return dve.tensor_scalar(w[:, p, :], bank(0)[:, 0:P], -1.0, None, ALU.mult)
                if s in (1, 4):
                    return dve.tensor_copy(uu[:, p, :], bank(2)[:, 0:P])
                if s == 2:
                    dve.tensor_copy(ya[:, 0, c * P:(c + 1) * P], bank(0)[:, 0:P])
                    return dve.tensor_scalar(state[:, p, :], bank(3)[:, 0:HD], carry[:, 0, c:c + 1], None, ALU.mult)
                for hp in range(2):
                    cols2 = slice(hp * HD, (hp + 1) * HD)
                    if s == 3:
                        last = dve.tensor_scalar(w[:, p, cols2], bank(hp)[:, 0:HD], -1.0, None, ALU.mult)
                    else:
                        last = dve.tensor_copy(ya[:, 1, c * P + hp * HD:c * P + (hp + 1) * HD], bank(hp)[:, 0:HD])
                return last

            order = [(2 * i + p, p, s) for i in range(RC // 2) for s in range(n_steps) for p in range(2)]
            with meeting() as block:
                @block.tensor
                def _(pe):
                    for n, (c, p, s) in enumerate(order):
                        if n >= 2:
                            pe.wait_ge(taken, n - 1)
                        products(pe, c, p, s).then_inc(made, 1)

                @block.vector
                def _(dve):
                    chain = Chain(dve, chain_sem)
                    for n, (c, p, s) in enumerate(order):
                        dve.wait_ge(made, n + 1)
                        if n >= 2:
                            dve.wait_ge(taken, n - 1)
                        results(dve, chain, c, p, s).then_inc(taken, 1)

        def rwkv_out(ya, v_tok, bonus, lora):
            with ExitStack() as on:
                w_g = sb("rw_wg", [P, RW], on=on)
                ln = sb("rw_ln", [P, 2, RW], on=on)
                gate = sb("rw_gate", [P, NT, RW], on=on)
                sq = sb("rw_sq", [P, NT, RW], on=on)
                st = sb("rw_gn", [P, 3, NT, RH], on=on)
                landed = sem("rw_out_landed")
                added = sb("rw_added", [P, NT, RW], on=on)
                centred, squared, rooted, work, extras = \
                    (sem("gn_" + s) for s in ("centred", "squared", "rooted", "work", "extras"))
                yh, sh_, vh = heads(ya), heads(sq), heads(v_tok)
                shape = [P, NT, RH, HD]
                wide = lambda z: z.unsqueeze(3).broadcast_to(shape)
                rows = lambda z: z.unsqueeze(1).broadcast_to([P, NT, RW])
                with meeting() as block:
                    @block.sync
                    def _(sp):
                        sp.dma_start(w_g[:, :], a["rwkv_w_g_2"][0]).then_inc(landed, 16)
                        sp.dma_start(ln[:, 0, :], everywhere(a["rwkv_ln_g_2"], RW)).then_inc(landed, 16)
                        sp.dma_start(ln[:, 1, :], everywhere(a["rwkv_ln_b_2"], RW)).then_inc(landed, 16)

                    @block.tensor
                    def _(pe):
                        pe.wait_ge(landed, 48)
                        for t in range(NT):
                            for h in range(2):
                                mm = pe.matmul(ps[:, 2 * t + h], lora[:, 1, t * P:(t + 1) * P],
                                               w_g[:, h * UC:(h + 1) * UC], start=True, stop=True)
                        mm.then_inc(squared, 1)

                    @block.scalar
                    def _(act):
                        act.wait_ge(squared, 1)
                        act.activation(gate[:, :, :], ps[:, 0:4].rearrange("p (t b) n -> p t (b n)", t=NT), ACT.Copy)\
                            .then_inc(squared, 1)
                        act.wait_ge(centred, 1)
                        act.activation(sh_, yh, ACT.Square).then_inc(squared, 1)
                        act.wait_ge(centred, 2)
                        act.activation(st[:, 2], st[:, 1], ACT.Sqrt).then_inc(rooted, 1)

                    @block.vector
                    def _(dve):
                        chain = Chain(dve, work)
                        chain(dve.tensor_reduce(st[:, 0], yh, AX.X, ALU.add))
                        chain(dve.tensor_scalar(st[:, 0], st[:, 0], 1.0 / HD, None, ALU.mult))
                        dve.tensor_tensor(yh, yh, wide(st[:, 0]), ALU.subtract).then_inc(centred, 1)
                        dve.wait_ge(squared, 3)
                        chain(dve.tensor_reduce(st[:, 1], sh_, AX.X, ALU.add))
                        dve.tensor_scalar(st[:, 1], st[:, 1], 1.0 / HD, GN_EPS, ALU.mult, ALU.add).then_inc(centred, 1)
                        dve.wait_ge(rooted, 1)
                        chain(dve.reciprocal(st[:, 0], st[:, 2]))
                        chain(dve.tensor_tensor(yh, yh, wide(st[:, 0]), ALU.mult))
                        dve.wait_ge(extras, 4)
                        chain(dve.tensor_tensor(ya[:, :, :], ya[:, :, :], gate[:, :, :], ALU.mult))
                        dve.tensor_tensor(ya[:, :, :], ya[:, :, :], added[:, :, :], ALU.add)

                    @block.gpsimd
                    def _(pool):
                        chain = Chain(pool, extras)
                        chain(pool.tensor_tensor(heads(added), vh, wide(bonus[:, :, :]), ALU.mult))
                        pool.wait_ge(landed, 48)
                        chain(pool.tensor_tensor(added[:, :, :], added[:, :, :], rows(ln[:, 1, :]), ALU.add))
                        pool.wait_ge(squared, 2)
                        chain(pool.tensor_tensor(added[:, :, :], added[:, :, :], gate[:, :, :], ALU.mult))
                        chain(pool.tensor_tensor(gate[:, :, :], gate[:, :, :], rows(ln[:, 0, :]), ALU.mult))

        def ssd(u_out):
            HG = SH // SG
            GW = SW // SG
            with ExitStack() as on:
                bc = sb("ssd_bc", [P, 2 * SG, S], on=on)
                xs = sb("ssd_x", [P, NT, SW], on=on)
                dts = sb("ssd_dt", [SH, 6, S], on=on)
                dt_tok = sb("ssd_dt_tok", [P, 2, NT, SH], on=on)
                u0, ud = unit["xbc"], unit["dt"]
                with ExitStack() as on2:
                    xT = sb("ssd_xT", [P, SW // P, S], on=on2)
                    nx, nb = SW // P, 2 * SG
                    part = lambda j: xT[:, j, :] if j < nx else bc[:, j - nx, :]

                    def produce(pe, j, bank):
                        if j == nx + nb:
                            stream.arrived(pe, ud)
                            return feature_chunk(pe, ud, 0, SH, bank[0:SH, 0:S])
                        if j % 4 == 0:
                            stream.arrived(pe, u0 + j // 4)
                        return feature_chunk(pe, u0 + j // 4, (j % 4) * P, P, bank[:, 0:S])

                    def consume(eng, j, bank, chain, vector):
                        if j == nx + nb:
                            return eng.tensor_scalar(dts[:, 0, :], bank[0:SH, 0:S], ssd_cols[:, 0:1], None, ALU.add)
                        d = part(j)
                        chain(eng.tensor_scalar(d, bank[:, 0:S], col("ssd_conv_w", 3 * (nx + nb) + j),
                                                col("ssd_conv_b", j), ALU.mult, ALU.add))
                        for tap in (2, 1, 0):
                            back = 3 - tap
                            last = eng.scalar_tensor_tensor(d[:, back:], bank[:, 0:S - back],
                                                            col("ssd_conv_w", tap * (nx + nb) + j), d[:, back:],
                                                            ALU.mult, ALU.add)
                            if tap:
                                chain(last)
                        return last

                    stage("xbc", nx + nb + 1, produce, consume, on_vector=lambda j: True,
                          uses={**{u0 + i: 4 * i + 3 for i in range(6)}, ud: nx + nb})

                    work, acted = sem("dt_work"), sem("dt_acted")
                    z_, e_, u_, d_, l_, out_ = (dts[:, i, :] for i in range(6))
                    with meeting() as block:
                        @block.scalar
                        def _(act):
                            act.activation(e_, z_, ACT.Abs).then_inc(acted, 1)
                            act.wait_ge(acted, 1)
                            act.activation(e_, e_, ACT.Exp, scale=-1.0).then_inc(acted, 1)
                            act.activation(ssd_cols[:, 2:3], ssd_cols[:, 1:2], ACT.Exp).then_inc(acted, 1)
                            act.wait_ge(work, 1)
                            act.activation(l_, u_, ACT.Ln).then_inc(acted, 1)
                            for i in range(0, nx, 4):
                                act.activation(xT[:, i:i + 4, :], xT[:, i:i + 4, :], ACT.Silu)
                            for i in range(0, nb, 4):
                                act.activation(bc[:, i:i + 4, :], bc[:, i:i + 4, :], ACT.Silu)

                        @block.vector
                        def _(dve):
                            chain = Chain(dve, work)
                            dve.wait_ge(acted, 3)
                            chain(dve.tensor_scalar(u_, e_, 1.0, None, ALU.add))
                            chain(dve.tensor_scalar(d_, u_, -1.0, None, ALU.add))
                            chain(dve.tensor_scalar(out_, d_, 0.0, None, ALU.is_equal))
                            chain(dve.tensor_tensor(out_, out_, e_, ALU.mult))
                            chain(dve.tensor_scalar(d_, d_, 1e-30, None, ALU.max))
                            dve.wait_ge(acted, 4)
                            chain(dve.reciprocal(u_, d_))
                            chain(dve.tensor_tensor(e_, e_, u_, ALU.mult))
                            chain(dve.tensor_tensor(e_, e_, l_, ALU.mult))
                            chain(dve.tensor_tensor(e_, e_, out_, ALU.add))
                            chain(dve.tensor_scalar(z_, z_, 0.0, None, ALU.max))
                            chain(dve.tensor_tensor(z_, z_, e_, ALU.add))
                            chain(dve.tensor_scalar(d_, z_, ssd_cols[:, 2:3], -1.0, ALU.mult, ALU.mult))
                            chain(dve.memset(l_, 1.0))
                            dve.tensor_tensor_scan(u_, l_, d_, 0.0, ALU.mult, ALU.add)

                    def turn(pe, j, bank):
                        if j == 8:
                            for i, src in enumerate((z_, u_)):
                                for t in range(NT):
                                    lo = (i * NT + t) * SH
                                    mm = pe.transpose(bank[:, lo:lo + SH], src[:, t * P:(t + 1) * P], ident[0:SH, 0:SH])
                            return mm
                        t, i4 = divmod(j, 4)
                        for i in range(4):
                            mm = pe.transpose(bank[:, i * P:(i + 1) * P], xT[:, i4 * 4 + i, t * P:(t + 1) * P], ident)
                        return mm

                    def take(eng, j, bank, chain, vector):
                        if j == 8:
                            return copy(eng, vector, dt_tok[:, :, :, :],
                                        bank[:, 0:2 * NT * SH].rearrange("p (i t h) -> p i t h", i=2, t=NT))
                        t, i4 = divmod(j, 4)
                        return copy(eng, vector, xs[:, t, i4 * 512:(i4 + 1) * 512], bank)

                    stage("ssd_turn", 9, turn, take, loads=[(acs_row, u_)])

                uz = unit["z"]
                assert GW == UC and HG * 2 == NT * KD
                acs = sb("ssd_acs", [P, 2, HG, S], on=on)
                cb = sb("ssd_cb", [P, SG, 3 * P], on=on)
                xdt = sb("ssd_xdt", [P, 2, NT, GW], on=on)
                seg = sb("ssd_seg", [P, 2, 3 * P], on=on)
                dec = sb("ssd_dec", [P, 2, 3 * P], on=on)
                mix = sb("ssd_mix", [P, 2, 3 * P], on=on)
                xd = sb("ssd_xd", [P, 2, GW], on=on)
                cb_made, cb_taken, rows_in, segs, decs, mixes, xdts, given, finished, chain_sem = \
                    (sem("ssd_" + s) for s in ("cb_made", "cb_taken", "rows_in", "segs", "decs", "mixes", "xdts",
                                               "given", "finished", "chain"))
                rows_in2, z_made, z_opened = sem("ssd_rows_in2"), sem("z_made"), sem("z_opened")
                z_bank = lambda g, t: ps[:, 2 * (g % 2) + t]
                incl = c_("strict_incl")[:, P:]
                per_head = lambda z: z.rearrange("p (h d) -> p h d", d=HD)
                wide = lambda z: z.unsqueeze(2).broadcast_to([P, HG, HD])
                with meeting() as block:
                    @block.sync
                    def _(sp):
                        for g in range(SG):
                            if g >= 2:
                                sp.wait_ge(segs, (g - 1) * HG)
                            sp.dma_start(acs[:, g % 2, :, :], bass.AP(acs_row.tensor, g * HG * S, [[0, P], [1, HG * S]])
                                         .rearrange("p (h s) -> p h s", h=HG)).then_inc((rows_in, rows_in2)[g % 2], 16)
                        for g in range(SG):
                            stream.done[uz + g] = (z_made, NT * (g + 1))
                        stream.prefetch(sp, uz + SG)

                    @block.tensor
                    def _(pe):
                        for g in range(SG):
                            pe.matmul(ps[:, g, 0:S], bc[:, g, 0:P], bc[:, SG + g, :], start=True, stop=True)
                            pe.matmul(ps[:, g, S:3 * P], bc[:, g, P:], bc[:, SG + g, P:], start=True, stop=True)\
                                .then_inc(cb_made, 1)
                        pe.wait_ge(cb_taken, SG)
                        for g in range(SG):
                            w = stream.arrived(pe, uz + g)
                            if g >= 2:
                                pe.wait_ge(finished, g - 1)
                                pe.wait_ge(z_opened, NT * (g - 1))
                            pe.wait_ge(xdts, g + 1)
                            for hg in range(HG):
                                h = g * HG + hg
                                pe.wait_ge(mixes, h + 1)
                                o = [ps[:, 4 + 2 * (g % 2) + t, hg * HD:(hg + 1) * HD] for t in range(NT)]
                                xv = [xdt[:, g % 2, t, hg * HD:(hg + 1) * HD] for t in range(NT)]
                                pe.matmul(o[0], mix[:, h % 2, 0:P], xv[0], start=True, stop=True)
                                pe.matmul(o[1], mix[:, h % 2, P:2 * P], xv[0], start=True, stop=False)
                                pe.matmul(o[1], mix[:, h % 2, 2 * P:], xv[1], start=False, stop=True).then_inc(given, 1)
                                for n in (2 * hg, 2 * hg + 1):
                                    t, k = divmod(n, KD)
                                    mm = pe.matmul(z_bank(g, t), hT[:, k, t * P:(t + 1) * P], w[:, k, :],
                                                   start=(k == 0), stop=(k == KD - 1))
                                if k == KD - 1:
                                    mm.then_inc(z_made, 1)

                    @block.scalar
                    def _(act):
                        def open_z(g):
                            act.wait_ge(z_made, NT * (g + 1))
                            for t in range(NT):
                                act.activation(u_out[:, t, g * GW:(g + 1) * GW], z_bank(g, t), ACT.Silu)\
                                    .then_inc(z_opened, 1)

                        for h in range(SH):
                            if h % HG == 2 and h >= HG:
                                open_z(h // HG - 1)
                            act.wait_ge(segs, h + 1)
                            if h >= 2:
                                act.wait_ge(mixes, h - 1)
                            act.activation(dec[:, h % 2, :], seg[:, h % 2, :], ACT.Exp).then_inc(decs, 1)
                        open_z(SG - 1)

                    @block.vector
                    def _(dve):
                        chain = Chain(dve, chain_sem)
                        for g in range(SG):
                            dve.wait_ge(cb_made, g + 1)
                            dve.tensor_tensor(cb[:, g, 0:P], ps[:, g, 0:P], incl, ALU.mult)
                            dve.tensor_copy(cb[:, g, P:2 * P], ps[:, g, P:2 * P])
                            dve.tensor_tensor(cb[:, g, 2 * P:], ps[:, g, 2 * P:3 * P], incl, ALU.mult)\
                                .then_inc(cb_taken, 1)

                        def differences(h):
                            g, hg = divmod(h, HG)
                            if hg == 0:
                                dve.wait_ge((rows_in, rows_in2)[g % 2], 16 * (g // 2 + 1))
                            if h >= 2:
                                dve.wait_ge(decs, h - 1)
                            dve.tensor_scalar(seg[:, h % 2, 0:S], acs[:, g % 2, hg, :], dt_tok[:, 1, 0, h:h + 1], 0.0,
                                              ALU.subtract, ALU.min)
                            dve.tensor_scalar(seg[:, h % 2, S:], acs[:, g % 2, hg, P:], dt_tok[:, 1, 1, h:h + 1], 0.0,
                                              ALU.subtract, ALU.min).then_inc(segs, 1)

                        def weigh(h):
                            dve.wait_ge(decs, h + 1)
                            if h >= 2:
                                dve.wait_ge(given, h - 1)
                            dve.tensor_tensor(mix[:, h % 2, :], dec[:, h % 2, :], cb[:, h // HG, :], ALU.mult)\
                                .then_inc(mixes, 1)

                        def inputs(g):
                            if g >= 2:
                                dve.wait_ge(given, (g - 1) * HG)
                            for t in range(NT):
                                last = dve.tensor_tensor(per_head(xdt[:, g % 2, t, :]),
                                                         per_head(xs[:, t, g * GW:(g + 1) * GW]),
                                                         wide(dt_tok[:, 0, t, g * HG:(g + 1) * HG]), ALU.mult)
                            last.then_inc(xdts, 1)

                        def finish(g):
                            dve.wait_ge(given, (g + 1) * HG)
                            dve.wait_ge(z_opened, NT * (g + 1))
                            for t in range(NT):
                                cols_g = slice(g * GW, (g + 1) * GW)
                                chain(dve.tensor_tensor(per_head(xd[:, t, :]), per_head(xs[:, t, cols_g]),
                                                        wide(gain("d_skip", g * HG, HG)), ALU.mult))
                                chain(dve.tensor_tensor(xd[:, t, :], xd[:, t, :], ps[:, 4 + 2 * (g % 2) + t], ALU.add))
                                last = dve.tensor_tensor(u_out[:, t, cols_g], u_out[:, t, cols_g], xd[:, t, :], ALU.mult)
                            last.then_inc(finished, 1)

                        dve.wait_ge(cb_taken, SG)
                        differences(0)
                        for h in range(SH):
                            if h % HG == 0:
                                inputs(h // HG)
                            if h + 1 < SH:
                                differences(h + 1)
                            weigh(h)
                            if h % HG == 3 and h >= HG:
                                finish(h // HG - 1)
                        finish(SG - 1)

                sums, scaled, rooted = sem("sn_sums"), sem("sn_scaled"), sem("sn_rooted")
                st = sb("ssd_st", [P, 3, NT, SG], on=on)
                junk = xs
                with meeting() as block:
                    @block.scalar
                    def _(act):
                        for t in range(NT):
                            for g in range(SG):
                                act.activation(junk[:, t, g * GW:(g + 1) * GW], u_out[:, t, g * GW:(g + 1) * GW],
                                               ACT.Square, accum_out=st[:, 0, t, g:g + 1]).then_inc(sums, 1)
                        act.wait_ge(scaled, 1)
                        act.activation(st[:, 2], st[:, 1], ACT.Sqrt).then_inc(rooted, 1)

                    @block.vector
                    def _(dve):
                        dve.wait_ge(sums, NT * SG)
                        dve.tensor_scalar(st[:, 1], st[:, 0], 1.0 / GW, EPS, ALU.mult, ALU.add).then_inc(scaled, 1)
                        dve.wait_ge(rooted, 1)
                        dve.reciprocal(st[:, 0], st[:, 2]).then_inc(scaled, 1)
                        dve.wait_ge(scaled, 2)
                        for t in range(NT):
                            v = u_out[:, t, :].rearrange("p (g n) -> p g n", g=SG)
                            dve.tensor_tensor(v, v, st[:, 0, t, :].unsqueeze(2).broadcast_to([P, SG, GW]), ALU.mult)

        def project(name, u0, src, dst, parts=1, pair=None, depth=3, loads=()):
            units = [(u0 + half * parts + r, r * KD, [(half * NT + t, "token", 0, UC, t, r == 0, r == parts - 1)
                                                      for t in range(NT)])
                     for half in range(2) for r in range(parts)]
            split_stage(name, units, lambda eng, j, bank, chain, vector:
                        copy(eng, vector, dst[:, j % NT, (j // NT) * UC:(j // NT + 1) * UC], bank),
                        src, pair=pair, depth=depth, loads=loads)

        def merge(by_a, by_b, bias, gates):
            with ExitStack() as on:
                ug = unit["gate"]

                cols_of = lambda j: slice((j // NT) * UC, (j // NT + 1) * UC)
                gate_of = lambda j: gates[:, j % NT, cols_of(j)]

                def weigh(dve, j, chain):
                    branch, half = divmod(j // NT, 2)
                    part = lambda by: by[:, j % NT, half * UC:(half + 1) * UC]
                    src = part((by_a, by_b)[branch])
                    chain(dve.tensor_tensor(src, src, gate_of(j), ALU.mult))
                    if branch:
                        dve.tensor_tensor(part(by_a), part(by_a), src, ALU.add)

                split_stage("gate", token_products(ug, 4), lambda eng, j, bank, chain, vector:
                            eng.tensor_tensor(gate_of(j), bank, bias[:, cols_of(j)], ALU.add),
                            hT, on_vector=lambda j: True,
                            act_then=lambda act, j: act.activation(gate_of(j), gate_of(j), ACT.Sigmoid),
                            dve_then=weigh)
            with ExitStack() as on:
                mT = sb("mergedT", [P, KD, S], on=on)
                turn_into("merge_turn", by_a, KD, mT)
                add_projection("out2", unit["out2"], mT)

        def router(flag, scaled, h_tok, rank):
            NR = NG + NE
            with ExitStack() as on:
                wr = sb("w_router", [P, KD, NR], on=on)
                lg = sb("router_logits", [P, NT, NR], on=on)
                gsel = sb("r_gsel", [P, NT, NG], on=on)
                t4 = sb("r_t4", [P, NT, NG], on=on)
                el = sb("r_el", [P, NT, EPG, NG], on=on)
                pr = sb("r_pr", [P, NT, EPG], on=on)
                left = sb("r_left", [P, NT, EPG], on=on)
                one = sb("r_one", [P, 2, NT, EPG], on=on)
                t8 = sb("r_t8", [P, NT, EPG], on=on)
                s1 = sb("r_s1", [P, 8, NT], on=on)
                dense = sb("r_dense", [P, NT, NG, EPG], on=on)
                mask = sb("r_mask", [P, NT, NG, EPG], on=on)
                late = sb("r_late", [P, NT, NE], on=on)
                late_any = sb("r_late_any", [P, 1], on=on)
                rows = sb("r_rows", [NE, 3, S], on=on)
                row = sb("r_gain", [P, D], on=on)
                landed = sem("router_landed")
                with meeting() as block:
                    @block.sync
                    def _(sp):
                        for lo, w in ((0, a["w_router_group_2"][0]), (NG, a["w_router_expert_2"][0])):
                            n = w.shape[1]
                            sp.dma_start(wr[:, :, lo:lo + n], w.rearrange("(k p) c -> p k c", p=P)).then_inc(landed, 16)
                        sp.dma_start(row[:, :], everywhere(a["ffn_norm_g_2"], D)).then_inc(landed, 16)
                        sp.wait_ge(landed, 48)

                def produce(pe, j, bank):
                    for k in range(KD):
                        mm = pe.matmul(bank[:, 0:NR], hT[:, k, j * P:(j + 1) * P], wr[:, k, :], start=(k == 0),
                                       stop=(k == KD - 1))
                    return mm

                stage("router", NT, produce, lambda eng, j, bank, chain, vector:
                      eng.tensor_tensor(lg[:, j, :], bank[:, 0:NR], gains[:, g_at["b_rg"][0]:g_at["b_rg"][0] + NR],
                                        ALU.add), on_vector=lambda j: True)
                work, asked, acted = sem("r_work"), sem("r_asked"), sem("r_acted")
                gl = lg[:, :, 0:NG]
                shape4, shape8 = [P, NT, NG], [P, NT, EPG]
                over = lambda v, shape: v.unsqueeze(2).broadcast_to(shape)
                with meeting() as block:
                    @block.scalar
                    def _(act):
                        act.wait_ge(asked, 1)
                        act.activation(t4[:, :, :], t4[:, :, :], ACT.Exp).then_inc(acted, 1)
                        act.wait_ge(asked, 2)
                        act.activation(pr[:, :, :], pr[:, :, :], ACT.Exp).then_inc(acted, 1)

                    @block.vector
                    def _(dve):
                        chain = Chain(dve, work)

                        def first_max(dst, src, top, desc, shape, scratch, s_top):
                            chain(dve.tensor_reduce(top, src, AX.X, ALU.max))
                            chain(dve.tensor_tensor(dst, src, over(top, shape), ALU.is_equal))
                            chain(dve.tensor_tensor(dst, dst, desc.unsqueeze(1).broadcast_to(shape), ALU.mult))
                            chain(dve.tensor_reduce(s_top, dst, AX.X, ALU.max))
                            chain(dve.tensor_tensor(dst, dst, over(s_top, shape), ALU.is_equal))

                        first_max(gsel[:, :, :], gl, s1[:, 0, :], c_("desc4"), shape4, None, s1[:, 1, :])
                        dve.tensor_tensor(t4[:, :, :], gl, over(s1[:, 0, :], shape4), ALU.subtract).then_inc(asked, 1)
                        for t in range(NT):
                            chain(dve.tensor_tensor(el[:, t], lg[:, t, NG:].rearrange("p (g e) -> p e g", g=NG),
                                                    gsel[:, t, :].unsqueeze(1).broadcast_to([P, EPG, NG]), ALU.mult))
                        chain(dve.tensor_reduce(left[:, :, :], el[:, :, :, :], AX.X, ALU.add))
                        chain(dve.tensor_reduce(s1[:, 2, :], left[:, :, :], AX.X, ALU.max))
                        dve.tensor_tensor(pr[:, :, :], left[:, :, :], over(s1[:, 2, :], shape8), ALU.subtract)\
                            .then_inc(asked, 1)
                        dve.wait_ge(acted, 1)
                        chain(dve.tensor_reduce(s1[:, 3, :], t4[:, :, :], AX.X, ALU.add))
                        dve.wait_ge(acted, 2)
                        chain(dve.tensor_reduce(s1[:, 4, :], pr[:, :, :], AX.X, ALU.add))
                        chain(dve.reciprocal(s1[:, 5, :], s1[:, 4, :]))
                        chain(dve.tensor_tensor(pr[:, :, :], pr[:, :, :], over(s1[:, 5, :], shape8), ALU.mult))
                        first_max(one[:, 0], pr[:, :, :], s1[:, 0, :], c_("desc8"), shape8, None, s1[:, 1, :])
                        chain(dve.tensor_scalar(t8[:, :, :], one[:, 0], -2.0, None, ALU.mult))
                        chain(dve.tensor_tensor(left[:, :, :], pr[:, :, :], t8[:, :, :], ALU.add))
                        first_max(one[:, 1], left[:, :, :], s1[:, 2, :], c_("desc8"), shape8, None, s1[:, 1, :])
                        chain(dve.tensor_tensor(s1[:, 4, :], s1[:, 0, :], s1[:, 2, :], ALU.add))
                        chain(dve.tensor_tensor(s1[:, 4, :], s1[:, 4, :], s1[:, 3, :], ALU.mult))
                        chain(dve.reciprocal(s1[:, 5, :], s1[:, 4, :]))
                        chain(dve.tensor_tensor(one[:, 0], one[:, 0], one[:, 1], ALU.add))
                        for t in range(NT):
                            chain(dve.tensor_tensor(mask[:, t], one[:, 0, t, :].unsqueeze(1).broadcast_to([P, NG, EPG]),
                                              gsel[:, t, :].unsqueeze(2).broadcast_to([P, NG, EPG]), ALU.mult))
                        chain(dve.tensor_tensor(one[:, 0], one[:, 0], pr[:, :, :], ALU.mult))
                        chain(dve.tensor_tensor(one[:, 0], one[:, 0], over(s1[:, 5, :], shape8), ALU.mult))
                        for t in range(NT):
                            dve.tensor_tensor(dense[:, t], one[:, 0, t, :].unsqueeze(1).broadcast_to([P, NG, EPG]),
                                              gsel[:, t, :].unsqueeze(2).broadcast_to([P, NG, EPG]), ALU.mult)

                flat = lambda v, t: v[:, t].rearrange("p g e -> p (g e)")
                counted, ranked, turned, split, taken, stored, work2 = \
                    (sem("r_" + n) for n in ("counted", "ranked", "turned", "split", "taken", "rows_stored", "work2"))
                before = c_("strict_incl")[:, 0:P]
                with meeting() as block:
                    @block.tensor
                    def _(pe):
                        pe.matmul(ps[:, 0, 0:NE], before, flat(mask, 0), start=True, stop=True)
                        pe.matmul(ps[:, 0, NE:2 * NE], c_("ones"), flat(mask, 0), start=True, stop=False)
                        pe.matmul(ps[:, 0, NE:2 * NE], before, flat(mask, 1), start=False, stop=True)\
                            .then_inc(counted, 1)
                        pe.wait_ge(ranked, 3)
                        for n, src in enumerate((rank[:, :, :], dense[:, :].rearrange("p t g e -> p t (g e)"), late[:, :, :])):
                            for t in range(NT):
                                mm = pe.transpose(ps[0:NE, 1 + n, t * P:(t + 1) * P], src[:, t], ident)
                            mm.then_inc(turned, 1)
                        pe.wait_ge(ranked, 4)
                        pe.matmul(ps[0:1, 4, 0:1], c_("ones")[:, 0:1], late_any[:, :], start=True, stop=True)\
                            .then_inc(turned, 1)

                    @block.scalar
                    def _(act):
                        act.wait_ge(split, 1)
                        act.activation(h_tok[0][:, :, :], scaled[:, :, :], ACT.Copy).then_inc(split, 1)
                        act.wait_ge(split, 3)
                        act.activation(h_tok[1][:, :, :], scaled[:, :, :], ACT.Copy).then_inc(split, 1)

                    @block.vector
                    def _(dve):
                        chain = Chain(dve, work2)
                        dve.wait_ge(counted, 1)
                        r_ = rank[:, :, :].rearrange("p t e -> p (t e)")
                        m_ = mask[:, :].rearrange("p t g e -> p (t g e)")
                        d_ = dense[:, :].rearrange("p t g e -> p (t g e)")
                        l_ = late[:, :, :].rearrange("p t e -> p (t e)")
                        chain(dve.tensor_scalar(r_, ps[:, 0, 0:2 * NE], -FAR, None, ALU.add))
                        chain(dve.tensor_scalar(l_, r_, SLOTS - FAR, None, ALU.is_ge))
                        chain(dve.tensor_tensor(r_, r_, m_, ALU.mult))
                        dve.tensor_scalar(r_, r_, FAR, None, ALU.add).then_inc(ranked, 1)
                        dve.tensor_tensor(l_, l_, d_, ALU.mult).then_inc(ranked, 1)
                        dve.wait_ge(ranked, 2)
                        dve.tensor_reduce(late_any[:, :], l_, AX.X, ALU.max).then_inc(ranked, 1)
                        dve.wait_ge(ranked, 3)
                        dve.tensor_scalar(late_any[:, :], late_any[:, :], 0.0, None, ALU.is_gt).then_inc(ranked, 1)
                        dve.tensor_tensor(scaled[:, :, :], scaled[:, :, :],
                                          row[:, :].unsqueeze(1).broadcast_to([P, NT, D]), ALU.mult).then_inc(split, 1)
                        for n in range(3):
                            dve.wait_ge(turned, n + 1)
                            dve.tensor_copy(rows[:, n, :], ps[0:NE, 1 + n, 0:S]).then_inc(taken, 1)
                        dve.wait_ge(turned, 4)
                        dve.tensor_copy(flag[:, :], ps[0:1, 4, 0:1])
                        dve.wait_ge(split, 2)
                        dve.tensor_tensor(scaled[:, :, :], scaled[:, :, :], h_tok[0][:, :, :], ALU.subtract)\
                            .then_inc(split, 1)
                        dve.wait_ge(split, 4)
                        dve.tensor_tensor(h_tok[2][:, :, :], scaled[:, :, :], h_tok[1][:, :, :], ALU.subtract)

                    @block.sync
                    def _(sp):
                        sp.wait_ge(taken, 3)
                        sp.dma_start(gate_row, rows[:, :, :]).then_inc(stored, 16)
                        sp.wait_ge(stored, 16)

        def experts_stage(h_tok, rank_col):
            u0 = unit["moe"]
            assert u0 % RING == 0
            body = 4
            trips = NE // body
            pieces = 6
            SPLIT = 4
            assert (body * pieces) % SPLIT == 0
            views = [a["w_exp_gate_2"][0].rearrange("(i b) (k p) c -> i b p k c", b=body, p=P),
                     a["w_exp_up_2"][0].rearrange("(i b) (k p) c -> i b p k c", b=body, p=P),
                     a["w_exp_down_2"][0].rearrange("(i b) (k p) c -> i b p k c", b=body, p=P)]
            rows_v = gate_row.rearrange("(i b) r s -> i b (r s)", b=body)
            nm = DE // P
            with ExitStack() as on:
                def two(name, shape):
                    return [sb(f"moe_{name}_{part}", shape, F32R, on=on) for part in ("hi", "lo")]

                w_split = two("w", [P, SPLIT, KD * UC // 2])
                h_sel = two("h", [P, KD, P])
                hid_T = two("hidT", [P, nm, P])
                y = two("y", [P, D])
                sel = sb("moe_sel", [P, NT, P], BF16, on=on)
                sel_T = sb("moe_selT", [P, 2, S], F32R, on=on)
                rows = sb("moe_rows", [P, 2, 2, S], on=on)
                gated = sb("moe_gated", [P, S], on=on)
                slot_gate = sb("moe_slot_gate", [P, 2], on=on)
                silu = sb("moe_silu", [P, DE], on=on)
                hid = sb("moe_hid", [P, DE], on=on)
                acc = lambda t, h: ps[:, 4 + 2 * t + h]
                flat = lambda v: v[:, :, :].rearrange("p c s -> p (c s)")
                wide = ps[:, 0:2].rearrange("p b c -> p (b c)")
                wide_y = ps[:, 2:4].rearrange("p b c -> p (b c)")

                def piece_slot(buf, j):
                    kc = 2 if j % pieces >= 4 else 4
                    return buf[:, j % SPLIT, :].rearrange("p (k c) -> p k c", k=kc)

                def raw_piece(j):
                    kc = 2 if j % pieces >= 4 else 4
                    return stream.view(u0 + j // 2)[:, (j % 2) * kc:(j % 2 + 1) * kc, :]

                def nth(i, per, n):
                    return i * per + n

                names = ("selected", "gathered", "h_hi", "h_lo", "used", "opened", "prepared", "hidden",
                         "turned", "hid_hi", "hid_lo", "w_hi", "w_lo", "y_hi", "y_lo", "closed")
                (selected, gathered, h_hi, h_lo, used, opened, prepared, hidden, turned, hid_hi, hid_lo, w_hi,
                 w_lo, y_hi, y_lo, closed) = (sem("moe_" + s) for s in names)
                rows_in = [sem("moe_rows_in0"), sem("moe_rows_in1")]

                with meeting() as block:
                    @block.tensor
                    def _(pe):
                        def gather(i, b):
                            pe.wait_ge(selected, nth(i, body, b + 1))
                            for c in range(KD):
                                dst = ps[:, c // 4, (c % 4) * P:(c % 4 + 1) * P]
                                for t in range(NT):
                                    for part in range(3):
                                        mm = pe.matmul(dst, h_tok[part][:, t, c * P:(c + 1) * P], sel[:, t, :],
                                                       start=(t == 0 and part == 0), stop=(t == NT - 1 and part == 2))
                            mm.then_inc(gathered, 1)

                        def scatter(i, n):
                            pe.wait_ge(y_lo, nth(i, body, n + 1))
                            pe.wait_ge(y_hi, nth(i, body, n + 1))
                            for t in range(NT):
                                for h in range(2):
                                    for part in range(2):
                                        mm = pe.matmul(acc(t, h), sel_T[:, (n + 1) % 2, t * P:(t + 1) * P],
                                                       y[part][:, h * UC:(h + 1) * UC], start=False, stop=False,
                                                       skip_group_check=True)
                            return mm

                        def product(i, b, kind):
                            for half in range(2):
                                j = b * pieces + 2 * kind + half
                                w = [piece_slot(p, j) for p in w_split]
                                pe.wait_ge(w_lo, nth(i, body * pieces, j + 1))
                                for k in range(4):
                                    c = 4 * half + k
                                    mm = three(pe, ps[:, kind], [p[:, c, :] for p in h_sel], [p[:, k, :] for p in w],
                                               start=(c == 0), stop=(c == KD - 1))
                                mm.then_inc(used, 1)

                        def expert(i, b, last=False):
                            pe.wait_ge(h_lo, nth(i, body, b + 1))
                            product(i, b, 0)
                            product(i, b, 1)
                            scatter(i, b)
                            pe.wait_ge(hidden, nth(i, body, b + 1))
                            for m in range(nm):
                                mm = pe.transpose(ps[:, 2, m * P:(m + 1) * P], hid[:, m * P:(m + 1) * P], ident)
                            mm.then_inc(turned, 1)
                            if not last:
                                gather(i, b + 1)
                            pe.wait_ge(hid_lo, nth(i, body, b + 1))
                            for half in range(2):
                                j = b * pieces + 4 + half
                                w = [piece_slot(p, j) for p in w_split]
                                pe.wait_ge(w_lo, nth(i, body * pieces, j + 1))
                                for h in range(2):
                                    for k in range(2):
                                        f = 2 * half + k
                                        mm = three(pe, ps[:, 2 + h], [p[:, f, :] for p in hid_T],
                                                   [p[:, k, h * UC:(h + 1) * UC] for p in w],
                                                   start=(f == 0), stop=(f == nm - 1))
                                mm.then_inc(used, 1)

                        for t in range(NT):
                            for h in range(2):
                                pe.matmul(acc(t, h), ident, x[:, t, h * UC:(h + 1) * UC], start=True, stop=False)
                        gather(0, 0)
                        with pe.Fori(0, trips - 1) as i:
                            for b in range(body):
                                expert(i, b)
                        for b in range(body):
                            expert(trips - 1, b, last=b == body - 1)
                        scatter(trips - 1, body)
                        close_sums(pe).then_inc(closed, 1)

                    @block.scalar
                    def _(act):
                        def split(i, j):
                            u = u0 + j // 2
                            if j % 2 == 0:
                                trip_loads = 3 * body // RING
                                act.wait_ge(stream.sems[u % RING],
                                            i * (16 * trip_loads) + (16 * (j // 2 // RING) + stream.need[u0 + u % RING]))
                            if j >= SPLIT:
                                act.wait_ge(used, nth(i, body * pieces, j + 1 - SPLIT))
                            act.activation(piece_slot(w_split[0], j % (body * pieces)), raw_piece(j % (body * pieces)),
                                           ACT.Copy).then_inc(w_hi, 1)

                        def tokens_split(i, b):
                            act.wait_ge(gathered, nth(i, body, b + 1))
                            act.activation(flat(h_sel[0]), wide, ACT.Copy).then_inc(h_hi, 1)

                        def expert(i, b, last=False):
                            j = b * pieces
                            after = (lambda n: None) if last else (lambda n: split(i, j + SPLIT + n))
                            split(i, j + SPLIT)
                            act.wait_ge(used, nth(i, body * pieces, j + 2))
                            act.activation(silu[:, :], ps[:, 0], ACT.Silu).then_inc(opened, 1)
                            split(i, j + SPLIT + 1)
                            after(2)
                            act.wait_ge(turned, nth(i, body, b + 1))
                            act.activation(flat(hid_T[0]), ps[:, 2], ACT.Copy).then_inc(hid_hi, 1)
                            if not last:
                                tokens_split(i, b + 1)
                            after(3)
                            after(4)
                            act.wait_ge(used, nth(i, body * pieces, j + 6))
                            act.activation(y[0][:, :], wide_y, ACT.Copy).then_inc(y_hi, 1)
                            after(5)

                        split(0, 0)
                        tokens_split(0, 0)
                        for j in range(1, SPLIT):
                            split(0, j)
                        act.activation(sel_T[:, 1, :], c_("noughts")[:, 0:S], ACT.Copy)
                        for half, given in ((0, y_hi), (1, y_lo)):
                            for h in range(2):
                                last = act.activation(y[half][:, h * UC:(h + 1) * UC], c_("noughts"), ACT.Copy)
                            last.then_inc(given, 1)
                        with act.Fori(0, trips - 1) as i:
                            for b in range(body):
                                expert(i, b)
                        for b in range(body):
                            expert(trips - 1, b, last=b == body - 1)

                    @block.vector
                    def _(dve):
                        def split(i, j):
                            dve.wait_ge(w_hi, nth(i, body * pieces, j + 1))
                            jj = j % (body * pieces)
                            dve.tensor_tensor(piece_slot(w_split[1], jj), raw_piece(jj),
                                              piece_slot(w_split[0], jj).bitcast(F32), ALU.subtract).then_inc(w_lo, 1)

                        def tokens_split(i, b):
                            dve.wait_ge(h_hi, nth(i, body, b + 1))
                            dve.tensor_tensor(flat(h_sel[1]), wide, flat(h_sel[0]).bitcast(F32), ALU.subtract)\
                                .then_inc(h_lo, 1)

                        def select(i, b):
                            if b:
                                dve.wait_ge(gathered, nth(i, body, b))
                            ranks = rank_col[:, :, bass.ds(i * body + b, 1)]
                            for t in range(NT):
                                last = dve.tensor_scalar(sel[:, t, :], c_("slot_row"), ranks[:, t, :], None, ALU.is_equal)
                            last.then_inc(selected, 1)

                        def prepare(i, b):
                            dve.wait_ge(rows_in[b % 2], nth(i, 16 * body // 2, 16 * (b // 2 + 1)))
                            slot = c_("slot_col")
                            dve.tensor_scalar(sel_T[:, b % 2, :], rows[:, b % 2, 0, :], slot, None, ALU.is_equal)
                            dve.scalar_tensor_tensor(gated[:, :], rows[:, b % 2, 0, :], slot, rows[:, b % 2, 1, :],
                                                     ALU.is_equal, ALU.mult, accum_out=slot_gate[:, b % 2:b % 2 + 1])\
                                .then_inc(prepared, 1)

                        def expert(i, b, last=False):
                            j = b * pieces
                            after = (lambda n: None) if last else (lambda n: split(i, j + SPLIT + n))
                            prepare(i, b)
                            if not last:
                                select(i, b + 1)
                            split(i, j + SPLIT)
                            split(i, j + SPLIT + 1)
                            dve.wait_ge(opened, nth(i, body, b + 1))
                            dve.wait_ge(prepared, nth(i, body, b + 1))
                            dve.wait_ge(used, nth(i, body * pieces, j + 4))
                            dve.scalar_tensor_tensor(hid[:, :], silu[:, :], slot_gate[:, b % 2:b % 2 + 1], ps[:, 1],
                                                     ALU.mult, ALU.mult).then_inc(hidden, 1)
                            dve.wait_ge(hid_hi, nth(i, body, b + 1))
                            dve.tensor_tensor(flat(hid_T[1]), ps[:, 2], flat(hid_T[0]).bitcast(F32), ALU.subtract)\
                                .then_inc(hid_lo, 1)
                            after(2)
                            if not last:
                                tokens_split(i, b + 1)
                            after(3)
                            after(4)
                            dve.wait_ge(y_hi, nth(i, body, b + 2))
                            dve.tensor_tensor(y[1][:, :], wide_y, y[0][:, :].bitcast(F32), ALU.subtract)\
                                .then_inc(y_lo, 1)
                            after(5)

                        select(0, 0)
                        split(0, 0)
                        tokens_split(0, 0)
                        for j in range(1, SPLIT):
                            split(0, j)
                        with dve.Fori(0, trips - 1) as i:
                            for b in range(body):
                                expert(i, b)
                        for b in range(body):
                            expert(trips - 1, b, last=b == body - 1)
                        dve.wait_ge(closed, 1)
                        for t in range(NT):
                            for h in range(2):
                                dve.tensor_copy(x[:, t, h * UC:(h + 1) * UC], acc(t, h))

                    @block.sync
                    def _(sp):
                        stream.prefetch(sp, u0)

                        def load(n, i):
                            j, m = (i, n - RING) if n >= RING else (i - 1, n - RING + 3 * body)
                            sp.wait_ge(w_lo, j * (body * pieces) + 2 * (m + 1))
                            sp.dma_start(stream.view(u0 + n), views[n % 3][i, n // 3])\
                                .then_inc(stream.sems[n % RING], 16)

                        def load_rows(b, i):
                            if b >= 2:
                                sp.wait_ge(prepared, i * body + (b - 1))
                            elif not isinstance(i, int) or i > 0:
                                sp.wait_ge(prepared, (i - 1) * body + (b - 1 + body))
                            sp.dma_start(rows[:, b % 2, :, :].rearrange("p r s -> p (r s)"),
                                         rows_v[i, b][0:2 * S].unsqueeze(0).broadcast_to([P, 2 * S]))\
                                .then_inc(rows_in[b % 2], 16)

                        load_rows(0, 0)
                        load_rows(1, 0)

                        def turn(i, last=False):
                            for b in range(body):
                                for n in range(RING + 3 * b, RING + 3 * b + 3):
                                    if n < 3 * body:
                                        load(n, i)
                                    elif not last:
                                        load(n - 3 * body, i + 1)
                                if b + 2 < body:
                                    load_rows(b + 2, i)
                                elif not last:
                                    load_rows(b + 2 - body, i + 1)

                        with sp.Fori(0, trips - 1) as i:
                            turn(i)
                        turn(trips - 1, last=True)

        def late_experts(flag):
            body = 4
            trips = NE // body
            per = 3 * body // RING
            views = [a["w_exp_gate_2"][0].rearrange("(i b) (k p) c -> i b p k c", b=body, p=P),
                     a["w_exp_up_2"][0].rearrange("(i b) (k p) c -> i b p k c", b=body, p=P),
                     a["w_exp_down_2"][0].rearrange("(i b) (k p) c -> i b p k c", b=body, p=P)]
            grown, opened, hid_ready, downs, weighed, rows_landed = \
                (sem("late_" + s) for s in ("grown", "opened", "hidden", "downs", "weighed", "rows_landed"))
            landed = [sem(f"late_landed_{s}") for s in range(RING)]
            nm = DE // P
            nb = nm // 2

            def unit_view(n):
                kc = 4 if n % 3 == 2 else KD
                return slots[:, n % RING, :].rearrange("p (k c) -> p k c", k=kc)

            with ExitStack() as on:
                gates = sb("late_gates", [P, NE, S], on=on)
                hid = sb("late_hid", [P, nm, S], on=on)
                act_ = sb("late_act", [P, nm, S], on=on)
                both = lambda buf, b: buf[:, 2 * b:2 * b + 2, :].rearrange("p m s -> p (m s)")

                def any_late(eng):
                    return eng.value_load(flag[0:1, 0:1], min_val=0, max_val=P) > 0

                with meeting() as block:
                    @block.tensor
                    def _(pe):
                        with pe.If(any_late(pe)):
                            for t in range(NT):
                                for h in range(2):
                                    pe.matmul(ps[:, 4 + 2 * t + h], ident, x[:, t, h * UC:(h + 1) * UC],
                                              start=True, stop=False)
                            with pe.Fori(0, trips) as i:
                                for b in range(body):
                                    for kind in range(2):
                                        n = 3 * b + kind
                                        w = unit_view(n)
                                        pe.wait_ge(landed[n % RING], i * (16 * per) + 16 * (n // RING + 1))
                                        for m in range(nm):
                                            dst = ps[:, 2 * kind + m // 2, (m % 2) * S:(m % 2 + 1) * S]
                                            for k in range(KD):
                                                mm = pe.matmul(dst, w[:, k, m * P:(m + 1) * P], hT[:, k, :],
                                                               start=(k == 0), stop=(k == KD - 1))
                                            if m % 2:
                                                mm.then_inc(grown, 1)
                                    n = 3 * b + 2
                                    w = unit_view(n)
                                    pe.wait_ge(landed[n % RING], i * (16 * per) + 16 * (n // RING + 1))
                                    for f in range(nm):
                                        if f % 2 == 0:
                                            pe.wait_ge(hid_ready, i * (body * nb) + (b * nb + f // 2 + 1))
                                        for t in range(NT):
                                            for h in range(2):
                                                mm = pe.matmul(ps[:, 4 + 2 * t + h], hid[:, f, t * P:(t + 1) * P],
                                                               w[:, f, h * UC:(h + 1) * UC], start=False, stop=False,
                                                               skip_group_check=True)
                                    mm.then_inc(downs, 1)
                            close_sums(pe).then_inc(downs, 1)

                    @block.scalar
                    def _(act):
                        with act.If(any_late(act)):
                            with act.Fori(0, trips) as i:
                                for b in range(body):
                                    for m in range(nb):
                                        act.wait_ge(grown, i * (body * 2 * nb) + (b * 2 * nb + m + 1))
                                        act.activation(both(act_, m), ps[:, m], ACT.Silu).then_inc(opened, 1)

                    @block.vector
                    def _(dve):
                        with dve.If(any_late(dve)):
                            dve.wait_ge(rows_landed, 16)
                            with dve.Fori(0, trips) as i:
                                rows_i = gates[:, bass.ds(i * body, body), :]
                                for b in range(body):
                                    for m in range(nb):
                                        dve.wait_ge(opened, i * (body * nb) + (b * nb + m + 1))
                                        dve.tensor_tensor(act_[:, 2 * m:2 * m + 2, :], act_[:, 2 * m:2 * m + 2, :],
                                                          rows_i[:, b, :].unsqueeze(1).broadcast_to([P, 2, S]),
                                                          ALU.mult).then_inc(weighed, 1)
                                        dve.wait_ge(weighed, i * (body * nb) + (b * nb + m + 1))
                                        dve.wait_ge(grown, i * (body * 2 * nb) + (b * 2 * nb + nb + m + 1))
                                        dve.tensor_tensor(both(hid, m), both(act_, m), ps[:, 2 + m], ALU.mult)\
                                            .then_inc(hid_ready, 1)
                            dve.wait_ge(downs, body * trips + 1)
                            for t in range(NT):
                                for h in range(2):
                                    dve.tensor_copy(x[:, t, h * UC:(h + 1) * UC], ps[:, 4 + 2 * t + h])

                    @block.sync
                    def _(sp):
                        def load(n, i):
                            m = n - RING
                            if m < 0 and isinstance(i, int):
                                pass
                            else:
                                b, kind = divmod(m % (3 * body), 3)
                                j = i if m >= 0 else i - 1
                                if kind == 2:
                                    sp.wait_ge(downs, j * body + (b + 1))
                                else:
                                    sp.wait_ge(grown, j * (body * 2 * nb) + (b * 2 * nb + (kind + 1) * nb))
                            sp.dma_start(unit_view(n), views[n % 3][i, n // 3]).then_inc(landed[n % RING], 16)

                        with sp.If(any_late(sp)):
                            sp.dma_start(gates[:, :, :], bass.AP(gate_row.tensor, 2 * S, [[0, P], [3 * S, NE], [1, S]]))\
                                .then_inc(rows_landed, 16)
                            for n in range(RING):
                                load(n, 0)
                            with sp.Fori(0, trips - 1) as i:
                                for n in range(RING, 3 * body):
                                    load(n, i)
                                for n in range(RING):
                                    load(n, i + 1)
                            for n in range(RING, 3 * body):
                                load(n, trips - 1)

        def final_norm():
            with ExitStack() as on:
                row = sb("final_gain", [P, D], on=on)
                sq = sb("final_sq", [P, D], on=on)
                st = sb("final_st", [P, 4, NT], on=on)
                y = sb("final_y", [P, NT, D], on=on)
                landed, sums, scaled, rooted, done = (sem("final_" + s) for s in ("landed", "sums", "scaled", "rooted", "done"))
                stored = sem("stored")
                with meeting() as block:
                    @block.sync
                    def _(sp):
                        sp.dma_start(row[:, :], everywhere(a["final_norm_g_2"], D)).then_inc(landed, 16)
                        for t in range(NT):
                            sp.wait_ge(done, t + 1)
                            sp.dma_start(out[0, t * P:(t + 1) * P, :], y[:, t, :]).then_inc(stored, 16)
                        sp.wait_ge(stored, 16 * NT)

                    @block.scalar
                    def _(act):
                        for t in range(NT):
                            if t:
                                act.wait_ge(sums, t)
                            act.activation(sq[:, :], x[:, t, :], ACT.Square, accum_out=st[:, 0, t:t + 1])\
                                .then_inc(sums, 1)
                        act.wait_ge(scaled, 1)
                        act.activation(st[:, 2, :], st[:, 1, :], ACT.Sqrt).then_inc(rooted, 1)

                    @block.vector
                    def _(dve):
                        dve.wait_ge(sums, NT)
                        dve.tensor_scalar(st[:, 1, :], st[:, 0, :], 1.0 / D, EPS, ALU.mult, ALU.add).then_inc(scaled, 1)
                        dve.wait_ge(rooted, 1)
                        dve.reciprocal(st[:, 3, :], st[:, 2, :]).then_inc(scaled, 1)
                        dve.wait_ge(scaled, 2)
                        dve.wait_ge(landed, 16)
                        for t in range(NT):
                            dve.scalar_tensor_tensor(y[:, t, :], x[:, t, :], st[:, 3, t:t + 1], row[:, :],
                                                     ALU.mult, ALU.mult).then_inc(done, 1)

        def block_mlp(layer):
            with ExitStack() as on:
                h_pair = [sb("mlp_h_" + part, [P, KD, S], F32R, on=on) for part in ("hi", "lo")]
                norm(f"mlp{layer}_norm", x, [("mlp_norm", layer * KD, h_pair)])
                mlp(layer, h_pair)

        with ExitStack() as on:
            mem = sb("mem", [P, NT, D], on=on)
            hb = sb("dist_rows", [NH, 512], on=on)
            with ExitStack() as on2:
                rows = sb("rows", [P, 3, P], on=on2)
                table = sb("table", [NBK + 1, NH], on=on2)
                setup(mem, rows, table, hb)
            norm("mem", mem, [("mem_norm", 0, hT)])
            memory(hT)
        late_loads()
        norm("n0", x, [("mix_norm", 0, hT)])
        conv_layer()
        block_mlp(0)
        with ExitStack() as on:
            sh = shared_buffers(on)
            with ExitStack() as on2:
                hkv = sb("hkv", [P, KD, S], on=on2)
                norm("n2", x, [("kv_norm", 0, hkv), ("mix_norm", KD, hT)])
                shared_kv(sh, hkv)
            nsa_layer(sh)
        block_mlp(1)
        first.close()
        with ExitStack() as on:
            by_a = sb("by_a", [P, NT, D], on=on)
            norm("n4", x, [("attn_norm", 0, hT)])
            with ExitStack() as on2:
                rwkv(by_a)
                dump("ya", by_a)
                ya_pair = [sb("yaT_" + part, [P, RC, S], F32R, on=on2) for part in ("hi", "lo")]
                turn_into_pair("ya_turn", by_a, RC, ya_pair)
                project("up_rwkv", unit["up_rwkv"], None, by_a, pair=ya_pair)
            by_b = sb("by_b", [P, NT, D], on=on)
            with ExitStack() as on2:
                yb = sb("yb", [P, NT, SW], on=on2)
                ssd(yb)
                dump("yb", yb)
                bias = sb("gate_bias", [P, 2 * D], on=on2)
                with ExitStack() as on3:
                    yb_pair = [sb("ybT_" + part, [P, SW // P, S], F32R, on=on3) for part in ("hi", "lo")]
                    turn_into_pair("yb_turn", yb, SW // P, yb_pair, scale=lambda j: col("ssd_norm", j))
                    project("up_ssd", unit["up_ssd"], None, by_b, parts=2, pair=yb_pair, depth=2,
                            loads=[(bias[:, :], everywhere(a["b_gate_2"], 2 * D))])
                merge(by_a, by_b, bias, yb)
                dump("x", x)
        with ExitStack() as on:
            flag = sb("late_flag", [1, 1], I32, on=on)
            with ExitStack() as on2:
                rank = sb("rank", [P, NT, NE], on=on2)
                h_tok = [sb("h_tok_" + part, [P, NT, D], BF16, on=on2) for part in ("hi", "mid", "lo")]
                with ExitStack() as on3:
                    scaled = sb("n5_scaled", [P, NT, D], on=on3)
                    norm("n5", x, [("ffn_norm", 0, hT)], scaled)
                    router(flag, scaled, h_tok, rank)
                experts_stage(h_tok, rank)
            late_experts(flag)
        final_norm()


NAMES = ("x mem mix_norm a_w_in a_conv_w b_w_in b_q_gain kv_norm w_kv_shared k_gain cmp_pos cmp_w1 cmp_w2 rel_bias "
         "mem_norm mem_w_kv mem_q_gain mem_k_gain w_out mlp_norm w_up w_down attn_norm_g_2 w_in_2 b_gate_2 rwkv_mu_2 "
         "rwkv_w0_2 rwkv_w_decay_2 rwkv_a0_2 rwkv_w_a_2 rwkv_w_g_2 rwkv_k_k_2 rwkv_k_a_2 rwkv_r_k_2 rwkv_ln_g_2 "
         "rwkv_ln_b_2 w_up_rwkv_2 ssd_conv_w_2 ssd_conv_b_2 ssd_dt_bias_2 ssd_a_log_2 ssd_d_2 ssd_norm_g_2 w_up_ssd_2 "
         "w_out_2 ffn_norm_g_2 w_router_group_2 b_router_group_2 w_router_expert_2 b_router_expert_2 w_exp_gate_2 "
         "w_exp_up_2 w_exp_down_2 final_norm_g_2").split()


def kernel(**inputs):
    import concourse.bacc as bacc
    from concourse.bass_utils import run_bass_kernel_spmd

    nc = bacc.Bacc("TRN2", target_bir_lowering=False, num_devices=1)
    const, at = constants()
    arrays = {f"in_{n}": np.ascontiguousarray(inputs[n]) for n in NAMES}
    arrays["in_const"] = const
    views = {k[3:]: nc.dram_tensor(k, v.shape, mybir.dt.from_np(v.dtype), kind="ExternalInput").ap()
             for k, v in arrays.items()}
    out = nc.dram_tensor("out_x", (1, S, D), F32, kind="ExternalOutput").ap()
    program(nc, views, out, at)
    r = run_bass_kernel_spmd(nc, [arrays], core_ids=[0])
    return r.results[0]["out_x"]
```
